# Optimizing a Trainium2 kernel written in Bass

```python
import jax, jax.numpy as jnp
from jax import lax
import numpy as np

D_MODEL = 1024
BATCH = 1
SEQ = 512
DEPTH = 1

HEAD_DIM = 64
ROPE_THETA = 10000.0
Q_BLOCK = 128
A_HEADS = 8
A_WIDTH = A_HEADS * HEAD_DIM
A_KV_RANK = 128
A_IDX_HEADS = 4
A_IDX_DIM = 64
A_TOPK_MAX = 256
B_HEADS = 8
B_GROUPS = 2
B_REP = B_HEADS // B_GROUPS
B_WIDTH = B_HEADS * HEAD_DIM
B_KV_WIDTH = B_GROUPS * HEAD_DIM
B_CMP_STRIDE = 16
B_CMP_LEN = 2 * B_CMP_STRIDE
B_CMP_HIDDEN = 256
B_SLC_LEN = 64
B_SLC_TOP = 16
B_WINDOW = 512
D_FF = 2816
MIX_IN_WIDTH = (A_WIDTH + A_KV_RANK + A_IDX_HEADS * A_IDX_DIM + A_IDX_DIM + A_IDX_HEADS
                + B_WIDTH + 6 * B_KV_WIDTH + 3 * B_HEADS + 2 * D_MODEL)
N_MOD = 9
ALPHA = (2.0 * DEPTH) ** 0.25
BETA = (8.0 * DEPTH) ** -0.25
LN_EPS = 1e-5
NEG = -1e30
FORCE_BONUS = 1e4

kernel_name = "hybrid_dsa_nsa_macaron_deepnorm_adaln"

def layer_norm(x, g, b):
    xf = x.astype(jnp.float32)
    mu = jnp.mean(xf, -1, keepdims=True)
    var = jnp.mean(jnp.square(xf - mu), -1, keepdims=True)
    return ((xf - mu) * lax.rsqrt(var + LN_EPS) * g + b).astype(x.dtype)

def rms_norm(x, g):
    xf = x.astype(jnp.float32)
    return (xf * lax.rsqrt(jnp.mean(jnp.square(xf), -1, keepdims=True) + LN_EPS) * g).astype(x.dtype)

def rope(x, pos):
    half = x.shape[-1] // 2
    inv = ROPE_THETA ** (-jnp.arange(half, dtype=jnp.float32) / half)
    ang = pos.astype(jnp.float32)[:, None] * inv[None, :]
    cos = jnp.cos(ang)[:, None, :]
    sin = jnp.sin(ang)[:, None, :]
    xf = x.astype(jnp.float32)
    x1, x2 = xf[..., :half], xf[..., half:]
    return jnp.concatenate([x1 * cos - x2 * sin, x1 * sin + x2 * cos], -1).astype(x.dtype)

def masked_softmax(s, mask):
    s = jnp.where(mask, s.astype(jnp.float32), NEG)
    return jax.nn.softmax(s, axis=-1) * mask

def swiglu(u, w_in, w_out):
    a, b = jnp.split(u @ w_in, 2, axis=-1)
    return (jax.nn.silu(a) * b) @ w_out

def modulate(x, shift, scale):
    return x * (1.0 + scale[:, None, :]) + shift[:, None, :]

def gather_rows(table, idx):
    return jax.vmap(lambda t, i: t[i])(table, idx)

def dsa_mixer(q, kv_lat, qi, ki, wi, kv_norm_g, w_kv_up, pos):
    B, S, _ = q.shape
    q = rope(q.reshape(B, S, A_HEADS, HEAD_DIM), pos)
    k, v = jnp.split(rms_norm(kv_lat, kv_norm_g) @ w_kv_up, 2, axis=-1)
    k = rope(k[:, :, None, :], pos)[:, :, 0]
    qi = rope(qi.reshape(B, S, A_IDX_HEADS, A_IDX_DIM), pos)
    ki = rope(ki[:, :, None, :], pos)[:, :, 0]
    wi = (wi * (A_IDX_HEADS ** -0.5)).astype(jnp.float32)
    topk = min(A_TOPK_MAX, S // 4)
    kpos = jnp.arange(S)

    def block(n):
        q0 = n * Q_BLOCK
        tq = q0 + jnp.arange(Q_BLOCK)
        qb = lax.dynamic_slice_in_dim(q, q0, Q_BLOCK, 1)
        qib = lax.dynamic_slice_in_dim(qi, q0, Q_BLOCK, 1)
        wib = lax.dynamic_slice_in_dim(wi, q0, Q_BLOCK, 1)
        logits = jnp.einsum('bqhd,bsd->bqhs', qib, ki).astype(jnp.float32)
        score = jnp.einsum('bqh,bqhs->bqs', wib, jax.nn.relu(logits))
        score = jnp.where(kpos[None, None, :] <= tq[None, :, None], score, NEG)
        _, sel = lax.top_k(score, topk)
        valid = sel <= tq[None, :, None]
        k_sel = gather_rows(k, sel)
        v_sel = gather_rows(v, sel)
        s = jnp.einsum('bqhd,bqkd->bhqk', qb, k_sel).astype(jnp.float32) * (HEAD_DIM ** -0.5)
        p = masked_softmax(s, valid[:, None])
        return jnp.einsum('bhqk,bqkd->bqhd', p.astype(v.dtype), v_sel)

    o = lax.map(block, jnp.arange(S // Q_BLOCK))
    return jnp.moveaxis(o, 0, 1).reshape(B, S, A_WIDTH)

def compress(t, pe, w1, w2):
    B, S, G, D = t.shape
    chunks = t.reshape(B, S // B_CMP_STRIDE, B_CMP_STRIDE, G, D)
    blocks = jnp.concatenate([chunks[:, :-1], chunks[:, 1:]], axis=2) + pe[:, None, :]
    flat = jnp.transpose(blocks, (0, 1, 3, 2, 4)).reshape(B, -1, G, B_CMP_LEN * D)
    return jax.nn.silu(flat @ w1) @ w2

def nsa_mixer(q, kv6, gates, pe_k, w1_k, w2_k, pe_v, w1_v, w2_v, pos):
    B, S, _ = q.shape
    q = rope(q.reshape(B, S, B_HEADS, HEAD_DIM), pos).reshape(B, S, B_GROUPS, B_REP, HEAD_DIM)
    kc, vc, ks, vs, kw, vw = [t.reshape(B, S, B_GROUPS, HEAD_DIM) for t in jnp.split(kv6, 6, axis=-1)]
    kc, ks, kw = rope(kc, pos), rope(ks, pos), rope(kw, pos)
    k_cmp = compress(kc, pe_k, w1_k, w2_k)
    v_cmp = compress(vc, pe_v, w1_v, w2_v)
    n_cmp = k_cmp.shape[1]
    cmp_start = jnp.arange(n_cmp) * B_CMP_STRIDE
    cmp_end = cmp_start + B_CMP_LEN - 1
    n_slc = S // B_SLC_LEN
    top_n = min(B_SLC_TOP, n_slc)
    ks_blk = jnp.transpose(ks.reshape(B, n_slc, B_SLC_LEN, B_GROUPS, HEAD_DIM), (0, 3, 1, 2, 4))
    vs_blk = jnp.transpose(vs.reshape(B, n_slc, B_SLC_LEN, B_GROUPS, HEAD_DIM), (0, 3, 1, 2, 4))
    slc_start = jnp.arange(n_slc) * B_SLC_LEN
    overlap = ((cmp_start[:, None] < slc_start[None, :] + B_SLC_LEN)
               & (slc_start[None, :] < cmp_start[:, None] + B_CMP_LEN)).astype(jnp.float32)
    jj = jnp.arange(n_slc)
    kw_pad = jnp.pad(kw, ((0, 0), (B_WINDOW, 0), (0, 0), (0, 0)))
    vw_pad = jnp.pad(vw, ((0, 0), (B_WINDOW, 0), (0, 0), (0, 0)))
    scale = HEAD_DIM ** -0.5

    def block(n):
        q0 = n * Q_BLOCK
        tq = q0 + jnp.arange(Q_BLOCK)
        qb = lax.dynamic_slice_in_dim(q, q0, Q_BLOCK, 1)
        s_c = jnp.einsum('bqgrd,bcgd->bgrqc', qb, k_cmp).astype(jnp.float32) * scale
        p_c = masked_softmax(s_c, cmp_end[None, :] <= tq[:, None])
        o_c = jnp.einsum('bgrqc,bcgd->bqgrd', p_c.astype(v_cmp.dtype), v_cmp)
        imp = jnp.einsum('bgrqc,cj->bgqj', p_c, overlap)
        blk_q = tq // B_SLC_LEN
        admissible = jj[None, :] <= blk_q[:, None]
        forced = (jj[None, :] == 0) | (jj[None, :] == blk_q[:, None]) | (jj[None, :] == blk_q[:, None] - 1)
        imp = jnp.where(admissible, imp + FORCE_BONUS * forced.astype(jnp.float32), NEG)
        _, sel = lax.top_k(imp, top_n)
        k_g = jax.vmap(gather_rows)(ks_blk, sel)
        v_g = jax.vmap(gather_rows)(vs_blk, sel).reshape(B, B_GROUPS, Q_BLOCK, top_n * B_SLC_LEN, HEAD_DIM)
        s_s = jnp.einsum('bqgrd,bgqnld->bgrqnl', qb, k_g).astype(jnp.float32) * scale
        s_s = s_s.reshape(B, B_GROUPS, B_REP, Q_BLOCK, top_n * B_SLC_LEN)
        tok = (sel[..., None] * B_SLC_LEN + jnp.arange(B_SLC_LEN)).reshape(B, B_GROUPS, Q_BLOCK, top_n * B_SLC_LEN)
        p_s = masked_softmax(s_s, (tok <= tq[None, None, :, None])[:, :, None])
        o_s = jnp.einsum('bgrqm,bgqmd->bqgrd', p_s.astype(v_g.dtype), v_g)
        kwin = lax.dynamic_slice_in_dim(kw_pad, q0, Q_BLOCK + B_WINDOW, 1)
        vwin = lax.dynamic_slice_in_dim(vw_pad, q0, Q_BLOCK + B_WINDOW, 1)
        kpos = q0 - B_WINDOW + jnp.arange(Q_BLOCK + B_WINDOW)
        mask_w = ((kpos[None, :] <= tq[:, None]) & (kpos[None, :] > tq[:, None] - B_WINDOW)
                  & (kpos[None, :] >= 0))
        s_w = jnp.einsum('bqgrd,bkgd->bgrqk', qb, kwin).astype(jnp.float32) * scale
        p_w = masked_softmax(s_w, mask_w)
        o_w = jnp.einsum('bgrqk,bkgd->bqgrd', p_w.astype(vwin.dtype), vwin)
        return o_c, o_s, o_w

    o_c, o_s, o_w = [jnp.moveaxis(o, 0, 1).reshape(B, S, B_GROUPS, B_REP, HEAD_DIM)
                     for o in lax.map(block, jnp.arange(S // Q_BLOCK))]
    g = jax.nn.sigmoid(gates.astype(jnp.float32)).astype(q.dtype).reshape(B, S, 3, B_GROUPS, B_REP, 1)
    o = g[:, :, 0] * o_c + g[:, :, 1] * o_s + g[:, :, 2] * o_w
    return o.reshape(B, S, B_WIDTH)

def setup_inputs(seed: int = 0) -> dict:
    key = jax.random.key(seed)
    ks = jax.random.split(key, 32)
    L = DEPTH

    def w(k, shape, fan_in, scale=1.0):
        return jax.random.normal(k, (L,) + shape, jnp.float32) * (scale * fan_in ** -0.5)

    def gain(k, n):
        return 1.0 + 0.02 * jax.random.normal(k, (L, n), jnp.float32)

    def bias(k, shape):
        return 0.02 * jax.random.normal(k, (L,) + shape, jnp.float32)

    D = D_MODEL
    return {
        "x": jax.random.normal(ks[0], (BATCH, SEQ, D), jnp.float32),
        "c": jax.random.normal(ks[1], (BATCH, D), jnp.float32),
        "w_ada": w(ks[2], (D, N_MOD * D), D),
        "b_ada": bias(ks[3], (N_MOD * D,)),
        "ffn1_w_in": w(ks[4], (D, 2 * D_FF), D),
        "ffn1_w_out": w(ks[5], (D_FF, D), D_FF, BETA),
        "ln1_g": gain(ks[6], D),
        "ln1_b": bias(ks[7], (D,)),
        "w_mix_in": w(ks[8], (D, MIX_IN_WIDTH), D),
        "kv_norm_g": gain(ks[9], A_KV_RANK),
        "w_kv_up": w(ks[10], (A_KV_RANK, 2 * HEAD_DIM), A_KV_RANK),
        "cmp_pe_k": 0.1 * jax.random.normal(ks[11], (L, B_CMP_LEN, HEAD_DIM), jnp.float32),
        "cmp_w1_k": w(ks[12], (B_CMP_LEN * HEAD_DIM, B_CMP_HIDDEN), B_CMP_LEN * HEAD_DIM),
        "cmp_w2_k": w(ks[13], (B_CMP_HIDDEN, HEAD_DIM), B_CMP_HIDDEN),
        "cmp_pe_v": 0.1 * jax.random.normal(ks[14], (L, B_CMP_LEN, HEAD_DIM), jnp.float32),
        "cmp_w1_v": w(ks[15], (B_CMP_LEN * HEAD_DIM, B_CMP_HIDDEN), B_CMP_LEN * HEAD_DIM),
        "cmp_w2_v": w(ks[16], (B_CMP_HIDDEN, HEAD_DIM), B_CMP_HIDDEN),
        "w_br_a": w(ks[17], (A_WIDTH, D), A_WIDTH),
        "w_br_b": w(ks[18], (B_WIDTH, D), B_WIDTH),
        "w_mix_out": w(ks[19], (D, D), D, BETA),
        "ln2_g": gain(ks[20], D),
        "ln2_b": bias(ks[21], (D,)),
        "ffn2_w_in": w(ks[22], (D, 2 * D_FF), D),
        "ffn2_w_out": w(ks[23], (D_FF, D), D_FF, BETA),
        "ln3_g": gain(ks[24], D),
        "ln3_b": bias(ks[25], (D,)),
    }

def reference(x, c, w_ada, b_ada, ffn1_w_in, ffn1_w_out, ln1_g, ln1_b, w_mix_in, kv_norm_g, w_kv_up,
              cmp_pe_k, cmp_w1_k, cmp_w2_k, cmp_pe_v, cmp_w1_v, cmp_w2_v, w_br_a, w_br_b, w_mix_out,
              ln2_g, ln2_b, ffn2_w_in, ffn2_w_out, ln3_g, ln3_b):
    S = x.shape[1]
    pos = jnp.arange(S)
    split_points = np.cumsum([A_WIDTH, A_KV_RANK, A_IDX_HEADS * A_IDX_DIM, A_IDX_DIM, A_IDX_HEADS,
                              B_WIDTH, 6 * B_KV_WIDTH, 3 * B_HEADS]).tolist()
    c_act = jax.nn.silu(c)
    for l in range(DEPTH):
        mod = c_act @ w_ada[l] + b_ada[l]
        sh1, sc1, g1, sh2, sc2, g2, sh3, sc3, g3 = jnp.split(mod, N_MOD, axis=-1)
        f1 = swiglu(modulate(x, sh1, sc1), ffn1_w_in[l], ffn1_w_out[l])
        x = layer_norm(ALPHA * x + 0.5 * g1[:, None, :] * f1, ln1_g[l], ln1_b[l])
        h = modulate(x, sh2, sc2) @ w_mix_in[l]
        qa, kv_lat, qi, ki, wi, qb, kv6, gb, gm = jnp.split(h, split_points, axis=-1)
        ya = dsa_mixer(qa, kv_lat, qi, ki, wi, kv_norm_g[l], w_kv_up[l], pos)
        yb = nsa_mixer(qb, kv6, gb, cmp_pe_k[l], cmp_w1_k[l], cmp_w2_k[l],
                       cmp_pe_v[l], cmp_w1_v[l], cmp_w2_v[l], pos)
        gate_a, gate_b = jnp.split(jax.nn.sigmoid(gm.astype(jnp.float32)).astype(x.dtype), 2, axis=-1)
        merged = gate_a * (ya @ w_br_a[l]) + gate_b * (yb @ w_br_b[l])
        mix = merged @ w_mix_out[l]
        x = layer_norm(ALPHA * x + g2[:, None, :] * mix, ln2_g[l], ln2_b[l])
        f2 = swiglu(modulate(x, sh3, sc3), ffn2_w_in[l], ffn2_w_out[l])
        x = layer_norm(ALPHA * x + 0.5 * g3[:, None, :] * f2, ln3_g[l], ln3_b[l])
    return x


_drawn_inputs = setup_inputs


def setup_inputs(seed=0):
    import zlib

    import numpy as np

    out = dict(_drawn_inputs(seed))
    spreads = {}
    factors = {'b_ada': 4.503,
     'ln1_g': 2.684,
     'ln1_b': 2.769,
     'kv_norm_g': 8.0,
     'cmp_pe_k': 8.0,
     'cmp_w1_k': 3.404,
     'cmp_w2_k': 3.312,
     'cmp_pe_v': 8.0,
     'ln2_g': 7.89,
     'ln2_b': 7.405,
     'ln3_g': 8.082,
     'ln3_b': 8.003}
    for name, (base, spread) in spreads.items():
        noise = np.random.default_rng([zlib.crc32(name.encode()), seed]).standard_normal(out[name].shape)
        drawn = base * np.exp(spread * noise) if base else spread * noise
        out[name] = __import__('jax').numpy.asarray(drawn.astype(out[name].dtype))
    for name, factor in factors.items():
        out[name] = (out[name] * factor).astype(out[name].dtype)
    return out
```

```python
from contextlib import ExitStack

import concourse.bass as bass
from concourse import mybir

F32 = mybir.dt.float32
F32R = mybir.dt.float32r
BF16 = mybir.dt.bfloat16
ACT = mybir.ActivationFunctionType
ALU = mybir.AluOpType
AX = mybir.AxisListType.X

P = 128
S = 512
D = 1024
DC = D // P
FF = 2816
FC = FF // P
HD = 64
QB = S // P
NH = 8
HC = NH * HD // P
NI = 4
TOPK = S // 4
ALPHA = 2.0 ** 0.25
EPS = 1e-5
NEG = -1e30
TAKEN = -3e38
NMOD = 9
NADA = NMOD * DC
NC = 31
CW = 32
CL2 = 16

UW = DC * P
OUT_UNITS = 3
FFN_UNITS = 2 * FC + OUT_UNITS * DC
MIX0 = FFN_UNITS
N_ROPE = 12
N_MIX = 18
N_GATE = 2 * DC
BR0 = MIX0 + N_MIX + N_GATE
MO0 = BR0 + DC
FFN2 = MO0 + DC
UNITS = FFN2 + FFN_UNITS
RAW = 4
SPLIT = 2
CREDIT = 2
ADA_FIRST = 2 * DC
ADA_START = ADA_FIRST + 4
ADA_RING = 2

V_BADA, V_LN, V_KVG = 0, NADA, NADA + 6 * DC
V_N = V_KVG + 1
C_ID, C_CAUSAL, C_CMP, C_VALID = 0, P, 2 * P, 2 * P + QB * CW
C_N = C_VALID + QB
M_W2K, M_W2V, M_WK, M_WV, M_PEK, M_PEV = 0, 256, 384, 512, 576, 608
M_N = 640


def schedule():
    items = []
    for q in range(QB):
        for h in range(NH):
            items.append(("a", q, h))
            if h == 4 and q:
                items.append(("yb", q - 1, 0))
        for h in range(NH):
            items.append(("s", q, h))
            if h == 4:
                items.append(("ya", q, 0))
        items += [("w", q, h) for h in range(NH)]
        items.append(("c", q, 0))
    return items + [("-", 0, 0)] * 5 + [("yb", QB - 1, 0)]


def decoder_layer(nc, x_t, c_row, w_ada_t, vecs, consts, rope_tab, small_w, cmp_w1, stream, out):
    items = schedule()
    n_items = len(items)
    turned = [i for i, it in enumerate(items) if it[0] != "-"]
    turn_no = {i: t for t, i in enumerate(turned)}
    scored = [i for i, it in enumerate(items) if it[0] in "aswc"]
    score_no = {i: n for n, i in enumerate(scored)}
    group_no = {}
    for kind, q, _ in items:
        if kind in "aswc":
            group_no.setdefault((kind, q), len(group_no))
    reader, counts = {}, [0, 0]
    for i in turned:
        by = 1 if items[i][0] in ("ya", "yb") else score_no[i] % 2
        counts[by] += 1
        reader[i] = (by, counts[by])
    group_end = {group_no[items[i][0], items[i][1]]: n for n, i in enumerate(scored)}

    ctx = ExitStack()
    with ctx:
        def sb(name, shape, dt=F32, stack=ctx):
            return stack.enter_context(nc.sbuf_tensor(name, shape, dt))

        def sem(name):
            return ctx.enter_context(nc.semaphore(name))

        xa = sb("xa", [P, DC, S])
        raw = [sb(f"raw{i}", [P, UW]) for i in range(RAW)]
        w_hi = [sb(f"w_hi{i}", [P, UW], F32R) for i in range(SPLIT)]
        w_lo = [sb(f"w_lo{i}", [P, UW], F32R) for i in range(SPLIT)]
        tmp = [sb(f"tmp{i}", [P, S]) for i in range(8)]
        vec = sb("vec", [P, V_N])
        con = sb("con", [P, C_N])
        smw = sb("smw", [P, M_N])
        mod = sb("mod", [P, NADA])
        aff = sb("aff", [P, 12, DC])
        ones_d = sb("ones_d", [P, P])
        ones_r = sb("ones_r", [P, P])
        eps = sb("eps", [P, 1])
        ident_b = sb("ident_b", [P, P], BF16)
        causal_b = sb("causal_b", [P, P], BF16)
        wi = sb("wi", [P, QB, NI])
        gb = sb("gb", [P, QB, 3 * NH])
        kcmp = sb("kcmp", [P, 2, CW])
        vbd = sb("vbd", [P, 2, 4 * HD])
        sums = sb("sums", [P, QB, 4, NH])
        fac = sb("fac", [P, 4, NH])
        nmax = sb("nmax", [P, 4 + NH])
        max8 = sb("max8", [P, 3, 8])

        with ExitStack() as use_u:
            u_hi = sb("u_hi", [P, DC, S], F32R, use_u)
            u_lo = sb("u_lo", [P, DC, S], F32R, use_u)
        probs = [sb(f"probs{i}", [P, S]) for i in range(3)]
        probs_t = [sb(f"probs_t{i}", [P, S]) for i in range(2)]
        o_a = sb("o_a", [P, S])
        o_b = sb("o_b", [P, S])
        o_tmp = sb("o_tmp", [P, S])
        cmp_s = sb("cmp_s", [P, NH, CW])
        sb("rest_of_u", [P, 2 * DC * S - 8 * S - NH * CW])

        with ExitStack() as use_ffn:
            h_hi = sb("h_hi", [P, FC, S], F32R, use_ffn)
            h_lo = sb("h_lo", [P, FC, S], F32R, use_ffn)
            ada = [sb(f"ada{i}", [P, D], F32, use_ffn) for i in range(ADA_RING)]
            c_act = sb("c_act", [P, D], F32, use_ffn)
        roped = sb("roped", [P, N_ROPE, S])
        k_a = sb("k_a", [P, S])
        v_a = sb("v_a", [P, QB, HD])
        v_s = sb("v_s", [P, QB, P])
        v_w = sb("v_w", [P, QB, P])
        gates = sb("gates", [P, N_GATE, S])
        w1 = gates[:, :, :].rearrange("p a b -> p (a b)").rearrange("p (t l n) -> p t l n", t=2, l=CL2)
        mask_a = [sb(f"mask_a{q}", [P, P * (q + 1)], BF16) for q in range(1, QB)]
        with ExitStack() as early:
            ki2 = sb("ki2", [P, S], F32, early)
            small = sb("small", [P, S], F32, early)
            kvl = sb("kvl", [P, S], F32, early)
            kvsq = sb("kvsq", [P, S], F32, early)
            kc = sb("kc", [P, S], F32, early)
            vc = sb("vc", [P, S], F32, early)
            vs_t = sb("vs_t", [P, S], F32, early)
            vw_t = sb("vw_t", [P, S], F32, early)
            cmp_in = [sb(f"cmp_in{t}", [P, CL2, 2, NC], F32, early) for t in range(2)]
            hid_k = sb("hid_k", [P, 2, 2, CW], F32, early)
            hid_v = sb("hid_v", [P, 2, 2, 4, CW], F32, early)
            cs_tab = sb("cs_tab", [P, 2, S], F32, early)
            acc = [sb(f"acc{q}", [P, P * (q + 1)], F32, early) for q in range(1, QB)]
        y_hi = [sb(f"y_hi{m}", [P, HC, S], F32R) for m in range(2)]
        y_lo = [sb(f"y_lo{m}", [P, HC, S], F32R) for m in range(2)]

        bank = [ctx.enter_context(nc.psum_tensor(f"bank{i}", [P, S], F32)) for i in range(8)]

        ident = con[:, C_ID:C_ID + P]
        causal = con[:, C_CAUSAL:C_CAUSAL + P]
        cmp_mask = con[:, C_CMP:C_VALID].rearrange("p (q c) -> p q c", q=QB)
        cos, sin = cs_tab[:, 0, :], cs_tab[:, 1, :]
        w2k = smw[:, M_W2K:M_W2V].rearrange("p (a b) -> p a b", a=2)
        w2v = smw[:, M_W2V:M_WK].rearrange("p (a b) -> p a b", a=2)
        pe_tab = [smw[:, o:o + 32].rearrange("p (a l) -> p a l", a=2) for o in (M_PEK, M_PEV)]

        x_loaded, c_loaded, vec_loaded, con_loaded = sem("x_loaded"), sem("c_loaded"), sem("vec_loaded"), sem("con_loaded")
        rope_loaded, w1_loaded = sem("rope_loaded"), sem("w1_loaded")
        raw_loaded = [sem(f"raw_loaded{i}") for i in range(RAW)]
        ada_loaded = [sem(f"ada_loaded{i}") for i in range(ADA_RING)]
        hi_ready, lo_ready = sem("hi_ready"), sem("lo_ready")
        units_done = sem("units_done")
        consts_ready = sem("consts_ready")
        c_ready, ada_done = sem("c_ready"), sem("ada_done")
        silu_done, hmul_done, hh_done, h_ready = sem("silu_done"), sem("hmul_done"), sem("hh_done"), sem("h_ready")
        z_done, sq_done = sem("z_done"), sem("sq_done")
        sum_ready, stats_done = sem("sum_ready"), sem("stats_done")
        mean_ready, var_ready, std_ready = sem("mean_ready"), sem("var_ready"), sem("std_ready")
        ub_ready, uh_ready, u_ready, xa_ready = sem("ub_ready"), sem("uh_ready"), sem("u_ready"), sem("xa_ready")
        mix_evac, rope_done = sem("mix_evac"), sem("rope_done")
        ms_done, kv_std, kvn_ready = sem("ms_done"), sem("kv_std"), sem("kvn_ready")
        small_turned, small_read = sem("small_turned"), sem("small_read")
        logits_done, relu_done, acc_done = sem("logits_done"), sem("relu_done"), sem("acc_done")
        kv_done, kv_read = sem("kv_done"), sem("kv_read")
        v_turned, v_read = sem("v_turned"), sem("v_read")
        cmp_in_ready, hid_done, hid_ready = sem("cmp_in_ready"), sem("hid_done"), sem("hid_ready")
        cmp_done, cmp_read = sem("cmp_done"), sem("cmp_read")
        gate_done, q_scaled, mask_ready = sem("gate_done"), sem("q_scaled"), sem("mask_ready")
        s_done, max_done, exp_done = sem("s_done"), sem("max_done"), sem("exp_done")
        t_done, pv_done, group_read = sem("t_done"), sem("pv_done"), sem("group_read")
        t_read = (sem("t_read_by_scalar"), sem("t_read_by_vector"))
        y_hi_done, ob_ready = sem("y_hi_done"), sem("ob_ready")
        merge_done, mf_ready, mh_done, m_ready = sem("merge_done"), sem("mf_ready"), sem("mh_done"), sem("m_ready")
        final_ready, stored = sem("final_ready"), sem("stored")
        dve_step = sem("dve_step")

        def q_rows(kind, h):
            if kind == "a":
                return 2 + h // 2, (h % 2) * HD
            return 8 + h % 4, (h // 4) * HD

        block = ctx.enter_context(nc.Block())

        @block.sync
        def _(sp):
            def load_unit(slot, u):
                src = stream[bass.ts(u, 1), :, :].rearrange("a p n -> (a p) n")
                sp.dma_start(raw[slot][:, :], src).then_inc(raw_loaded[slot], 16)

            def load_ada(slot, b):
                src = w_ada_t[bass.ts(b, 1), :, :].rearrange("a p n -> (a p) n")
                sp.dma_start(ada[slot][:, :], src).then_inc(ada_loaded[slot], 16)

            def units(first, count, with_ada=False):
                with sp.Fori(0, count // RAW) as it:
                    for k in range(RAW):
                        sp.wait_ge(lo_ready, it * RAW + (first + k - RAW + 1))
                        load_unit((first + k) % RAW, it * RAW + (first + k))
                        if with_ada:
                            sp.wait_ge(ada_done, it * RAW + (ADA_START + k - ADA_RING + 1))
                            load_ada(k % ADA_RING, it * RAW + (ADA_START + k))

            sp.dma_start(c_act[:, :], c_row.partition_broadcast(P)).then_inc(c_loaded, 16)
            for b in range(ADA_RING):
                load_ada(b, b)
            sp.dma_start(vec[:, :], vecs).then_inc(vec_loaded, 16)
            sp.dma_start(con[:, :], consts).then_inc(con_loaded, 16)
            sp.dma_start(smw[:, :], small_w).then_inc(con_loaded, 16)
            for k in range(DC):
                sp.dma_start(xa[:, k, :], x_t[:, k, :]).then_inc(x_loaded, 16)
            for b in range(ADA_RING, ADA_START):
                sp.wait_ge(ada_done, b - ADA_RING + 1)
                load_ada(b % ADA_RING, b)
                if b < ADA_RING + RAW:
                    load_unit(b - ADA_RING, b - ADA_RING)
            units(RAW, 2 * FC - RAW, with_ada=True)
            first, b = 2 * FC, ADA_START + 2 * FC - RAW
            for u in range(2 * FC, MIX0 + RAW):
                if u < 2 * FC + RAW or (u - 2 * FC - RAW) % OUT_UNITS == OUT_UNITS - 1:
                    sp.wait_ge(ada_done, b - ADA_RING + 1)
                    load_ada(b % ADA_RING, b)
                    b += 1
                sp.wait_ge(lo_ready, u - RAW + 1)
                load_unit(u % RAW, u)
            assert b == NADA
            first = MIX0 + RAW
            sp.wait_ge(ada_done, NADA)
            sp.wait_ge(units_done, MIX0 + CREDIT)
            sp.dma_start(cs_tab[:, :, :], rope_tab).then_inc(rope_loaded, 16)
            sp.dma_start(w1, cmp_w1).then_inc(w1_loaded, 16)
            rest = UNITS - first
            units(first, rest)
            for k in range(rest // RAW * RAW, rest):
                sp.wait_ge(lo_ready, first + k - RAW + 1)
                load_unit((first + k) % RAW, first + k)
            for k in range(DC):
                sp.wait_ge(final_ready, k + 1)
                sp.dma_start(out[:, k, :], xa[:, k, :]).then_inc(stored, 16)
            sp.wait_ge(stored, 16 * DC)

        @block.gpsimd
        def _(pool):
            nc.gpsimd.memset(ones_d[:, :], 1.0 / D).then_inc(consts_ready, 1)
            nc.gpsimd.memset(ones_r[:, :], 1.0 / P).then_inc(consts_ready, 1)
            nc.gpsimd.memset(eps[:, :], EPS).then_inc(consts_ready, 1)
            nc.gpsimd.memset(vbd[:, :, :], 0.0).then_inc(consts_ready, 1)
            nc.gpsimd.memset(kcmp[:, :, :], 0.0).then_inc(consts_ready, 1)
            pool.wait_ge(con_loaded, 32)
            nc.gpsimd.tensor_copy(ident_b[:, :], ident).then_inc(consts_ready, 1)
            nc.gpsimd.tensor_copy(causal_b[:, :], causal).then_inc(consts_ready, 1)
            pool.wait_ge(units_done, MIX0 + CREDIT)
            nc.gpsimd.memset(hid_k[:, :, :, :], 0.0).then_inc(consts_ready, 1)
            nc.gpsimd.memset(hid_v[:, :, :, :, :], 0.0).then_inc(consts_ready, 1)
            pool.wait_ge(rope_done, N_ROPE + 2)
            for first in (2, 8):
                q = roped[:, first:first + 4, :]
                nc.gpsimd.tensor_scalar(q, q, HD ** -0.5, 0.0, ALU.mult, ALU.add).then_inc(q_scaled, 1)

        @block.tensor
        def _(pe):
            def unit(u, slot, groups, before=None):
                pe.wait_ge(lo_ready, u + 1)
                at = 0
                for psum, x_hi, x_lo, chunks, first, last in groups:
                    for n, k in enumerate(chunks):
                        if before is not None:
                            before(k)
                        w = slice(at * P, (at + 1) * P)
                        one, end = first and n == 0, last and n == len(chunks) - 1
                        nc.tensor.matmul(psum, w_hi[slot][:, w], x_hi[:, k, :], start=one, stop=False)
                        nc.tensor.matmul(psum, w_hi[slot][:, w], x_lo[:, k, :], start=False, stop=False)
                        mm = nc.tensor.matmul(psum, w_lo[slot][:, w], x_hi[:, k, :], start=False, stop=end)
                        at += 1
                mm.then_inc(units_done, 1)

            def input_ready(phase):
                return lambda k: pe.wait_ge(u_ready, phase * DC + k + 1)

            def ffn(f, u0, phase):
                with pe.Fori(0, FC // 2) as it:
                    for jj in range(2):
                        j = it * 2 + (FC * f + jj)
                        u = it * 4 + (u0 + 2 * jj)
                        ready = input_ready(phase) if jj == 0 else None
                        pe.wait_ge(silu_done, j + 1)
                        unit(u, 0, [(bank[2 * jj][:, :], u_hi, u_lo, range(DC), True, True)], ready)
                        pe.wait_ge(hmul_done, j + 1)
                        unit(u + 1, 1, [(bank[2 * jj + 1][:, :], u_hi, u_lo, range(DC), True, True)])
                with pe.Fori(0, DC // 2) as it:
                    for cc in range(2):
                        z = it * 2 + (2 * DC * f + cc)
                        pe.wait_ge(z_done, z + 1)
                        for n in range(OUT_UNITS):
                            ks = range(8 * n, min(8 * n + 8, FC))
                            u = it * (2 * OUT_UNITS) + (u0 + 2 * FC + cc * OUT_UNITS + n)
                            pe.wait_ge(h_ready, FC * f + ks[-1] + 1)
                            unit(u, (cc * OUT_UNITS + n) % SPLIT,
                                 [(bank[4 + cc][:, :], h_hi, h_lo, ks, n == 0, n == OUT_UNITS - 1)])

            def stats(p):
                for n in range(2):
                    pe.wait_ge(sum_ready, 2 * p + n + 1)
                    nc.tensor.matmul(bank[6 + n][:, :], ones_d[:, :], tmp[4 + n][:, :], start=True, stop=True)\
                        .then_inc(stats_done, 1)

            pe.sem_inc(units_done, CREDIT)
            pe.wait_ge(consts_ready, 7)
            ffn(0, 0, 0)
            stats(0)

            with pe.Fori(0, N_MIX // 2) as it:
                for b in range(2):
                    pe.wait_ge(mix_evac, it * 2 + (b + 1))
                    unit(it * 2 + (MIX0 + b), b, [(bank[b][:, :], u_hi, u_lo, range(DC), True, True)],
                         input_ready(1) if b == 0 else None)
            pe.wait_ge(mix_evac, CREDIT + 2)
            nc.tensor.matmul(bank[2][:, :], ones_r[:, :], kvsq[:, :], start=True, stop=True).then_inc(ms_done, 1)
            for q in range(QB):
                tr = nc.tensor.transpose(bank[3][:, q * P:(q + 1) * P], small[:, q * P:(q + 1) * P], ident)
            tr.then_inc(small_turned, 1)
            pe.wait_ge(rope_done, 4)
            for n in range((QB - 1) * NI):
                q, h = 1 + n // NI, n % NI
                rows = slice((h % 2) * HD, (h % 2) * HD + HD)
                if n >= 2:
                    pe.wait_ge(relu_done, n - 1)
                nc.tensor.matmul(bank[4 + n % 2][:, :P * (q + 1)], roped[rows, h // 2, q * P:(q + 1) * P],
                                 ki2[rows, :P * (q + 1)], start=True, stop=True).then_inc(logits_done, 1)
            pe.wait_ge(kvn_ready, 1)
            nc.tensor.matmul(bank[6][:, :], smw[:, M_WK:M_WV], kvl[:, :], start=True, stop=True).then_inc(kv_done, 1)
            for t in range(QB):
                mm = nc.tensor.matmul(bank[7][:, t * HD:(t + 1) * HD], kvl[:, t * P:(t + 1) * P],
                                      smw[:, M_WV:M_PEK], start=True, stop=True)
            mm.then_inc(kv_done, 1)
            pe.wait_ge(mix_evac, CREDIT + N_MIX)
            pe.wait_ge(kv_std, 1)
            pe.wait_ge(small_read, 2)
            for n, src in enumerate((vs_t, vw_t)):
                for t in range(QB):
                    tr = nc.tensor.transpose(bank[2 + n][:, t * P:(t + 1) * P], src[:, t * P:(t + 1) * P], ident)
                tr.then_inc(v_turned, 1)
            pe.wait_ge(w1_loaded, 16)
            for t in range(2):
                pe.wait_ge(cmp_in_ready, 4 * (t + 1))
                for hc in range(2):
                    for l in range(CL2):
                        mm = nc.tensor.matmul(bank[t][:, hc * 64:hc * 64 + 2 * NC], w1[:, t, l, hc * P:(hc + 1) * P],
                                              cmp_in[t][:, l, :, :].rearrange("p g i -> p (g i)"),
                                              start=l == 0, stop=l == CL2 - 1)
                mm.then_inc(hid_done, 1)
            pe.wait_ge(hid_ready, 2)
            pe.wait_ge(relu_done, (QB - 1) * NI)
            for hc in range(2):
                mm = nc.tensor.matmul(bank[4][:, :2 * CW], w2k[:, hc, :],
                                      hid_k[:, hc, :, :].rearrange("p g i -> p (g i)"), start=hc == 0, stop=hc == 1)
            mm.then_inc(cmp_done, 1)
            pe.wait_ge(hid_ready, 2 + 16)
            for g in range(2):
                for hc in range(2):
                    mm = nc.tensor.matmul(bank[5][:, g * HD:(g + 1) * HD],
                                          hid_v[:, hc, g, :, :].rearrange("p r i -> p (r i)"), w2v[:, hc, :],
                                          start=hc == 0, stop=hc == 1)
            mm.then_inc(cmp_done, 1)
            pe.wait_ge(kv_read, 2)
            with pe.Fori(0, N_GATE // 2) as it:
                for b in range(2):
                    pe.wait_ge(gate_done, it * 2 + (b + 1))
                    unit(it * 2 + (MIX0 + N_MIX + b), b, [(bank[6 + b][:, :], u_hi, u_lo, range(DC), True, True)])

            def scores(i):
                kind, q, h = items[i]
                n = score_no[i]
                keys = P * (q + 1)
                if n >= 3:
                    pe.wait_ge(exp_done, n - 2)
                ps = bank[n % 3]
                if kind == "c":
                    heads = ps[:, :NH * CW].rearrange("p (g c i) -> p c g i", g=2, c=NH // 2)
                    for c in range(NH // 2):
                        mm = nc.tensor.matmul(heads[:, c, :, :], roped[:, 8 + c, q * P:(q + 1) * P],
                                              kcmp[:, :, :].rearrange("p g i -> p (g i)"), start=True, stop=True)
                    mm.then_inc(s_done, 1)
                    return
                tile, r = q_rows(kind, h)
                k_tile = k_a[r:r + HD, :keys] if kind == "a" else roped[r:r + HD, 6 + (kind == "w"), :keys]
                nc.tensor.matmul(ps[:, :keys], roped[r:r + HD, tile, q * P:(q + 1) * P], k_tile, start=True, stop=False)
                if kind == "a" and q:
                    pe.wait_ge(mask_ready, q)
                    mm = nc.tensor.matmul(ps[:, :keys], ident_b[:, :], mask_a[q - 1][:, :], start=False, stop=True)
                else:
                    mm = nc.tensor.matmul(ps[:, keys - P:keys], ident_b[:, :], causal_b[:, :], start=False, stop=True)
                mm.then_inc(s_done, 1)

            def turns(i):
                kind, q, h = items[i]
                if kind == "-":
                    return
                t = turn_no[i]
                if t >= 2:
                    by, count = reader[turned[t - 2]]
                    pe.wait_ge(t_read[by], count)
                ps = bank[3 + t % 2]
                if kind == "ya":
                    src, width = o_a, HC
                    pe.wait_ge(group_read, group_no["a", q] + 1)
                elif kind == "yb":
                    src, width = o_b, HC
                    pe.wait_ge(ob_ready, q + 1)
                else:
                    src = probs[score_no[i] % 3]
                    pe.wait_ge(exp_done, score_no[i] + 1)
                    width = 2 if kind == "c" else q + 1
                for t in range(width):
                    tr = nc.tensor.transpose(ps[:, t * P:(t + 1) * P], src[:, t * P:(t + 1) * P], ident)
                tr.then_inc(t_done, 1)

            def values(i):
                kind, q, h = items[i]
                if kind not in "aswc":
                    return
                n, g = score_no[i], group_no[kind, q]
                by, count = reader[i]
                pe.wait_ge(t_read[by], count)
                if g >= 3 and h == 0:
                    pe.wait_ge(group_read, g - 2)
                ps, pt = bank[5 + g % 3], probs_t[n % 2]
                if kind == "c":
                    for gg in range(2):
                        mm = nc.tensor.matmul(ps[:, gg * 4 * HD:(gg + 1) * 4 * HD], pt[:, gg * P:(gg + 1) * P],
                                              vbd[:, gg, :], start=True, stop=True)
                else:
                    for t in range(q + 1):
                        v = v_a[:, t, :] if kind == "a" else (v_s if kind == "s" else v_w)[:, t, (h // 4) * HD:(h // 4 + 1) * HD]
                        mm = nc.tensor.matmul(ps[:, h * HD:(h + 1) * HD], pt[:, t * P:(t + 1) * P], v,
                                              start=t == 0, stop=t == q)
                mm.then_inc(pv_done, 1)

            pe.wait_ge(q_scaled, 2)
            pe.wait_ge(rope_done, N_ROPE + 4)
            pe.wait_ge(v_read, 2)
            pe.wait_ge(cmp_read, 10)
            pe.wait_ge(gate_done, CREDIT + N_GATE)
            for i in range(n_items + 3):
                if i < n_items and items[i][0] in "aswc":
                    scores(i)
                if 0 <= i - 2 < n_items:
                    turns(i - 2)
                if 0 <= i - 3 < n_items:
                    values(i - 3)
            pe.wait_ge(t_read[1], counts[1])
            with pe.Fori(0, DC // 2) as it:
                for b in range(2):
                    pe.wait_ge(merge_done, it * 2 + (b + 1))
                    unit(it * 2 + (BR0 + b), b,
                         [(bank[2 * b + m][:, :], y_hi[m], y_lo[m], range(HC), True, True) for m in range(2)])
            with pe.Fori(0, DC // 2) as it:
                for b in range(2):
                    pe.wait_ge(z_done, it * 2 + (DC + b + 1))
                    unit(it * 2 + (MO0 + b), b, [(bank[4 + b][:, :], u_hi, u_lo, range(DC), True, True)],
                         (lambda k: pe.wait_ge(m_ready, k + 1)) if b == 0 else None)
            stats(1)
            ffn(1, FFN2, 2)
            stats(2)

        @block.scalar
        def _(act):
            def copy(to, of, scale=1.0):
                return nc.scalar.activation(to, of, ACT.Copy, scale=scale)

            def hi_at(base, it, per, n):
                u = base + n
                act.wait_ge(raw_loaded[u % RAW], it * (16 * per // RAW) + 16 * (u // RAW + 1))
                act.wait_ge(units_done, it * per + (u + 1))
                copy(w_hi[u % SPLIT][:, :], raw[u % RAW][:, :]).then_inc(hi_ready, 1)

            def unit_hi(u):
                if u < UNITS:
                    act.wait_ge(raw_loaded[u % RAW], 16 * (u // RAW + 1))
                    act.wait_ge(units_done, u + 1)
                    copy(w_hi[u % SPLIT][:, :], raw[u % RAW][:, :]).then_inc(hi_ready, 1)

            def inputs(p, ready):
                for k in range(DC):
                    act.wait_ge(ub_ready, p * DC + k + 1)
                    copy(u_hi[:, k, :], tmp[k % 2][:, :]).then_inc(uh_ready, 1)
                    scale, shift = ready(k)
                    nc.scalar.activation(xa[:, k, :], xa[:, k, :], ACT.Identity, scale=scale, bias=shift)\
                        .then_inc(xa_ready, 1)

            def squares(z0, u0, per):
                for c in range(DC):
                    for n in range(per):
                        unit_hi(u0 + c * per + n + 2)
                    act.wait_ge(z_done, CREDIT + z0 + c + 1)
                    nc.scalar.activation(tmp[6 + c % 2][:, :], xa[:, c, :], ACT.Square).then_inc(sq_done, 1)

            def norm(p):
                act.wait_ge(stats_done, 2 * p + 1)
                copy(tmp[2][:, :], bank[6][:, :]).then_inc(mean_ready, 1)
                act.wait_ge(var_ready, p + 1)
                nc.scalar.activation(tmp[3][:, :], tmp[3][:, :], ACT.Sqrt, bias=eps[:, :]).then_inc(std_ready, 1)

            def ffn(f, u0):
                with act.Fori(0, FC // 2) as it:
                    for jj in range(2):
                        j = it * 2 + (FC * f + jj)
                        hi_at(u0, it, 4, 2 * jj + 2)
                        act.wait_ge(units_done, it * 4 + (u0 + 2 * jj + 1 + CREDIT))
                        nc.scalar.activation(tmp[jj][:, :], bank[2 * jj][:, :], ACT.Silu).then_inc(silu_done, 1)
                        hi_at(u0, it, 4, 2 * jj + 3)
                        act.wait_ge(hmul_done, j + (CREDIT + 1))
                        act.wait_ge(consts_ready, 1)
                        copy(h_hi[:, bass.ts(it * 2 + jj, 1), :], tmp[2 + jj][:, :].unsqueeze(1)).then_inc(hh_done, 1)
                squares(2 * DC * f, u0 + 2 * FC, OUT_UNITS)

            act.sem_inc(silu_done, CREDIT)
            act.sem_inc(mix_evac, CREDIT)
            act.sem_inc(gate_done, CREDIT)
            act.wait_ge(c_loaded, 16)
            nc.scalar.activation(c_act[:, :], c_act[:, :], ACT.Silu).then_inc(c_ready, 1)
            for u in range(2):
                unit_hi(u)
            inputs(0, lambda k: (ALPHA, 0.0))
            ffn(0, 0)
            act.wait_ge(consts_ready, 7)
            norm(0)
            inputs(1, lambda k: (aff[:, 2, k:k + 1], aff[:, 3, k:k + 1]))

            def swap(to, of, rows):
                for r in range(0, rows, 64):
                    copy(to[r:r + 32, :], of[r + 32:r + 64, :])
                    last = copy(to[r + 32:r + 64, :], of[r:r + 32, :])
                return last

            act.wait_ge(units_done, CREDIT + MIX0)
            for b in range(2):
                unit_hi(MIX0 + b + 2)
                act.wait_ge(units_done, CREDIT + MIX0 + b + 1)
                if b == 0:
                    copy(small[:, :], bank[0][:, :])
                    swap(tmp[2], bank[0], HD).then_inc(mix_evac, 1)
                else:
                    copy(kvl[:, :], bank[1][:, :])
                    nc.scalar.activation(kvsq[:, :], bank[1][:, :], ACT.Square).then_inc(mix_evac, 1)
            with act.Fori(0, N_ROPE // 4) as it:
                for b in range(4):
                    hi_at(MIX0 + 2, it, 4, b + 2)
                    act.wait_ge(units_done, it * 4 + (MIX0 + 2 + b + 1 + CREDIT))
                    act.wait_ge(consts_ready, 1)
                    act.wait_ge(rope_done, it * 4 + (b + 1))
                    copy(tmp[b % 2][:, :], bank[b % 2][:, :])
                    swap(tmp[2 + b % 2], bank[b % 2], P).then_inc(mix_evac, 1)
            for n, to in ((14, kc), (15, vc), (16, vs_t), (17, vw_t)):
                unit_hi(MIX0 + n + 2)
                act.wait_ge(units_done, CREDIT + MIX0 + n + 1)
                if n == 14:
                    act.wait_ge(rope_done, 13)
                    copy(tmp[0][:, :], bank[0][:, :])
                    swap(tmp[2], bank[0], P).then_inc(mix_evac, 1)
                else:
                    copy(to[:, :], bank[n % 2][:, :]).then_inc(mix_evac, 1)
            act.wait_ge(ms_done, 1)
            nc.scalar.activation(kvsq[:, :], bank[2][:, :], ACT.Sqrt, bias=eps[:, :]).then_inc(kv_std, 1)
            act.wait_ge(small_turned, 1)
            turned = bank[3][:, :].rearrange("p (q f) -> p q f", q=QB)
            copy(wi[:, :, :], turned[:, :, HD:HD + NI], scale=NI ** -0.5).then_inc(small_read, 1)
            nc.scalar.activation(gb[:, :, :], turned[:, :, HD + NI:HD + NI + 3 * NH], ACT.Sigmoid).then_inc(small_read, 1)
            for n in range((QB - 1) * NI):
                q = 1 + n // NI
                act.wait_ge(logits_done, n + 1)
                if n >= 2:
                    act.wait_ge(acc_done, n - 1)
                else:
                    act.wait_ge(rope_done, N_ROPE + 3)
                nc.scalar.activation(tmp[n % 2][:, :P * (q + 1)], bank[4 + n % 2][:, :P * (q + 1)], ACT.Relu)\
                    .then_inc(relu_done, 1)
            act.wait_ge(kv_done, 2)
            copy(tmp[6][:, :], bank[6][:, :])
            swap(tmp[7], bank[6], P).then_inc(kv_read, 1)
            copy(v_a[:, :, :], bank[7][:, :QB * HD].rearrange("p (t d) -> p t d", t=QB)).then_inc(kv_read, 1)
            act.wait_ge(v_turned, 2)
            for n, to in enumerate((v_s, v_w)):
                copy(to[:, :, :], bank[2 + n][:, :].rearrange("p (t d) -> p t d", t=QB)).then_inc(v_read, 1)
            act.wait_ge(consts_ready, 9)
            for t in range(2):
                act.wait_ge(hid_done, t + 1)
                for hc in range(2):
                    hid = bank[t][:, hc * 64:hc * 64 + 2 * NC].rearrange("p (g i) -> p g i", g=2)
                    if t == 0:
                        nc.scalar.activation(hid_k[:, hc, :, 0:NC], hid, ACT.Silu).then_inc(hid_ready, 1)
                    else:
                        for g in range(2):
                            for r in range(4):
                                nc.scalar.activation(hid_v[:, hc, g, r, 0:NC], hid[:, g, :], ACT.Silu)\
                                    .then_inc(hid_ready, 1)
            act.wait_ge(cmp_done, 1)
            for g in range(2):
                rows = slice(g * HD, (g + 1) * HD)
                copy(kcmp[rows, g, :], bank[4][rows, g * CW:(g + 1) * CW]).then_inc(cmp_read, 1)
            act.wait_ge(cmp_done, 2)
            for g in range(2):
                for r in range(4):
                    copy(vbd[r * CW:(r + 1) * CW, g, r * HD:(r + 1) * HD],
                         bank[5][r * CW:(r + 1) * CW, g * HD:(g + 1) * HD]).then_inc(cmp_read, 1)
            with act.Fori(0, N_GATE // 4) as it:
                for b in range(4):
                    hi_at(MIX0 + N_MIX, it, 4, b + 2)
                    act.wait_ge(units_done, it * 4 + (MIX0 + N_MIX + b + 1 + CREDIT))
                    act.wait_ge(consts_ready, 1)
                    nc.scalar.activation(gates[:, bass.ts(it * 4 + b, 1), :], bank[6 + b % 2][:, :].unsqueeze(1),
                                         ACT.Sigmoid).then_inc(gate_done, 1)

            def exps(i):
                kind, q, h = items[i]
                n = score_no[i]
                act.wait_ge(max_done, n + 1)
                if n >= 3:
                    act.wait_ge(t_done, turn_no[scored[n - 3]] + 1)
                if kind == "c":
                    nc.scalar.activation(probs[n % 3][:, :NH * CW], cmp_s[:, :, :].rearrange("p h c -> p (h c)"),
                                         ACT.Exp).then_inc(exp_done, 1)
                else:
                    keys = P * (q + 1)
                    nc.scalar.activation(probs[n % 3][:, :keys], bank[n % 3][:, :keys], ACT.Exp,
                                         bias=nmax[:, n % 4:n % 4 + 1],
                                         accum_out=sums[:, q, "aswc".index(kind), h:h + 1]).then_inc(exp_done, 1)

            def reads(i):
                kind, q, h = items[i]
                if kind == "-":
                    return
                ps = bank[3 + turn_no[i] % 2]
                if kind in ("ya", "yb"):
                    m = int(kind == "yb")
                    act.wait_ge(t_done, turn_no[i] + 1)
                    copy(y_hi[m][:, :, q * P:(q + 1) * P], ps[:, :].rearrange("p (t c) -> p t c", t=HC))\
                        .then_inc(y_hi_done, 1)
                elif score_no[i] % 2 == 0:
                    n = score_no[i]
                    act.wait_ge(t_done, turn_no[i] + 1)
                    if n >= 2:
                        act.wait_ge(pv_done, n - 1)
                    width = (2 if kind == "c" else q + 1) * P
                    copy(probs_t[0][:, :width], ps[:, :width]).then_inc(t_read[0], 1)

            for i in range(n_items + 2):
                if i < n_items and items[i][0] in "aswc":
                    exps(i)
                if 0 <= i - 2 < n_items:
                    reads(i - 2)
            for c in range(DC):
                unit_hi(BR0 + c + 2)
                act.wait_ge(mf_ready, c + 1)
                copy(u_hi[:, c, :], tmp[c % 2][:, :]).then_inc(mh_done, 1)
            squares(DC, MO0, 1)
            norm(1)
            inputs(2, lambda k: (aff[:, 6, k:k + 1], aff[:, 7, k:k + 1]))
            ffn(1, FFN2)
            norm(2)
            for k in range(DC):
                act.wait_ge(ub_ready, 3 * DC + k + 1)
                nc.scalar.activation(xa[:, k, :], xa[:, k, :], ACT.Identity, scale=vec[:, V_LN + 4 * DC + k:V_LN + 4 * DC + k + 1],
                                     bias=vec[:, V_LN + 5 * DC + k:V_LN + 5 * DC + k + 1]).then_inc(final_ready, 1)

        @block.vector
        def _(dve):
            count, turn = [0], [None]

            def mark(instruction):
                instruction.then_inc(dve_step, 1)
                count[0] += 1

            def hold():
                dve.wait_ge(dve_step, count[0] if turn[0] is None else turn[0][0] * turn[0][1] + count[0])

            def step(instruction):
                mark(instruction)
                hold()

            tt = nc.vector.tensor_tensor

            def lo_at(u0, it, per, n):
                u = u0 + n
                dve.wait_ge(hi_ready, u + 1 if it is None else it * per + (u + 1))
                tt(w_lo[u % SPLIT][:, :], raw[u % RAW][:, :], w_hi[u % SPLIT][:, :].bitcast(F32), ALU.subtract)\
                    .then_inc(lo_ready, 1)

            def unit_lo(u):
                if u < UNITS:
                    lo_at(u, None, 0, 0)

            def ada_block(slot, turn, b):
                dve.wait_ge(ada_loaded[slot], turn)
                nc.vector.scalar_tensor_tensor(out=ada[slot][:, :], in0=ada[slot][:, :], scalar=1.0, in1=c_act[:, :],
                                               op0=ALU.mult, op1=ALU.mult, accum_out=mod[:, bass.ts(b, 1)])\
                    .then_inc(ada_done, 1)

            def add_bias(b0, b1):
                dve.wait_ge(ada_done, b1)
                step(tt(mod[:, b0:b1], mod[:, b0:b1], vec[:, V_BADA + b0:V_BADA + b1], ALU.add))

            def group(m):
                return mod[:, m * DC:(m + 1) * DC]

            def ln(n):
                return vec[:, V_LN + n * DC:V_LN + (n + 1) * DC]

            def prepare(at, g, b, shift, scale):
                step(nc.vector.tensor_scalar(aff[:, at + 1, :], group(scale), 1.0, None, ALU.add))
                step(tt(aff[:, at, :], aff[:, at + 1, :], ln(g), ALU.mult))
                step(tt(aff[:, at + 1, :], aff[:, at + 1, :], ln(b), ALU.mult))
                step(tt(aff[:, at + 1, :], aff[:, at + 1, :], group(shift), ALU.add))
                step(nc.vector.tensor_scalar(aff[:, at + 2, :], ln(g), ALPHA, None, ALU.mult))
                step(nc.vector.tensor_scalar(aff[:, at + 3, :], ln(b), ALPHA, None, ALU.mult))

            def inputs(p, scale, shift, normed):
                def lo(k):
                    dve.wait_ge(uh_ready, p * DC + k + 1)
                    tt(u_lo[:, k, :], tmp[k % 2][:, :], u_hi[:, k, :].bitcast(F32), ALU.subtract).then_inc(u_ready, 1)

                for k in range(DC):
                    if normed:
                        step(tt(xa[:, k, :], xa[:, k, :], tmp[2][:, :], ALU.subtract))
                        step(tt(xa[:, k, :], xa[:, k, :], tmp[3][:, :], ALU.mult))
                    if k >= 2:
                        dve.wait_ge(u_ready, p * DC + k - 1)
                    nc.vector.tensor_scalar(tmp[k % 2][:, :], xa[:, k, :], scale(k), shift(k), ALU.mult, ALU.add)\
                        .then_inc(ub_ready, 1)
                    if k:
                        lo(k - 1)
                lo(DC - 1)

            def outputs(z0, u0, per, gate, sublayer):
                step(nc.vector.memset(tmp[4][:, :], 0.0))
                step(nc.vector.memset(tmp[5][:, :], 0.0))
                for c in range(DC):
                    for n in range(per):
                        unit_lo(u0 + c * per + n + 2)
                    if sublayer == 0:
                        b = ADA_START + 2 * FC + c
                        ada_block(b % ADA_RING, 16 * (b // ADA_RING + 1), b)
                    dve.wait_ge(units_done, CREDIT + u0 + (c + 1) * per)
                    dve.wait_ge(xa_ready, DC * sublayer + c + 1)
                    nc.vector.scalar_tensor_tensor(out=xa[:, c, :], in0=bank[4 + c % 2][:, :], scalar=gate(c),
                                                   in1=xa[:, c, :], op0=ALU.mult, op1=ALU.add).then_inc(z_done, 1)
                    dve.wait_ge(z_done, CREDIT + z0 + c + 1)
                    add = tt(tmp[4][:, :], tmp[4][:, :], xa[:, c, :], ALU.add)
                    if c == DC - 1:
                        add.then_inc(sum_ready, 1)
                    else:
                        step(add)
                    dve.wait_ge(sq_done, z0 + c + 1)
                    add = tt(tmp[5][:, :], tmp[5][:, :], tmp[6 + c % 2][:, :], ALU.add)
                    if c == DC - 1:
                        add.then_inc(sum_ready, 1)
                    else:
                        step(add)

            def norm(p):
                dve.wait_ge(mean_ready, p + 1)
                step(tt(tmp[3][:, :], tmp[2][:, :], tmp[2][:, :], ALU.mult))
                dve.wait_ge(stats_done, 2 * p + 2)
                step(tt(tmp[3][:, :], bank[7][:, :], tmp[3][:, :], ALU.subtract))
                nc.vector.tensor_scalar(tmp[3][:, :], tmp[3][:, :], 0.0, None, ALU.max).then_inc(var_ready, 1)
                dve.wait_ge(std_ready, p + 1)
                step(nc.vector.reciprocal(tmp[3][:, :], tmp[3][:, :]))

            def ffn(f, u0, sublayer):
                with dve.Fori(0, FC // 2) as it:
                    for jj in range(2):
                        j = it * 2 + (FC * f + jj)
                        for n in range(2):
                            lo_at(u0, it, 4, 2 * jj + n + 2)
                            if f == 0:
                                k = 2 * jj + n
                                ada_block(k % ADA_RING, it * (16 * 4 // ADA_RING) + 16 * ((ADA_START + k) // ADA_RING + 1),
                                          it * 4 + (ADA_START + k))
                        dve.wait_ge(units_done, it * 4 + (u0 + 2 * jj + 2 + CREDIT))
                        dve.wait_ge(silu_done, j + (CREDIT + 1))
                        tt(tmp[2 + jj][:, :], bank[2 * jj + 1][:, :], tmp[jj][:, :], ALU.mult).then_inc(hmul_done, 1)
                        dve.wait_ge(hh_done, j + 1)
                        tt(h_lo[:, bass.ts(it * 2 + jj, 1), :], tmp[2 + jj][:, :].unsqueeze(1),
                           h_hi[:, bass.ts(it * 2 + jj, 1), :].bitcast(F32), ALU.subtract).then_inc(h_ready, 1)
                if f == 0:
                    add_bias(ADA_FIRST, ADA_START + 2 * FC)
                    step(nc.vector.tensor_scalar(group(2), group(2), 0.5, None, ALU.mult))
                    prepare(0, 0, 1, 3, 4)
                    prepare(4, 2, 3, 6, 7)
                m = 2 if f == 0 else 8
                outputs(2 * DC * f, u0 + 2 * FC, OUT_UNITS, lambda c: mod[:, m * DC + c:m * DC + c + 1], sublayer)

            dve.sem_inc(hmul_done, CREDIT)
            dve.sem_inc(z_done, CREDIT)
            dve.sem_inc(merge_done, CREDIT)
            dve.wait_ge(c_ready, 1)
            for b in range(ADA_FIRST):
                ada_block(b % ADA_RING, 16 * (b // ADA_RING + 1), b)
            dve.wait_ge(vec_loaded, 16)
            add_bias(0, ADA_FIRST)
            step(nc.vector.tensor_scalar(aff[:, 0, :], group(1), 1.0, None, ALU.add))
            dve.wait_ge(x_loaded, 16 * DC)
            inputs(0, lambda k: aff[:, 0, k:k + 1], lambda k: mod[:, k:k + 1], False)
            unit_lo(0)
            unit_lo(1)
            for b in range(ADA_FIRST, ADA_START):
                ada_block(b % ADA_RING, 16 * (b // ADA_RING + 1), b)
            ffn(0, 0, 0)
            add_bias(ADA_START + 2 * FC, NADA)
            step(nc.vector.tensor_scalar(group(8), group(8), 0.5, None, ALU.mult))
            norm(0)
            inputs(1, lambda k: aff[:, 0, k:k + 1], lambda k: aff[:, 1, k:k + 1], True)

            def rotate(to, x, turned, rows, count, part):
                tt(part[:rows, :], x[:rows, :], cos[:rows, :], ALU.mult)
                step(tt(turned[:rows, :], turned[:rows, :], sin[:rows, :], ALU.mult))
                tt(to, part[:rows, :] if count is None else part[:rows, :].unsqueeze(1),
                   turned[:rows, :] if count is None else turned[:rows, :].unsqueeze(1), ALU.add).then_inc(rope_done, 1)

            dve.wait_ge(rope_loaded, 16)
            unit_lo(MIX0 + 2)
            dve.wait_ge(mix_evac, CREDIT + 1)
            rotate(ki2[:HD, :], small, tmp[2], HD, None, tmp[4])
            dve.wait_ge(rope_done, 1)
            nc.vector.tensor_copy(ki2[HD:, :], ki2[:HD, :]).then_inc(rope_done, 1)
            unit_lo(MIX0 + 3)
            with dve.Fori(0, N_ROPE // 4) as it:
                turn[0] = (it, 4)
                for b in range(4):
                    lo_at(MIX0 + 2, it, 4, b + 2)
                    dve.wait_ge(mix_evac, it * 4 + (CREDIT + 2 + b + 1))
                    dve.wait_ge(rope_done, it * 4 + (b + 1))
                    rotate(roped[:, bass.ts(it * 4 + b, 1), :], tmp[b % 2], tmp[2 + b % 2], P, 1, tmp[4 + b % 2])
                turn[0], count[0] = None, count[0] + 4 * (N_ROPE // 4 - 1)
            unit_lo(MIX0 + 16)
            dve.wait_ge(mix_evac, CREDIT + 15)
            dve.wait_ge(rope_done, N_ROPE + 1)
            rotate(kc[:, :], tmp[0], tmp[2], P, None, tmp[4])
            for t, src in enumerate((kc, vc)):
                unit_lo(MIX0 + 17 + t)
                if t == 0:
                    dve.wait_ge(rope_done, N_ROPE + 3)
                else:
                    dve.wait_ge(mix_evac, CREDIT + 16)
                for par in range(2):
                    for g in range(2):
                        rows = slice(g * HD, (g + 1) * HD)
                        x = src[rows, :].rearrange("p (i l a) -> p a l i", i=S // 16, l=8, a=2)
                        for half in range(2):
                            dst = cmp_in[t][par * HD:(par + 1) * HD, half * 8:(half + 1) * 8, g, :]
                            pe_v = pe_tab[t][rows, par, half * 8:(half + 1) * 8].unsqueeze(2).to_broadcast([HD, 8, NC])
                            add = tt(dst, x[:, par, :, half:half + NC], pe_v, ALU.add)
                        add.then_inc(cmp_in_ready, 1)
            unit_lo(MIX0 + 19)
            dve.wait_ge(kv_std, 1)
            step(nc.vector.reciprocal(kvsq[:, :], kvsq[:, :]))
            nc.vector.scalar_tensor_tensor(out=kvl[:, :], in0=kvl[:, :], scalar=vec[:, V_KVG:V_KVG + 1], in1=kvsq[:, :],
                                           op0=ALU.mult, op1=ALU.mult).then_inc(kvn_ready, 1)
            dve.wait_ge(small_read, 1)
            for n in range((QB - 1) * NI):
                q, h = 1 + n // NI, n % NI
                a, r = acc[q - 1][:, :], tmp[n % 2][:, :P * (q + 1)]
                dve.wait_ge(relu_done, n + 1)
                if h == 0:
                    nc.vector.tensor_scalar(a, r, wi[:, q, h:h + 1], None, ALU.mult).then_inc(acc_done, 1)
                else:
                    dve.wait_ge(acc_done, n)
                    nc.vector.scalar_tensor_tensor(out=a, in0=r, scalar=wi[:, q, h:h + 1], in1=a,
                                                   op0=ALU.mult, op1=ALU.add).then_inc(acc_done, 1)
            dve.wait_ge(acc_done, (QB - 1) * NI)
            for q in range(1, QB):
                last = acc[q - 1][:, q * P:]
                step(tt(last, last, causal, ALU.add))
            dve.wait_ge(kv_read, 1)
            rotate(k_a[:, :], tmp[6], tmp[7], P, None, tmp[5])
            with dve.Fori(0, N_GATE // 4) as it:
                turn[0] = (it, 2 * 4)
                for b in range(4):
                    u = MIX0 + N_MIX + b + 2
                    lo = [lambda cols=slice(x * UW // 2, (x + 1) * UW // 2): tt(
                        w_lo[u % SPLIT][:, cols], raw[u % RAW][:, cols], w_hi[u % SPLIT][:, cols].bitcast(F32),
                        ALU.subtract) for x in range(2)]
                    hold()
                    dve.wait_ge(hi_ready, it * 4 + (u + 1))
                    lo[0]()
                    for q in range(3):
                        last = nc.vector.max(max8[:, q, :], acc[q][:, :])
                    mark(last)
                    hold()
                    lo[1]().then_inc(lo_ready, 1)
                    for q in range(3):
                        last = nc.vector.match_replace(acc[q][:, :], max8[:, q, :], acc[q][:, :], TAKEN)
                    mark(last)
                turn[0], count[0] = None, count[0] + 2 * 4 * (N_GATE // 4 - 1)
            hold()
            for q in range(3):
                nc.vector.tensor_scalar(mask_a[q][:, :], acc[q][:, :], TAKEN / 2, NEG, ALU.is_gt, ALU.mult)\
                    .then_inc(mask_ready, 1)

            def maxima(i):
                kind, q, h = items[i]
                n = score_no[i]
                dve.wait_ge(s_done, n + 1)
                ps = bank[n % 3]
                if kind != "c":
                    if n >= 4:
                        dve.wait_ge(exp_done, n - 3)
                    nc.vector.tensor_reduce(nmax[:, n % 4:n % 4 + 1], ps[:, :P * (q + 1)], AX, ALU.max, negate=True)\
                        .then_inc(max_done, 1)
                    return
                mask = cmp_mask[:, q, :].unsqueeze(1).to_broadcast([P, NH, CW])
                step(tt(cmp_s[:, :, :], ps[:, :NH * CW].rearrange("p (h c) -> p h c", h=NH), mask, ALU.add))
                step(nc.vector.tensor_reduce(nmax[:, 4:], cmp_s[:, :, :], AX, ALU.max, negate=True))
                tt(cmp_s[:, :, :], cmp_s[:, :, :], nmax[:, 4:].unsqueeze(2).to_broadcast([P, NH, CW]), ALU.add)\
                    .then_inc(max_done, 1)

            def reads(i):
                kind, q, h = items[i]
                if kind == "-":
                    return
                ps = bank[3 + turn_no[i] % 2]
                if kind == "c":
                    n = score_no[i]
                    dve.wait_ge(exp_done, n + 1)
                    p = probs[n % 3][:, :NH * CW].rearrange("p (h c) -> p h c", h=NH)
                    step(nc.vector.tensor_reduce(sums[:, q, 3, :], p, AX, ALU.add))
                if kind in ("ya", "yb"):
                    m = int(kind == "yb")
                    dve.wait_ge(y_hi_done, 2 * q + m + 1)
                    tt(y_lo[m][:, :, q * P:(q + 1) * P], ps[:, :].rearrange("p (t c) -> p t c", t=HC),
                       y_hi[m][:, :, q * P:(q + 1) * P].bitcast(F32), ALU.subtract).then_inc(t_read[1], 1)
                elif score_no[i] % 2:
                    n = score_no[i]
                    dve.wait_ge(t_done, turn_no[i] + 1)
                    if n >= 2:
                        dve.wait_ge(pv_done, n - 1)
                    width = (2 if kind == "c" else q + 1) * P
                    nc.vector.tensor_copy(probs_t[1][:, :width], ps[:, :width]).then_inc(t_read[1], 1)

            def finish(g, kind, q):
                n = "aswc".index(kind)
                dve.wait_ge(pv_done, group_end[g] + 1)
                step(nc.vector.reciprocal(fac[:, n, :], sums[:, q, n, :]))
                if kind != "a":
                    gate = {"c": 0, "s": NH, "w": 2 * NH}[kind]
                    step(tt(fac[:, n, :], fac[:, n, :], gb[:, q, gate:gate + NH], ALU.mult))
                if kind == "c":
                    step(nc.vector.tensor_scalar(fac[:, n, :], fac[:, n, :],
                                                       con[:, C_VALID + q:C_VALID + q + 1], None, ALU.mult))
                if kind in "as" and q:
                    before = items.index(("ya" if kind == "a" else "yb", q - 1, 0))
                    dve.wait_ge(t_done, turn_no[before] + 1)
                f = fac[:, n, :].unsqueeze(2).to_broadcast([P, NH, HD])
                ps = bank[5 + g % 3][:, :].rearrange("p (h d) -> p h d", h=NH)
                to = {"a": o_a, "s": o_b}.get(kind, o_tmp)
                tt(to[:, :].rearrange("p (h d) -> p h d", h=NH), ps, f, ALU.mult).then_inc(group_read, 1)
                dve.wait_ge(group_read, g + 1)
                if kind == "w":
                    step(tt(o_b[:, :], o_b[:, :], o_tmp[:, :], ALU.add))
                if kind == "c":
                    tt(o_b[:, :], o_b[:, :], o_tmp[:, :], ALU.add).then_inc(ob_ready, 1)

            ends = {}
            for g, n in group_end.items():
                ends.setdefault(scored[n] + 4, []).append(g)
            names = {g: kq for kq, g in group_no.items()}
            for i in range(n_items + 6):
                if i < n_items and items[i][0] in "aswc":
                    maxima(i)
                if 0 <= i - 2 < n_items:
                    reads(i - 2)
                for g in ends.get(i, []):
                    finish(g, *names[g])

            for c in range(DC):
                unit_lo(BR0 + c + 2)
                b = c % 2
                dve.wait_ge(units_done, CREDIT + BR0 + c + 1)
                tt(tmp[b][:, :], bank[2 * b][:, :], gates[:, c, :], ALU.mult)
                tt(tmp[2 + b][:, :], bank[2 * b + 1][:, :], gates[:, DC + c, :], ALU.mult).then_inc(merge_done, 1)
                dve.wait_ge(merge_done, CREDIT + c + 1)
                tt(tmp[b][:, :], tmp[b][:, :], tmp[2 + b][:, :], ALU.add).then_inc(mf_ready, 1)
                dve.wait_ge(mh_done, c + 1)
                tt(u_lo[:, c, :], tmp[b][:, :], u_hi[:, c, :].bitcast(F32), ALU.subtract).then_inc(m_ready, 1)
            outputs(DC, MO0, 1, lambda c: mod[:, 5 * DC + c:5 * DC + c + 1], 1)
            norm(1)
            inputs(2, lambda k: aff[:, 4, k:k + 1], lambda k: aff[:, 5, k:k + 1], True)
            ffn(1, FFN2, 2)
            norm(2)
            for k in range(DC):
                step(tt(xa[:, k, :], xa[:, k, :], tmp[2][:, :], ALU.subtract))
                tt(xa[:, k, :], xa[:, k, :], tmp[3][:, :], ALU.mult).then_inc(ub_ready, 1)


def _layout(inputs, np):
    f = {k: np.asarray(v) for k, v in inputs.items()}

    def unit_blocks(w):
        k, n = w.shape
        return w.reshape(k // P, P, n // P, P).transpose(2, 1, 0, 3).reshape(n // P, P, k)

    def ffn(w_in, w_out):
        a, b = unit_blocks(w_in[:, :FF]), unit_blocks(w_in[:, FF:])
        first = np.stack([a, b], 1).reshape(2 * FC, P, UW)
        o = unit_blocks(w_out)
        o = np.concatenate([o, np.zeros((DC, P, OUT_UNITS * UW - FF), o.dtype)], 2)
        return [first, o.reshape(DC, P, OUT_UNITS, UW).transpose(0, 2, 1, 3).reshape(OUT_UNITS * DC, P, UW)]

    w = f["w_mix_in"][0]
    cut = np.cumsum([NH * HD, P, NI * HD, HD, NI, NH * HD, 6 * P, 3 * NH, 2 * D])
    qa, kv, qi, ki, wi, qb, kv6, gb, gm = np.split(w, cut[:-1], axis=1)
    small = np.concatenate([ki, wi, gb, np.zeros((D, P - HD - NI - 3 * NH), w.dtype)], 1)
    pairs = np.arange(NH).reshape(2, NH // 2).T.ravel()
    qb = qb.reshape(D, NH, HD)[:, pairs, :].reshape(D, NH * HD)
    kc, vc, ks, vs, kw, vw = np.split(kv6, 6, axis=1)
    mix = unit_blocks(np.concatenate([small, kv, qi, qa, ks, kw, qb, kc, vc, vs, vw, gm], 1))
    br = np.concatenate([unit_blocks(f["w_br_a"][0]), unit_blocks(f["w_br_b"][0])], 2)
    stream = np.concatenate(
        ffn(f["ffn1_w_in"][0], f["ffn1_w_out"][0]) + [mix, br, unit_blocks(f["w_mix_out"][0])]
        + ffn(f["ffn2_w_in"][0], f["ffn2_w_out"][0]), 0)

    def col(v):
        return v.reshape(-1, P).T

    vecs = np.concatenate([col(f[k][0]) for k in ("b_ada", "ln1_g", "ln1_b", "ln2_g", "ln2_b", "ln3_g", "ln3_b", "kv_norm_g")], 1)
    up = f["w_kv_up"][0]
    w2k = f["cmp_w2_k"][0].reshape(2, P, HD).transpose(1, 0, 2)
    w2v = f["cmp_w2_v"][0].reshape(2, P, HD).transpose(1, 0, 2)

    def pe(v):
        v = v.reshape(CL2, 2, HD).transpose(2, 1, 0).reshape(HD, 2 * CL2)
        return np.concatenate([v, v], 0)

    small_w = np.concatenate([
        np.concatenate([w2k, w2k], 2).reshape(P, 4 * HD), w2v.reshape(P, 2 * HD),
        up[:, :HD], up[:, :HD], up[:, HD:], pe(f["cmp_pe_k"][0]), pe(f["cmp_pe_v"][0])], 1)
    cmp_w1 = np.stack([f[k][0].reshape(CL2, P, 2 * P).transpose(1, 0, 2) for k in ("cmp_w1_k", "cmp_w1_v")], 1)

    row = np.arange(P)
    consts = np.zeros((P, C_N), np.float32)
    consts[:, C_ID:C_ID + P] = np.eye(P)
    consts[:, C_CAUSAL:C_CAUSAL + P] = np.where(row[None, :] <= row[:, None], 0.0, NEG)
    token = row[:, None, None] + P * np.arange(QB)[None, :, None]
    block = np.arange(CW)[None, None, :]
    seen = (block < NC) & (16 * block + 31 <= token)
    consts[:, C_CMP:C_VALID] = np.where(seen, 0.0, NEG).reshape(P, QB * CW)
    consts[:, C_VALID:] = seen.any(2)
    half = HD // 2
    inv = (10000.0 ** (-np.arange(half) / half)).astype(np.float32)
    ang = (np.arange(S, dtype=np.float32)[None, :] * inv[:, None]).astype(np.float32)
    cos, sin = np.cos(ang).astype(np.float32), np.sin(ang).astype(np.float32)
    rope = np.stack([np.concatenate([cos] * 4, 0), np.concatenate([-sin, sin, -sin, sin], 0)], 1)

    c = np.ascontiguousarray
    return {
        "x_t": c(f["x"][0].T.reshape(DC, P, S).transpose(1, 0, 2)),
        "c_row": c(f["c"].reshape(1, D)),
        "w_ada_t": c(f["w_ada"][0].T.reshape(NADA, P, D)),
        "vecs": c(vecs),
        "consts": consts,
        "rope_tab": c(rope),
        "small_w": c(small_w),
        "cmp_w1": c(cmp_w1.reshape(P, 2, CL2, 2 * P)),
        "stream": c(stream),
    }


def kernel(**inputs):
    import numpy as np
    import concourse.bacc as bacc
    from concourse.bass_utils import run_bass_kernel_spmd

    arrays = _layout(inputs, np)
    nc = bacc.Bacc("TRN2", target_bir_lowering=False, num_devices=1)
    args = [nc.dram_tensor(k, a.shape, mybir.dt.from_np(a.dtype), kind="ExternalInput").ap()
            for k, a in arrays.items()]
    out = nc.dram_tensor("out", (P, DC, S), F32, kind="ExternalOutput").ap()
    decoder_layer(nc, *args, out)
    got = run_bass_kernel_spmd(nc, [arrays], core_ids=[0]).results[0]["out"]
    return np.ascontiguousarray(got.transpose(1, 0, 2).reshape(D, S).T).reshape(1, S, D)
```

```python
from contextlib import ExitStack

import concourse.bass as bass
from concourse import mybir

F32 = mybir.dt.float32
F32R = mybir.dt.float32r
BF16 = mybir.dt.bfloat16
ACT = mybir.ActivationFunctionType
ALU = mybir.AluOpType
AX = mybir.AxisListType.X

P = 128
S = 512
D = 1024
DC = D // P
FF = 2816
FC = FF // P
HD = 64
QB = S // P
NH = 8
HC = NH * HD // P
NI = 4
TOPK = S // 4
ALPHA = 2.0 ** 0.25
EPS = 1e-5
NEG = -1e30
TAKEN = -3e38
NMOD = 9
NADA = NMOD * DC
NC = 31
CW = 32
CL2 = 16

UW = DC * P
OUT_UNITS = 3
FFN_UNITS = 2 * FC + OUT_UNITS * DC
MIX0 = FFN_UNITS
N_ROPE = 12
N_MIX = 18
N_GATE = 2 * DC
BR0 = MIX0 + N_MIX + N_GATE
MO0 = BR0 + DC
FFN2 = MO0 + DC
UNITS = FFN2 + FFN_UNITS
RAW = 4
SPLIT = 2
CREDIT = 2
ADA_FIRST = 2 * DC
ADA_LATE = ADA_FIRST + 2 * FC
ADA_RING = 2
TURN_LAG, VALUE_LAG, SUM_LAG, CUT_LAG = 4, 6, 7, 8
ADA_WITH = [[ADA_LATE + 2 * c, ADA_LATE + 2 * c + 1] if c < 4 else [ADA_LATE + 4 + c] for c in range(DC)]

V_BADA, V_LN, V_KVG = 0, NADA, NADA + 6 * DC
V_N = V_KVG + 1
C_ID, C_CAUSAL, C_CMP, C_VALID = 0, P, 2 * P, 2 * P + QB * CW
C_N = C_VALID + QB
M_W2K, M_W2V, M_WK, M_WV, M_PEK, M_PEV = 0, 256, 384, 512, 576, 608
M_N = 640


def batch(q):
    return max(1, S // (P * (q + 1)))


def schedule():
    items = []
    for q in range(QB):
        items += [("a", q, h) for h in range(0, NH, batch(q))]
        items.append(("c", q, 0))
        for g in range(2):
            items += [(kind, q, h) for kind in "sw" for h in range(4 * g, 4 * g + 4, batch(q))]
    return items


def decoder_layer(nc, x_t, c_row, w_ada_t, vecs, consts, rope_tab, small_w, cmp_w1, stream, out):
    items = schedule()
    n_items = len(items)
    pairs = []
    for i, (kind, q, h) in enumerate(items):
        if kind == "c":
            continue
        if batch(q) == 1 and h % 2:
            pairs[-1][1].append(i)
        else:
            pairs.append((4 * q + 2 * (kind != "a") + h // 4, [i]))
    pair_of = {i: (u, part) for u, (_, its) in enumerate(pairs) for part, i in enumerate(its)}
    cut_no = {i: n for n, i in enumerate(pair_of)}
    result_end = {r: its[-1] for r, its in pairs}
    last_a = {q: max(i for i, it in enumerate(items) if it[:2] == ("a", q)) for q in range(QB)}
    last_b = {q: max(i for i, it in enumerate(items) if it[:2] == ("w", q)) for q in range(QB)}

    ctx = ExitStack()
    with ctx:
        def sb(name, shape, dt=F32, stack=ctx):
            return stack.enter_context(nc.sbuf_tensor(name, shape, dt))

        def sem(name):
            return ctx.enter_context(nc.semaphore(name))

        xa = sb("xa", [P, DC, S])
        raw = [sb(f"raw{i}", [P, UW]) for i in range(RAW)]
        w_hi = [sb(f"w_hi{i}", [P, UW], F32R) for i in range(SPLIT)]
        w_lo = [sb(f"w_lo{i}", [P, UW], F32R) for i in range(SPLIT)]
        tmp = [sb(f"tmp{i}", [P, S]) for i in range(8)]
        vec = sb("vec", [P, V_N])
        con = sb("con", [P, C_N])
        smw = sb("smw", [P, M_N])
        mod = sb("mod", [P, NADA])
        aff = sb("aff", [P, 12, DC])
        ones_d = sb("ones_d", [P, P])
        ones_r = sb("ones_r", [P, P])
        eps = sb("eps", [P, 1])
        warm = sb("warm", [P, 1])
        ident_b = sb("ident_b", [P, P], BF16)
        causal_b = sb("causal_b", [P, P], BF16)
        wi = sb("wi", [P, QB, NI])
        gb = sb("gb", [P, QB, 3 * NH])
        kcmp = sb("kcmp", [P, 2, CW])
        vbd = sb("vbd", [P, 2, 4 * HD])
        sums = sb("sums", [P, QB, 4, NH])
        fac = sb("fac", [P, 4, NH])
        nmax = sb("nmax", [P, 4, 4])
        nmax_c = sb("nmax_c", [P, NH])
        ub = [tmp[0], tmp[1], tmp[6], tmp[7]]
        max8 = sb("max8", [P, 3, 8])

        with ExitStack() as use_u:
            u_hi = sb("u_hi", [P, DC, S], F32R, use_u)
            u_lo = sb("u_lo", [P, DC, S], F32R, use_u)
        y_hi = [sb(f"y_hi{m}", [P, HC, S], F32R) for m in range(2)]
        y_lo = [sb(f"y_lo{m}", [P, HC, S], F32R) for m in range(2)]
        k_a = tmp[4]
        probs = [tmp[i] for i in (0, 1, 2, 5, 7)]
        y_part, y_sum = tmp[3], tmp[4]
        probs_t_hi, probs_t_lo = w_hi, w_lo
        cmp_s = tmp[6][:, :NH * CW].rearrange("p (h c) -> p h c", h=NH)
        cmp_t = tmp[6][:, NH * CW:]

        with ExitStack() as use_start:
            ada_first = sb("ada_first", [P, ADA_FIRST, D], F32, use_start)
        with ExitStack() as use_ffn:
            h_hi = sb("h_hi", [P, FC, S], F32R, use_ffn)
            h_lo = sb("h_lo", [P, FC, S], F32R, use_ffn)
            ada = [sb(f"ada{i}", [P, D], F32, use_ffn) for i in range(ADA_RING)]
            c_act = sb("c_act", [P, D], F32, use_ffn)
        with ExitStack() as mixers:
            with ExitStack() as use_rope:
                roped = sb("roped", [P, N_ROPE, S], F32, use_rope)
            v_s = sb("v_s", [P, QB * 2, 2, HD], F32R, mixers)
            sb("rest_of_roped", [P, (N_ROPE - 2) * S], F32, mixers)
            v_a = sb("v_a", [P, QB, 2, HD], F32R, mixers)
            v_w = sb("v_w", [P, QB * 2, 2, HD], F32R, mixers)
            mask_a = [sb(f"mask_a{q}", [P, P * (q + 1)], BF16, mixers) for q in range(1, QB)]
        m_hi = sb("m_hi", [P, DC, S], F32R)
        m_lo = sb("m_lo", [P, DC, S], F32R)
        sb("rest_of_masks", [P, 64])
        gates = sb("gates", [P, N_GATE, S])
        w1 = gates[:, :, :].rearrange("p a b -> p (a b)").rearrange("p (t l n) -> p t l n", t=2, l=CL2)
        with ExitStack() as early:
            ki2 = sb("ki2", [P, S], F32, early)
            small = sb("small", [P, S], F32, early)
            kvl = sb("kvl", [P, S], F32, early)
            kvsq = sb("kvsq", [P, S], F32, early)
            kc = sb("kc", [P, S], F32, early)
            vc = sb("vc", [P, S], F32, early)
            vs_t = sb("vs_t", [P, S], F32, early)
            vw_t = sb("vw_t", [P, S], F32, early)
            cmp_in = [sb(f"cmp_in{t}", [P, CL2, 2, NC], F32, early) for t in range(2)]
            hid_k = sb("hid_k", [P, 2, 2, CW], F32, early)
            hid_v = sb("hid_v", [P, 2, 2, 4, CW], F32, early)
            cs_tab = sb("cs_tab", [P, 2, S], F32, early)
            acc = [sb(f"acc{q}", [P, P * (q + 1)], F32, early) for q in range(1, QB)]
        k_hi = sb("k_hi", [P, 5, S], F32R)
        k_lo = sb("k_lo", [P, 5, S], F32R)
        q_cut = [sb(f"q_cut{m}", [P, NH, P], F32R) for m in range(2)]

        bank = [ctx.enter_context(nc.psum_tensor(f"bank{i}", [P, S], F32)) for i in range(8)]

        ident = con[:, C_ID:C_ID + P]
        causal = con[:, C_CAUSAL:C_CAUSAL + P]
        cmp_mask = con[:, C_CMP:C_VALID].rearrange("p (q c) -> p q c", q=QB)
        cos, sin = cs_tab[:, 0, :], cs_tab[:, 1, :]
        w2k = smw[:, M_W2K:M_W2V].rearrange("p (a b) -> p a b", a=2)
        w2v = smw[:, M_W2V:M_WK].rearrange("p (a b) -> p a b", a=2)
        pe_tab = [smw[:, o:o + 32].rearrange("p (a l) -> p a l", a=2) for o in (M_PEK, M_PEV)]

        c_loaded, vec_loaded, con_loaded = sem("c_loaded"), sem("vec_loaded"), sem("con_loaded")
        rope_loaded, w1_loaded = sem("rope_loaded"), sem("w1_loaded")
        raw_loaded = [sem(f"raw_loaded{i}") for i in range(RAW)]
        chunk_loaded = [sem(f"chunk_loaded{k}") for k in range(DC)]
        ada_loaded = [sem(f"ada_loaded{i}") for i in range(ADA_RING)]
        hi_ready, lo_ready = sem("hi_ready"), sem("lo_ready")
        units_done = sem("units_done")
        consts_ready = sem("consts_ready")
        c_ready, ada_done = sem("c_ready"), sem("ada_done")
        silu_done, hmul_done, hh_done, h_ready = sem("silu_done"), sem("hmul_done"), sem("hh_done"), sem("h_ready")
        z_done, sq_done, added_done = sem("z_done"), sem("sq_done"), sem("added_done")
        centred, t_ready = sem("centred"), sem("t_ready")
        sum_ready, stats_done = sem("sum_ready"), sem("stats_done")
        mean_ready, mean2_ready = sem("mean_ready"), sem("mean2_ready")
        var_ready, std_ready = sem("var_ready"), sem("std_ready")
        ub_ready, uh_ready, u_ready, xa_ready = sem("ub_ready"), sem("uh_ready"), sem("u_ready"), sem("xa_ready")
        mix_evac, rope_done = sem("mix_evac"), sem("rope_done")
        ms_done, kv_std, kvn_ready = sem("ms_done"), sem("kv_std"), sem("kvn_ready")
        small_turned, small_read = sem("small_turned"), sem("small_read")
        logits_done, relu_done, acc_done = sem("logits_done"), sem("relu_done"), sem("acc_done")
        kv_done, kv_read = sem("kv_done"), sem("kv_read")
        v_turned, v_read = sem("v_turned"), sem("v_read")
        cmp_in_ready, hid_done, hid_ready = sem("cmp_in_ready"), sem("hid_done"), sem("hid_ready")
        cmp_done, cmp_read = sem("cmp_done"), sem("cmp_read")
        gate_done, q_scaled, mask_ready = sem("gate_done"), sem("q_scaled"), sem("mask_ready")
        s_done, max_done, exp_done = sem("s_done"), sem("max_done"), sem("exp_done")
        fac_ready, scaled = sem("fac_ready"), sem("scaled")
        t_done, t_hi_done, t_read, pv_done = sem("t_done"), sem("t_hi_done"), sem("t_read"), sem("pv_done")
        y_part_ready, y_summed = sem("y_part_ready"), sem("y_summed")
        y_hi_done, y_ready = sem("y_hi_done"), sem("y_ready")
        k_hi_done, k_ready = sem("k_hi_done"), sem("k_ready")
        v_cut, q_hi_done, q_ready = sem("v_cut"), sem("q_hi_done"), sem("q_ready")
        merge_done, mf_ready, mh_done, m_ready = sem("merge_done"), sem("mf_ready"), sem("mh_done"), sem("m_ready")
        final_ready, stored = sem("final_ready"), sem("stored")
        dve_step = sem("dve_step")

        key_pieces = [(0, k_a[:, :], slice(0, P), slice(0, P))]
        for g in range(2):
            for at in (0, HD):
                for n in range(2):
                    rows = slice(g * HD, (g + 1) * HD)
                    key_pieces.append((1 + 2 * n + g, roped[rows, 6 + n, :], rows, slice(at, at + HD)))

        def query_pieces(m, q):
            pieces = []
            for r in range(2):
                rows = slice(r * HD, (r + 1) * HD)
                src = roped[rows, (2, 8)[m]:(2, 8)[m] + 4, q * P:(q + 1) * P]
                heads = slice(r, NH, 2) if m == 0 else slice(r * 4, r * 4 + 4)
                other = slice((1 - r) * HD, (2 - r) * HD)
                pieces.append((src, q_cut[m][rows, heads, :], q_cut[m][other, heads, :]))
            return pieces

        def pair_heads(tile, q, t):
            heads = max(2, batch(q))
            apart = S if batch(q) == 1 else P * (q + 1)
            return tile[:, :heads * apart].rearrange("p (h k) -> p h k", h=heads)[:, :, t * P:(t + 1) * P]

        def y_cut(tile, r):
            q, x = r // 4, r % 2
            return tile[r % 4 // 2][:, 2 * x:2 * x + 2, q * P:(q + 1) * P]

        block = ctx.enter_context(nc.Block())

        @block.sync
        def _(sp):
            def load_unit(slot, u):
                src = stream[bass.ts(u, 1), :, :].rearrange("a p n -> (a p) n")
                sp.dma_start(raw[slot][:, :], src).then_inc(raw_loaded[slot], 16)

            def load_ada(slot, b):
                src = w_ada_t[bass.ts(b, 1), :, :].rearrange("a p n -> (a p) n")
                sp.dma_start(ada[slot][:, :], src).then_inc(ada_loaded[slot], 16)

            def units(first, count, with_ada=False):
                with sp.Fori(0, count // RAW) as it:
                    for k in range(RAW):
                        sp.wait_ge(lo_ready, it * RAW + (first + k - RAW + 1))
                        load_unit((first + k) % RAW, it * RAW + (first + k))
                        if with_ada:
                            sp.wait_ge(ada_done, it * RAW + (ADA_FIRST + k - ADA_RING + 1))
                            load_ada(k % ADA_RING, it * RAW + (ADA_FIRST + k))

            sp.dma_start(c_act[:, :], c_row.partition_broadcast(P)).then_inc(c_loaded, 16)
            sp.dma_start(vec[:, :], vecs).then_inc(vec_loaded, 16)
            for k in range(DC):
                for b in (k, DC + k):
                    sp.dma_start(ada_first[:, b, :], w_ada_t[b]).then_inc(chunk_loaded[k], 16)
                sp.dma_start(xa[:, k, :], x_t[:, k, :]).then_inc(chunk_loaded[k], 16)
                if 2 <= k < 4:
                    load_unit(k - 2, k - 2)
            for u in range(2, RAW):
                load_unit(u, u)
            sp.dma_start(con[:, :], consts).then_inc(con_loaded, 16)
            sp.dma_start(smw[:, :], small_w).then_inc(con_loaded, 16)
            units(RAW, 2 * FC - RAW, with_ada=True)
            b = ADA_FIRST + 2 * FC - RAW
            ada_at = [*range(RAW)] + [RAW + OUT_UNITS * c + i for c in range(4) for i in range(2)] \
                + [RAW + OUT_UNITS * c for c in range(4, 8)]
            for u in range(2 * FC, MIX0 + RAW):
                if u - 2 * FC in ada_at:
                    sp.wait_ge(ada_done, b - ADA_RING + 1)
                    load_ada(b % ADA_RING, b)
                    b += 1
                sp.wait_ge(lo_ready, u - RAW + 1)
                load_unit(u % RAW, u)
            assert b == NADA
            first = MIX0 + RAW
            sp.wait_ge(ada_done, NADA)
            sp.wait_ge(units_done, MIX0 + CREDIT)
            sp.dma_start(cs_tab[:, :, :], rope_tab).then_inc(rope_loaded, 16)
            sp.dma_start(w1, cmp_w1).then_inc(w1_loaded, 16)
            rest = UNITS - first
            units(first, rest)
            for k in range(rest // RAW * RAW, rest):
                sp.wait_ge(lo_ready, first + k - RAW + 1)
                load_unit((first + k) % RAW, first + k)
            for k in range(DC):
                sp.wait_ge(final_ready, k + 1)
                sp.dma_start(out[:, k, :], xa[:, k, :]).then_inc(stored, 16)
            sp.wait_ge(stored, 16 * DC)

        @block.gpsimd
        def _(pool):
            nc.gpsimd.memset(ones_d[:, :], 1.0 / D).then_inc(consts_ready, 1)
            nc.gpsimd.memset(ones_r[:, :], 1.0 / P).then_inc(consts_ready, 1)
            nc.gpsimd.memset(warm[:, :], 1.0).then_inc(consts_ready, 1)
            nc.gpsimd.memset(eps[:, :], EPS).then_inc(consts_ready, 1)
            nc.gpsimd.memset(vbd[:, :, :], 0.0).then_inc(consts_ready, 1)
            nc.gpsimd.memset(kcmp[:, :, :], 0.0).then_inc(consts_ready, 1)
            pool.wait_ge(con_loaded, 32)
            nc.gpsimd.tensor_copy(ident_b[:, :], ident).then_inc(consts_ready, 1)
            nc.gpsimd.tensor_copy(causal_b[:, :], causal).then_inc(consts_ready, 1)
            def centre(p):
                pool.wait_ge(mean_ready, p + 1)
                for k in range(DC):
                    nc.gpsimd.tensor_tensor(xa[:, k, :], xa[:, k, :], tmp[2][:, :], ALU.subtract).then_inc(centred, 1)

            centre(0)
            pool.wait_ge(units_done, MIX0 + CREDIT)
            nc.gpsimd.memset(hid_k[:, :, :, :], 0.0).then_inc(consts_ready, 1)
            nc.gpsimd.memset(hid_v[:, :, :, :, :], 0.0).then_inc(consts_ready, 1)
            pool.wait_ge(rope_done, N_ROPE + 2)
            for first in (2, 8):
                q = roped[:, first:first + 4, :]
                nc.gpsimd.tensor_scalar(q, q, HD ** -0.5, 0.0, ALU.mult, ALU.add).then_inc(q_scaled, 1)
            def queries_lo(m, q):
                for r, (src, hi, lo) in enumerate(query_pieces(m, q)):
                    pool.wait_ge(q_hi_done, 4 * q + 2 * m + r + 1)
                    nc.gpsimd.tensor_tensor(lo, src, hi.bitcast(F32), ALU.subtract).then_inc(q_ready, 1)
                    pool.wait_ge(q_ready, 4 * q + 2 * m + r + 1)

            pool.wait_ge(q_scaled, 2)
            for m in range(2):
                queries_lo(m, 0)
            for n, (j, src, rows, to) in enumerate(key_pieces):
                pool.wait_ge(k_hi_done, len(key_pieces))
                nc.gpsimd.tensor_tensor(k_lo[to, j, :], src, k_hi[rows, j, :].bitcast(F32), ALU.subtract)\
                    .then_inc(k_ready, 1)
                pool.wait_ge(k_ready, n + 1)
            for i, (kind, q, h) in enumerate(items):
                heads = NH if kind == "c" else batch(q)
                width = CW if kind == "c" else P * (q + 1)
                p = probs[i % 5][:, :heads * width].rearrange("p (h k) -> p h k", h=heads)
                pool.wait_ge(fac_ready, i + 1)
                nc.gpsimd.tensor_tensor(p, p, fac[:, i % 4, :heads].unsqueeze(2).to_broadcast([P, heads, width]),
                                        ALU.mult).then_inc(scaled, 1)
                if q + 1 < QB and i in (last_a[q], last_b[q]):
                    pool.wait_ge(scaled, i + 1)
                    queries_lo(int(i == last_b[q]), q + 1)
            centre(1)
            centre(2)

        @block.tensor
        def _(pe):
            def unit(u, slot, groups):
                pe.wait_ge(lo_ready, u + 1)
                at = 0
                for psum, x_hi, x_lo, chunks, first, last in groups:
                    for n, k in enumerate(chunks):
                        w = slice(at * P, (at + 1) * P)
                        one, end = first and n == 0, last and n == len(chunks) - 1
                        nc.tensor.matmul(psum, w_hi[slot][:, w], x_hi[:, k, :], start=one, stop=False)
                        nc.tensor.matmul(psum, w_hi[slot][:, w], x_lo[:, k, :], start=False, stop=False)
                        mm = nc.tensor.matmul(psum, w_lo[slot][:, w], x_hi[:, k, :], start=False, stop=end)
                        at += 1
                mm.then_inc(units_done, 1)

            def first_pair(u, psums, ready, count, x_hi=u_hi, x_lo=u_lo):
                pe.wait_ge(lo_ready, u + 2)
                for k in range(DC):
                    pe.wait_ge(ready, count + k + 1)
                    w = slice(k * P, (k + 1) * P)
                    for i, psum in enumerate(psums):
                        slot = (u + i) % SPLIT
                        nc.tensor.matmul(psum, w_hi[slot][:, w], x_hi[:, k, :], start=k == 0, stop=False)
                        nc.tensor.matmul(psum, w_hi[slot][:, w], x_lo[:, k, :], start=False, stop=False)
                        mm = nc.tensor.matmul(psum, w_lo[slot][:, w], x_hi[:, k, :], start=False, stop=k == DC - 1)
                        if k == DC - 1:
                            mm.then_inc(units_done, 1)

            def ffn(f, u0, phase):
                def hidden(j, u, jj):
                    pe.wait_ge(silu_done, j + 1)
                    unit(u, 0, [(bank[2 * jj][:, :], u_hi, u_lo, range(DC), True, True)])
                    pe.wait_ge(hmul_done, j + 1)
                    unit(u + 1, 1, [(bank[2 * jj + 1][:, :], u_hi, u_lo, range(DC), True, True)])

                pe.wait_ge(silu_done, FC * f + 1)
                pe.wait_ge(hmul_done, FC * f + 1)
                first_pair(u0, (bank[0][:, :], bank[1][:, :]), u_ready, phase * DC)
                hidden(FC * f + 1, u0 + 2, 1)
                with pe.Fori(0, FC // 2 - 1) as it:
                    for jj in range(2):
                        hidden(it * 2 + (FC * f + 2 + jj), it * 4 + (u0 + 4 + 2 * jj), jj)

                def output(it, cc, last=False):
                    pe.wait_ge(z_done, it * 2 + (2 * DC * f + cc + 1))
                    for n in range(OUT_UNITS):
                        ks = range(8 * n, min(8 * n + 8, FC))
                        u = it * (2 * OUT_UNITS) + (u0 + 2 * FC + cc * OUT_UNITS + n)
                        pe.wait_ge(h_ready, FC * f + ks[-1] + 1)
                        if last and n == OUT_UNITS - 1:
                            stats(phase, "sums")
                        unit(u, (cc * OUT_UNITS + n) % SPLIT,
                             [(bank[4 + cc][:, :], h_hi, h_lo, ks, n == 0, n == OUT_UNITS - 1)])

                with pe.Fori(0, DC // 2 - 1) as it:
                    for cc in range(2):
                        output(it, cc)
                for cc in range(2):
                    output(DC // 2 - 1, cc, last=cc == 1)
                stats(phase, "last chunk")

            def stats(p, part):
                for n in range(2):
                    if part == "sums":
                        pe.wait_ge(*((added_done, (DC - 1) * (p + 1)) if n else (sum_ready, p + 1)))
                        of = tmp[4 + n][:, :]
                    elif n == 0:
                        pe.wait_ge(z_done, CREDIT + DC * (p + 1))
                        of = xa[:, DC - 1, :]
                    else:
                        pe.wait_ge(sq_done, DC * (p + 1))
                        of = tmp[6 + (DC - 1) % 2][:, :]
                    mm = nc.tensor.matmul(bank[6 + n][:, :], ones_d[:, :], of, start=part == "sums", stop=part != "sums")
                    if part != "sums":
                        mm.then_inc(stats_done, 1)

            pe.sem_inc(units_done, CREDIT)
            pe.wait_ge(consts_ready, 1)
            ffn(0, 0, 0)
            pe.wait_ge(consts_ready, 8)

            first_pair(MIX0, (bank[0][:, :], bank[1][:, :]), u_ready, DC)
            with pe.Fori(0, N_MIX // 2 - 1) as it:
                for b in range(2):
                    pe.wait_ge(mix_evac, it * 2 + (b + 1 + CREDIT))
                    unit(it * 2 + (MIX0 + 2 + b), b, [(bank[b][:, :], u_hi, u_lo, range(DC), True, True)])
            pe.wait_ge(mix_evac, CREDIT + 2)
            nc.tensor.matmul(bank[2][:, :], ones_r[:, :], kvsq[:, :], start=True, stop=True).then_inc(ms_done, 1)
            for q in range(QB):
                tr = nc.tensor.transpose(bank[3][:, q * P:(q + 1) * P], small[:, q * P:(q + 1) * P], ident)
            tr.then_inc(small_turned, 1)
            pe.wait_ge(rope_done, 4)
            for n in range((QB - 1) * NI):
                q, h = 1 + n // NI, n % NI
                rows = slice((h % 2) * HD, (h % 2) * HD + HD)
                if n >= 2:
                    pe.wait_ge(relu_done, n - 1)
                nc.tensor.matmul(bank[4 + n % 2][:, :P * (q + 1)], roped[rows, h // 2, q * P:(q + 1) * P],
                                 ki2[rows, :P * (q + 1)], start=True, stop=True).then_inc(logits_done, 1)
            pe.wait_ge(kvn_ready, 1)
            nc.tensor.matmul(bank[6][:, :], smw[:, M_WK:M_WV], kvl[:, :], start=True, stop=True).then_inc(kv_done, 1)
            for t in range(QB):
                mm = nc.tensor.matmul(bank[7][:, t * HD:(t + 1) * HD], kvl[:, t * P:(t + 1) * P],
                                      smw[:, M_WV:M_PEK], start=True, stop=True)
            mm.then_inc(kv_done, 1)
            pe.wait_ge(mix_evac, CREDIT + N_MIX)
            pe.wait_ge(kv_std, 1)
            pe.wait_ge(small_read, 2)
            for n, src in enumerate((vs_t, vw_t)):
                for t in range(QB):
                    tr = nc.tensor.transpose(bank[2 + n][:, t * P:(t + 1) * P], src[:, t * P:(t + 1) * P], ident)
                tr.then_inc(v_turned, 1)
            pe.wait_ge(w1_loaded, 16)
            for t in range(2):
                pe.wait_ge(cmp_in_ready, 4 * (t + 1))
                for hc in range(2):
                    for l in range(CL2):
                        mm = nc.tensor.matmul(bank[t][:, hc * 64:hc * 64 + 2 * NC], w1[:, t, l, hc * P:(hc + 1) * P],
                                              cmp_in[t][:, l, :, :].rearrange("p g i -> p (g i)"),
                                              start=l == 0, stop=l == CL2 - 1)
                mm.then_inc(hid_done, 1)
            pe.wait_ge(hid_ready, 2)
            pe.wait_ge(relu_done, (QB - 1) * NI)
            for hc in range(2):
                mm = nc.tensor.matmul(bank[4][:, :2 * CW], w2k[:, hc, :],
                                      hid_k[:, hc, :, :].rearrange("p g i -> p (g i)"), start=hc == 0, stop=hc == 1)
            mm.then_inc(cmp_done, 1)
            pe.wait_ge(hid_ready, 2 + 16)
            for g in range(2):
                for hc in range(2):
                    mm = nc.tensor.matmul(bank[5][:, g * HD:(g + 1) * HD],
                                          hid_v[:, hc, g, :, :].rearrange("p r i -> p (r i)"), w2v[:, hc, :],
                                          start=hc == 0, stop=hc == 1)
            mm.then_inc(cmp_done, 1)
            pe.wait_ge(kv_read, 2)
            pe.wait_ge(v_cut, 1)
            with pe.Fori(0, N_GATE // 2) as it:
                for b in range(2):
                    pe.wait_ge(gate_done, it * 2 + (b + 1))
                    unit(it * 2 + (MIX0 + N_MIX + b), b, [(bank[6 + b][:, :], u_hi, u_lo, range(DC), True, True)])

            def scores(i):
                kind, q, h = items[i]
                keys = P * (q + 1)
                if i >= 3:
                    pe.wait_ge(exp_done, i - 2)
                ps = bank[i % 3]
                if kind == "c":
                    heads = ps[:, :NH * CW].rearrange("p (g c i) -> p c g i", g=2, c=NH // 2)
                    for c in range(NH // 2):
                        mm = nc.tensor.matmul(heads[:, c, :, :], roped[:, 8 + c, q * P:(q + 1) * P],
                                              kcmp[:, :, :].rearrange("p g i -> p (g i)"), start=True, stop=True)
                    mm.then_inc(s_done, 1)
                    return
                if h == 0 and kind != "w":
                    pe.wait_ge(q_ready, 4 * q + 2 * (1 + (kind == "s")))
                for hh in range(h, h + batch(q)):
                    to = ps[:, (hh - h) * keys:(hh - h + 1) * keys]
                    j = 0 if kind == "a" else (1 if kind == "s" else 3) + hh // 4
                    query = q_cut[int(kind != "a")][:, hh, :]
                    nc.tensor.matmul(to, query, k_hi[:, j, :keys], start=True, stop=False)
                    nc.tensor.matmul(to, query, k_lo[:, j, :keys], start=False, stop=False)
                    if kind == "a" and q:
                        pe.wait_ge(mask_ready, q)
                        mm = nc.tensor.matmul(to, ident_b[:, :], mask_a[q - 1][:, :], start=False, stop=True)
                    else:
                        mm = nc.tensor.matmul(to[:, keys - P:], ident_b[:, :], causal_b[:, :], start=False, stop=True)
                mm.then_inc(s_done, 1)

            def turns(i):
                kind, q, h = items[i]
                if i >= 2:
                    pe.wait_ge(t_read, i - 1)
                pe.wait_ge(scaled, i + 1)
                for t in range(2 if kind == "c" else batch(q) * (q + 1)):
                    tr = nc.tensor.transpose(bank[3 + i % 2][:, t * P:(t + 1) * P], probs[i % 5][:, t * P:(t + 1) * P], ident)
                tr.then_inc(t_done, 1)

            def values(u):
                r, its = pairs[u]
                kind, q, h = items[its[0]]
                pe.wait_ge(t_read, its[-1] + 1)
                first, last = u == 0 or pairs[u - 1][0] != r, its[-1] == result_end[r]
                if first and r >= 3:
                    pe.wait_ge(y_summed, r - 2)
                ps = bank[5 + r % 3]
                heads = max(2, batch(q))
                to = ps[:, h % 4 * P:(h % 4 + heads) * P].rearrange("p (h k) -> p h k", h=heads)
                if kind == "w" and last:
                    for x in range(4):
                        nc.tensor.matmul(ps[:HD, x * P:(x + 1) * P], vbd[:, h // 4, x * HD:(x + 1) * HD],
                                         cmp_t[:, h // 4 * P:(h // 4 + 1) * P], start=False, stop=False)
                for t in range(q + 1):
                    v = v_a[:, t, :, :] if kind == "a" else (v_s if kind == "s" else v_w)[:, 2 * t + h // 4, :, :]
                    v = v.rearrange("p a d -> p (a d)")
                    for n, part in enumerate((probs_t_hi, probs_t_lo)):
                        mm = nc.tensor.matmul(to, v, pair_heads(part[u % 2], q, t), start=first and t == 0 and n == 0,
                                              stop=last and t == q and n == 1)
                mm.then_inc(pv_done, 1)

            pe.wait_ge(k_ready, len(key_pieces))
            pe.wait_ge(v_cut, 3)
            pe.wait_ge(cmp_read, 10)
            pe.wait_ge(gate_done, CREDIT + N_GATE)
            for i in range(n_items + VALUE_LAG):
                if i < n_items:
                    scores(i)
                if 0 <= i - TURN_LAG < n_items:
                    turns(i - TURN_LAG)
                j = i - VALUE_LAG
                if j in pair_of and pairs[pair_of[j][0]][1][-1] == j:
                    values(pair_of[j][0])
            pe.wait_ge(y_ready, 4 * QB)
            with pe.Fori(0, DC // 2) as it:
                for b in range(2):
                    pe.wait_ge(merge_done, it * 2 + (b + 1))
                    unit(it * 2 + (BR0 + b), b,
                         [(bank[2 * b + m][:, :], y_hi[m], y_lo[m], range(HC), True, True) for m in range(2)])
            first_pair(MO0, (bank[4][:, :], bank[5][:, :]), m_ready, 0, m_hi, m_lo)
            with pe.Fori(0, DC // 2 - 1) as it:
                for b in range(2):
                    pe.wait_ge(z_done, it * 2 + (DC + b + 1 + CREDIT))
                    unit(it * 2 + (MO0 + 2 + b), b, [(bank[4 + b][:, :], m_hi, m_lo, range(DC), True, True)])
            for part in ("sums", "last chunk"):
                stats(1, part)
            ffn(1, FFN2, 2)

        @block.scalar
        def _(act):
            def copy(to, of, scale=1.0):
                return nc.scalar.activation(to, of, ACT.Copy, scale=scale)

            def hi_at(base, it, per, n):
                u = base + n
                act.wait_ge(raw_loaded[u % RAW], it * (16 * per // RAW) + 16 * (u // RAW + 1))
                act.wait_ge(units_done, it * per + (u + 1))
                copy(w_hi[u % SPLIT][:, :], raw[u % RAW][:, :]).then_inc(hi_ready, 1)

            def unit_hi(u):
                if u < UNITS:
                    act.wait_ge(raw_loaded[u % RAW], 16 * (u // RAW + 1))
                    act.wait_ge(units_done, u + 1)
                    copy(w_hi[u % SPLIT][:, :], raw[u % RAW][:, :]).then_inc(hi_ready, 1)

            def inputs(p, ready):
                def hi(k):
                    act.wait_ge(ub_ready, p * DC + k + 1)
                    copy(u_hi[:, k, :], ub[k % 4][:, :]).then_inc(uh_ready, 1)

                for k in range(DC):
                    act.wait_ge(t_ready, p * DC + k + 1)
                    if k >= 4:
                        act.wait_ge(u_ready, p * DC + k - 3)
                    scale, shift = ready(k)
                    nc.scalar.activation(ub[k % 4][:, :], xa[:, k, :], ACT.Identity, scale=scale, bias=shift)\
                        .then_inc(ub_ready, 1)
                    if k:
                        hi(k - 1)
                    if p == 0 and 3 <= k < 5:
                        unit_hi(k - 3)
                hi(DC - 1)

            def squares(z0, u0, per, residual):
                for c in range(DC):
                    late = per - 1 if c == DC - 1 else per
                    scale, shift = residual(c)
                    nc.scalar.activation(xa[:, c, :], xa[:, c, :], ACT.Identity, scale=scale, bias=shift)\
                        .then_inc(xa_ready, 1)
                    for n in range(late):
                        unit_hi(u0 + c * per + n + 2)
                    act.wait_ge(z_done, CREDIT + z0 + c + 1)
                    if c >= 2:
                        act.wait_ge(added_done, z0 // DC * (DC - 1) + c - 1)
                    nc.scalar.activation(tmp[6 + c % 2][:, :], xa[:, c, :], ACT.Square).then_inc(sq_done, 1)

            def norm(p, next_unit):
                unit_hi(next_unit)
                act.wait_ge(stats_done, 2 * p + 1)
                copy(tmp[2][:, :], bank[6][:, :]).then_inc(mean_ready, 1)
                nc.scalar.activation(tmp[3][:, :], bank[6][:, :], ACT.Square).then_inc(mean2_ready, 1)
                nc.scalar.activation(warm[:, :], warm[:, :], ACT.Sqrt)
                act.wait_ge(var_ready, p + 1)
                nc.scalar.activation(tmp[3][:, :], tmp[3][:, :], ACT.Sqrt).then_inc(std_ready, 1)

            def ffn(f, u0, residual):
                with act.Fori(0, FC // 2) as it:
                    for jj in range(2):
                        j = it * 2 + (FC * f + jj)
                        hi_at(u0, it, 4, 2 * jj + 2)
                        act.wait_ge(units_done, it * 4 + (u0 + 2 * jj + 1 + CREDIT))
                        nc.scalar.activation(tmp[jj][:, :], bank[2 * jj][:, :], ACT.Silu).then_inc(silu_done, 1)
                        hi_at(u0, it, 4, 2 * jj + 3)
                        act.wait_ge(hmul_done, j + (CREDIT + 1))
                        act.wait_ge(consts_ready, 1)
                        copy(h_hi[:, bass.ts(it * 2 + jj, 1), :], tmp[2 + jj][:, :].unsqueeze(1)).then_inc(hh_done, 1)
                squares(2 * DC * f, u0 + 2 * FC, OUT_UNITS, residual)

            act.sem_inc(silu_done, CREDIT)
            act.sem_inc(mix_evac, CREDIT)
            act.sem_inc(gate_done, CREDIT)
            act.wait_ge(c_loaded, 16)
            nc.scalar.activation(c_act[:, :], c_act[:, :], ACT.Silu).then_inc(c_ready, 1)
            inputs(0, lambda k: (aff[:, 0, k:k + 1], mod[:, k:k + 1]))
            ffn(0, 0, lambda c: (ALPHA, 0.0))
            act.wait_ge(consts_ready, 8)
            norm(0, MIX0 + 1)
            inputs(1, lambda k: (aff[:, 0, k:k + 1], aff[:, 1, k:k + 1]))

            def swap(to, of, rows):
                for r in range(0, rows, 64):
                    copy(to[r:r + 32, :], of[r + 32:r + 64, :])
                    last = copy(to[r + 32:r + 64, :], of[r:r + 32, :])
                return last

            act.wait_ge(units_done, CREDIT + MIX0)
            for b in range(2):
                unit_hi(MIX0 + b + 2)
                act.wait_ge(units_done, CREDIT + MIX0 + b + 1)
                if b == 0:
                    copy(small[:, :], bank[0][:, :])
                    swap(tmp[2], bank[0], HD).then_inc(mix_evac, 1)
                else:
                    copy(kvl[:, :], bank[1][:, :])
                    nc.scalar.activation(kvsq[:, :], bank[1][:, :], ACT.Square).then_inc(mix_evac, 1)
            with act.Fori(0, N_ROPE // 4) as it:
                for b in range(4):
                    hi_at(MIX0 + 2, it, 4, b + 2)
                    act.wait_ge(units_done, it * 4 + (MIX0 + 2 + b + 1 + CREDIT))
                    act.wait_ge(consts_ready, 1)
                    act.wait_ge(rope_done, it * 4 + (b + 1))
                    copy(tmp[b % 2][:, :], bank[b % 2][:, :])
                    swap(tmp[2 + b % 2], bank[b % 2], P).then_inc(mix_evac, 1)
            for n, to in ((14, kc), (15, vc), (16, vs_t), (17, vw_t)):
                unit_hi(MIX0 + n + 2)
                act.wait_ge(units_done, CREDIT + MIX0 + n + 1)
                if n == 14:
                    act.wait_ge(rope_done, 13)
                    copy(tmp[0][:, :], bank[0][:, :])
                    swap(tmp[2], bank[0], P).then_inc(mix_evac, 1)
                else:
                    copy(to[:, :], bank[n % 2][:, :]).then_inc(mix_evac, 1)
            act.wait_ge(ms_done, 1)
            nc.scalar.activation(kvsq[:, :], bank[2][:, :], ACT.Sqrt, bias=eps[:, :]).then_inc(kv_std, 1)
            act.wait_ge(small_turned, 1)
            turned = bank[3][:, :].rearrange("p (q f) -> p q f", q=QB)
            copy(wi[:, :, :], turned[:, :, HD:HD + NI], scale=NI ** -0.5).then_inc(small_read, 1)
            nc.scalar.activation(gb[:, :, :], turned[:, :, HD + NI:HD + NI + 3 * NH], ACT.Sigmoid).then_inc(small_read, 1)
            for n in range((QB - 1) * NI):
                q = 1 + n // NI
                act.wait_ge(logits_done, n + 1)
                if n >= 2:
                    act.wait_ge(acc_done, n - 1)
                else:
                    act.wait_ge(rope_done, N_ROPE + 3)
                nc.scalar.activation(tmp[n % 2][:, :P * (q + 1)], bank[4 + n % 2][:, :P * (q + 1)], ACT.Relu)\
                    .then_inc(relu_done, 1)
            act.wait_ge(kv_done, 2)
            copy(tmp[6][:, :], bank[6][:, :])
            swap(tmp[7], bank[6], P).then_inc(kv_read, 1)
            copy(v_a[:, :, 0, :], bank[7][:, :QB * HD].rearrange("p (t d) -> p t d", t=QB)).then_inc(kv_read, 1)
            act.wait_ge(v_turned, 2)
            for n, to in enumerate((v_s, v_w)):
                copy(to[:, :, 0, :], bank[2 + n][:, :].rearrange("p (t d) -> p t d", t=2 * QB)).then_inc(v_read, 1)
            act.wait_ge(consts_ready, 10)
            for t in range(2):
                act.wait_ge(hid_done, t + 1)
                for hc in range(2):
                    hid = bank[t][:, hc * 64:hc * 64 + 2 * NC].rearrange("p (g i) -> p g i", g=2)
                    if t == 0:
                        nc.scalar.activation(hid_k[:, hc, :, 0:NC], hid, ACT.Silu).then_inc(hid_ready, 1)
                    else:
                        for g in range(2):
                            for r in range(4):
                                nc.scalar.activation(hid_v[:, hc, g, r, 0:NC], hid[:, g, :], ACT.Silu)\
                                    .then_inc(hid_ready, 1)
            act.wait_ge(cmp_done, 1)
            for g in range(2):
                rows = slice(g * HD, (g + 1) * HD)
                copy(kcmp[rows, g, :], bank[4][rows, g * CW:(g + 1) * CW]).then_inc(cmp_read, 1)
            act.wait_ge(cmp_done, 2)
            for g in range(2):
                for r in range(4):
                    copy(vbd[r * CW:(r + 1) * CW, g, r * HD:(r + 1) * HD],
                         bank[5][r * CW:(r + 1) * CW, g * HD:(g + 1) * HD]).then_inc(cmp_read, 1)
            def queries_hi(m, q):
                for src, hi, _ in query_pieces(m, q):
                    copy(hi, src).then_inc(q_hi_done, 1)

            def keys_hi(pieces):
                for j, src, rows, to in pieces:
                    copy(k_hi[to, j, :], src).then_inc(k_hi_done, 1)

            beside = [lambda: keys_hi(key_pieces[1:5]), lambda: keys_hi(key_pieces[5:]),
                      lambda: queries_hi(0, 0), lambda: queries_hi(1, 0)]
            for b in range(4):
                unit_hi(MIX0 + N_MIX + b + 2)
                act.wait_ge(units_done, MIX0 + N_MIX + b + 1 + CREDIT)
                nc.scalar.activation(gates[:, b, :], bank[6 + b % 2][:, :], ACT.Sigmoid).then_inc(gate_done, 1)
                if b == 2:
                    act.wait_ge(q_scaled, 2)
                if b == 3:
                    act.wait_ge(rope_done, N_ROPE + 4)
                    keys_hi(key_pieces[:1])
                beside[b]()
            with act.Fori(0, N_GATE // 4 - 2) as it:
                for b in range(4):
                    hi_at(MIX0 + N_MIX + 4, it, 4, b + 2)
                    act.wait_ge(units_done, it * 4 + (MIX0 + N_MIX + b + 5 + CREDIT))
                    act.wait_ge(consts_ready, 1)
                    nc.scalar.activation(gates[:, bass.ts(it * 4 + (b + 4), 1), :], bank[6 + b % 2][:, :].unsqueeze(1),
                                         ACT.Sigmoid).then_inc(gate_done, 1)

            for b in range(N_GATE - 4, N_GATE):
                if MIX0 + N_MIX + b + 2 < BR0:
                    unit_hi(MIX0 + N_MIX + b + 2)
                act.wait_ge(units_done, MIX0 + N_MIX + b + 1 + CREDIT)
                nc.scalar.activation(gates[:, b, :], bank[6 + b % 2][:, :], ACT.Sigmoid).then_inc(gate_done, 1)

            def exps(i):
                kind, q, h = items[i]
                act.wait_ge(max_done, i + 1)
                if i >= 5:
                    act.wait_ge(t_done, i - 4)
                if kind == "c":
                    nc.scalar.activation(probs[i % 5][:, :NH * CW], tmp[6][:, :NH * CW], ACT.Exp).then_inc(exp_done, 1)
                else:
                    keys = P * (q + 1)
                    for b in range(batch(q)):
                        col = slice(b * keys, (b + 1) * keys)
                        last = nc.scalar.activation(probs[i % 5][:, col], bank[i % 3][:, col], ACT.Exp,
                                                    bias=nmax[:, i % 4, b:b + 1],
                                                    accum_out=sums[:, q, "aswc".index(kind), h + b:h + b + 1])
                    last.then_inc(exp_done, 1)
                if q + 1 < QB and i in (last_a[q], last_b[q]):
                    queries_hi(int(i == last_b[q]), q + 1)

            def turned_hi(i):
                if items[i][0] == "c":
                    return
                u, part = pair_of[i]
                q = items[i][1]
                act.wait_ge(t_done, i + 1)
                if u >= 2:
                    act.wait_ge(pv_done, u - 1)
                width = batch(q) * (q + 1) * P
                copy(probs_t_hi[u % 2][:, part * S:part * S + width], bank[3 + i % 2][:, :width]).then_inc(t_hi_done, 1)

            results = {i: r for r, i in result_end.items()}
            for i in range(n_items + CUT_LAG - 1):
                if 0 <= i - TURN_LAG < n_items:
                    turned_hi(i - TURN_LAG)
                if i < n_items:
                    exps(i)
                if i - CUT_LAG in results:
                    r = results[i - CUT_LAG]
                    act.wait_ge(y_summed, r + 1)
                    copy(y_cut(y_hi, r), y_sum[:, :2 * P].rearrange("p (c k) -> p c k", c=2)).then_inc(y_hi_done, 1)
                if i - SUM_LAG in results:
                    r = results[i - SUM_LAG]
                    act.wait_ge(pv_done, pair_of[i - SUM_LAG][0] + 1)
                    if r:
                        act.wait_ge(y_summed, r)
                    copy(y_part[:HD, :], bank[5 + r % 3][HD:, :]).then_inc(y_part_ready, 1)
            unit_hi(BR0)
            act.wait_ge(y_summed, 4 * QB)
            copy(y_cut(y_hi, 4 * QB - 1), y_sum[:, :2 * P].rearrange("p (c k) -> p c k", c=2)).then_inc(y_hi_done, 1)
            unit_hi(BR0 + 1)
            for c in range(DC):
                unit_hi(BR0 + c + 2)
                act.wait_ge(mf_ready, c + 1)
                copy(m_hi[:, c, :], tmp[c % 2][:, :]).then_inc(mh_done, 1)
            squares(DC, MO0, 1, lambda c: (aff[:, 2, c:c + 1], aff[:, 3, c:c + 1]))
            norm(1, FFN2 + 1)
            inputs(2, lambda k: (aff[:, 4, k:k + 1], aff[:, 5, k:k + 1]))
            ffn(1, FFN2, lambda c: (aff[:, 6, c:c + 1], aff[:, 7, c:c + 1]))
            norm(2, UNITS)
            for k in range(DC):
                act.wait_ge(t_ready, 3 * DC + k + 1)
                nc.scalar.activation(xa[:, k, :], xa[:, k, :], ACT.Identity, scale=vec[:, V_LN + 4 * DC + k:V_LN + 4 * DC + k + 1],
                                     bias=vec[:, V_LN + 5 * DC + k:V_LN + 5 * DC + k + 1]).then_inc(final_ready, 1)

        @block.vector
        def _(dve):
            count, turn = [0], [None]

            def mark(instruction):
                instruction.then_inc(dve_step, 1)
                count[0] += 1

            def hold():
                dve.wait_ge(dve_step, count[0] if turn[0] is None else turn[0][0] * turn[0][1] + count[0])

            def step(instruction):
                mark(instruction)
                hold()

            tt = nc.vector.tensor_tensor

            def lo_at(u0, it, per, n):
                u = u0 + n
                dve.wait_ge(hi_ready, u + 1 if it is None else it * per + (u + 1))
                tt(w_lo[u % SPLIT][:, :], raw[u % RAW][:, :], w_hi[u % SPLIT][:, :].bitcast(F32), ALU.subtract)\
                    .then_inc(lo_ready, 1)

            def unit_lo(u):
                if u < UNITS:
                    lo_at(u, None, 0, 0)

            def ada_block(slot, turn, b):
                dve.wait_ge(ada_loaded[slot], turn)
                ada_product(ada[slot][:, :], b)

            def ada_product(w, b):
                nc.vector.scalar_tensor_tensor(out=w, in0=w, scalar=1.0, in1=c_act[:, :],
                                               op0=ALU.mult, op1=ALU.mult, accum_out=mod[:, bass.ts(b, 1)])\
                    .then_inc(ada_done, 1)

            def add_bias(b0, b1):
                dve.wait_ge(ada_done, b1)
                step(tt(mod[:, b0:b1], mod[:, b0:b1], vec[:, V_BADA + b0:V_BADA + b1], ALU.add))

            def group(m):
                return mod[:, m * DC:(m + 1) * DC]

            def ln(n):
                return vec[:, V_LN + n * DC:V_LN + (n + 1) * DC]

            def prepare(at, g, b, shift, scale):
                step(nc.vector.tensor_scalar(aff[:, at + 1, :], group(scale), 1.0, None, ALU.add))
                step(tt(aff[:, at, :], aff[:, at + 1, :], ln(g), ALU.mult))
                step(tt(aff[:, at + 1, :], aff[:, at + 1, :], ln(b), ALU.mult))
                step(tt(aff[:, at + 1, :], aff[:, at + 1, :], group(shift), ALU.add))
                step(nc.vector.tensor_scalar(aff[:, at + 2, :], ln(g), ALPHA, None, ALU.mult))
                step(nc.vector.tensor_scalar(aff[:, at + 3, :], ln(b), ALPHA, None, ALU.mult))

            def input_lo(p, k):
                dve.wait_ge(uh_ready, p * DC + k + 1)
                tt(u_lo[:, k, :], ub[k % 4][:, :], u_hi[:, k, :].bitcast(F32), ALU.subtract).then_inc(u_ready, 1)

            def inputs(p):
                for k in range(DC):
                    dve.wait_ge(centred, (p - 1) * DC + k + 1)
                    tt(xa[:, k, :], xa[:, k, :], tmp[3][:, :], ALU.mult).then_inc(t_ready, 1)
                    if k >= 2:
                        input_lo(p, k - 2)
                for k in range(DC - 2, DC):
                    input_lo(p, k)

            def outputs(z0, u0, per, gate, sublayer):
                step(nc.vector.memset(tmp[4][:, :], 0.0))
                step(nc.vector.memset(tmp[5][:, :], 0.0))
                for c in range(DC):
                    late = per - 1 if c == DC - 1 else per
                    if sublayer == 0:
                        for b in ADA_WITH[c]:
                            ada_block(b % ADA_RING, 16 * ((b - ADA_FIRST) // ADA_RING + 1), b)
                    for n in range(late):
                        unit_lo(u0 + c * per + n + 2)
                    dve.wait_ge(units_done, CREDIT + u0 + (c + 1) * per)
                    dve.wait_ge(xa_ready, DC * sublayer + c + 1)
                    nc.vector.scalar_tensor_tensor(out=xa[:, c, :], in0=bank[4 + c % 2][:, :], scalar=gate(c),
                                                   in1=xa[:, c, :], op0=ALU.mult, op1=ALU.add).then_inc(z_done, 1)
                    if c == DC - 1:
                        break
                    dve.wait_ge(z_done, CREDIT + z0 + c + 1)
                    add = tt(tmp[4][:, :], tmp[4][:, :], xa[:, c, :], ALU.add)
                    if c == DC - 2:
                        add.then_inc(sum_ready, 1)
                    else:
                        step(add)
                    dve.wait_ge(sq_done, z0 + c + 1)
                    tt(tmp[5][:, :], tmp[5][:, :], tmp[6 + c % 2][:, :], ALU.add).then_inc(added_done, 1)
                    dve.wait_ge(added_done, (DC - 1) * sublayer + c + 1)

            def norm(p, next_unit):
                unit_lo(next_unit)
                dve.wait_ge(mean2_ready, p + 1)
                dve.wait_ge(stats_done, 2 * p + 2)
                step(tt(tmp[3][:, :], bank[7][:, :], tmp[3][:, :], ALU.subtract))
                nc.vector.tensor_scalar(tmp[3][:, :], tmp[3][:, :], 0.0, EPS, ALU.max, ALU.add).then_inc(var_ready, 1)
                dve.wait_ge(std_ready, p + 1)
                step(nc.vector.reciprocal(tmp[3][:, :], tmp[3][:, :]))

            def ffn(f, u0, sublayer):
                with dve.Fori(0, FC // 2) as it:
                    for jj in range(2):
                        j = it * 2 + (FC * f + jj)
                        for n in range(2):
                            lo_at(u0, it, 4, 2 * jj + n + 2)
                            if f == 0:
                                k = 2 * jj + n
                                ada_block(k % ADA_RING, it * (16 * 4 // ADA_RING) + 16 * (k // ADA_RING + 1),
                                          it * 4 + (ADA_FIRST + k))
                        dve.wait_ge(units_done, it * 4 + (u0 + 2 * jj + 2 + CREDIT))
                        dve.wait_ge(silu_done, j + (CREDIT + 1))
                        tt(tmp[2 + jj][:, :], bank[2 * jj + 1][:, :], tmp[jj][:, :], ALU.mult).then_inc(hmul_done, 1)
                        dve.wait_ge(hh_done, j + 1)
                        tt(h_lo[:, bass.ts(it * 2 + jj, 1), :], tmp[2 + jj][:, :].unsqueeze(1),
                           h_hi[:, bass.ts(it * 2 + jj, 1), :].bitcast(F32), ALU.subtract).then_inc(h_ready, 1)
                if f == 0:
                    add_bias(ADA_FIRST, ADA_LATE)
                    step(nc.vector.tensor_scalar(group(2), group(2), 0.5, None, ALU.mult))
                    prepare(0, 0, 1, 3, 4)
                m = 2 if f == 0 else 8
                outputs(2 * DC * f, u0 + 2 * FC, OUT_UNITS, lambda c: mod[:, m * DC + c:m * DC + c + 1], sublayer)

            dve.sem_inc(hmul_done, CREDIT)
            dve.sem_inc(z_done, CREDIT)
            dve.sem_inc(merge_done, CREDIT)
            dve.wait_ge(c_ready, 1)
            dve.wait_ge(vec_loaded, 16)
            for k in range(DC):
                dve.wait_ge(chunk_loaded[k], 48)
                for n in range(2):
                    ada_product(ada_first[:, n * DC + k, :], n * DC + k)
                dve.wait_ge(ada_done, 2 * k + 2)
                pair = mod[:, k:k + DC + 1:DC]
                step(tt(pair, pair, vec[:, V_BADA + k:V_BADA + k + DC + 1:DC], ALU.add))
                nc.vector.tensor_scalar(aff[:, 0, k:k + 1], mod[:, DC + k:DC + k + 1], 1.0, None, ALU.add)\
                    .then_inc(t_ready, 1)
                if k >= 2:
                    input_lo(0, k - 2)
                if 4 <= k < 6:
                    unit_lo(k - 4)
            for k in range(DC - 2, DC):
                input_lo(0, k)
            ffn(0, 0, 0)
            norm(0, MIX0 + 1)
            inputs(1)

            def rotate(to, x, turned, rows, count, part):
                tt(part[:rows, :], x[:rows, :], cos[:rows, :], ALU.mult)
                step(tt(turned[:rows, :], turned[:rows, :], sin[:rows, :], ALU.mult))
                tt(to, part[:rows, :] if count is None else part[:rows, :].unsqueeze(1),
                   turned[:rows, :] if count is None else turned[:rows, :].unsqueeze(1), ALU.add).then_inc(rope_done, 1)

            dve.wait_ge(rope_loaded, 16)
            unit_lo(MIX0 + 2)
            dve.wait_ge(mix_evac, CREDIT + 1)
            rotate(ki2[:HD, :], small, tmp[2], HD, None, tmp[4])
            dve.wait_ge(rope_done, 1)
            nc.vector.tensor_copy(ki2[HD:, :], ki2[:HD, :]).then_inc(rope_done, 1)
            unit_lo(MIX0 + 3)
            with dve.Fori(0, N_ROPE // 4) as it:
                turn[0] = (it, 4)
                for b in range(4):
                    lo_at(MIX0 + 2, it, 4, b + 2)
                    dve.wait_ge(mix_evac, it * 4 + (CREDIT + 2 + b + 1))
                    dve.wait_ge(rope_done, it * 4 + (b + 1))
                    rotate(roped[:, bass.ts(it * 4 + b, 1), :], tmp[b % 2], tmp[2 + b % 2], P, 1, tmp[4 + b % 2])
                turn[0], count[0] = None, count[0] + 4 * (N_ROPE // 4 - 1)
            unit_lo(MIX0 + 16)
            dve.wait_ge(mix_evac, CREDIT + 15)
            dve.wait_ge(rope_done, N_ROPE + 1)
            rotate(kc[:, :], tmp[0], tmp[2], P, None, tmp[4])
            for t, src in enumerate((kc, vc)):
                unit_lo(MIX0 + 17 + t)
                if t == 0:
                    dve.wait_ge(rope_done, N_ROPE + 3)
                else:
                    dve.wait_ge(mix_evac, CREDIT + 16)
                for par in range(2):
                    for g in range(2):
                        rows = slice(g * HD, (g + 1) * HD)
                        x = src[rows, :].rearrange("p (i l a) -> p a l i", i=S // 16, l=8, a=2)
                        for half in range(2):
                            dst = cmp_in[t][par * HD:(par + 1) * HD, half * 8:(half + 1) * 8, g, :]
                            pe_v = pe_tab[t][rows, par, half * 8:(half + 1) * 8].unsqueeze(2).to_broadcast([HD, 8, NC])
                            add = tt(dst, x[:, par, :, half:half + NC], pe_v, ALU.add)
                        add.then_inc(cmp_in_ready, 1)
            unit_lo(MIX0 + 19)
            dve.wait_ge(kv_std, 1)
            step(nc.vector.reciprocal(kvsq[:, :], kvsq[:, :]))
            nc.vector.scalar_tensor_tensor(out=kvl[:, :], in0=kvl[:, :], scalar=vec[:, V_KVG:V_KVG + 1], in1=kvsq[:, :],
                                           op0=ALU.mult, op1=ALU.mult).then_inc(kvn_ready, 1)
            dve.wait_ge(small_read, 1)
            for n in range((QB - 1) * NI):
                q, h = 1 + n // NI, n % NI
                a, r = acc[q - 1][:, :], tmp[n % 2][:, :P * (q + 1)]
                dve.wait_ge(relu_done, n + 1)
                if h == 0:
                    nc.vector.tensor_scalar(a, r, wi[:, q, h:h + 1], None, ALU.mult).then_inc(acc_done, 1)
                else:
                    dve.wait_ge(acc_done, n)
                    nc.vector.scalar_tensor_tensor(out=a, in0=r, scalar=wi[:, q, h:h + 1], in1=a,
                                                   op0=ALU.mult, op1=ALU.add).then_inc(acc_done, 1)
            dve.wait_ge(acc_done, (QB - 1) * NI)
            for q in range(1, QB):
                last = acc[q - 1][:, q * P:]
                step(tt(last, last, causal, ALU.add))
            dve.wait_ge(kv_read, 1)
            rotate(k_a[:, :], tmp[6], tmp[7], P, None, tmp[5])
            dve.wait_ge(kv_read, 2)
            tt(v_a[:, :, 1, :], bank[7][:, :QB * HD].rearrange("p (t d) -> p t d", t=QB), v_a[:, :, 0, :].bitcast(F32),
               ALU.subtract).then_inc(v_cut, 1)
            for n, v in enumerate((v_s, v_w)):
                dve.wait_ge(v_read, n + 1)
                tt(v[:, :, 1, :], bank[2 + n][:, :].rearrange("p (t d) -> p t d", t=2 * QB), v[:, :, 0, :].bitcast(F32),
                   ALU.subtract).then_inc(v_cut, 1)
            def top_round(u, done, with_unit=True):
                def lo(x):
                    if with_unit:
                        cols = slice(x * UW // 2, (x + 1) * UW // 2)
                        return tt(w_lo[u % SPLIT][:, cols], raw[u % RAW][:, cols], w_hi[u % SPLIT][:, cols].bitcast(F32),
                                  ALU.subtract)

                hold()
                if with_unit:
                    dve.wait_ge(hi_ready, done)
                lo(0)
                for q in range(3):
                    last = nc.vector.max(max8[:, q, :], acc[q][:, :])
                mark(last)
                hold()
                if with_unit:
                    lo(1).then_inc(lo_ready, 1)
                for q in range(3):
                    last = nc.vector.match_replace(acc[q][:, :], max8[:, q, :], acc[q][:, :], TAKEN)
                mark(last)

            with dve.Fori(0, N_GATE // 4 - 1) as it:
                turn[0] = (it, 2 * 4)
                for b in range(4):
                    u = MIX0 + N_MIX + b + 2
                    top_round(u, it * 4 + (u + 1))
                turn[0], count[0] = None, count[0] + 2 * 4 * (N_GATE // 4 - 2)
            for u in range(BR0 - 2, BR0 + 2):
                top_round(u, u + 1, with_unit=u < BR0)
            hold()
            for q in range(3):
                nc.vector.tensor_scalar(mask_a[q][:, :], acc[q][:, :], TAKEN / 2, NEG, ALU.is_gt, ALU.mult)\
                    .then_inc(mask_ready, 1)

            def maxima(i):
                kind, q, h = items[i]
                dve.wait_ge(s_done, i + 1)
                ps = bank[i % 3]
                if kind != "c":
                    if i >= 4:
                        dve.wait_ge(exp_done, i - 3)
                    heads = ps[:, :batch(q) * P * (q + 1)].rearrange("p (b k) -> p b k", b=batch(q))
                    nc.vector.tensor_reduce(nmax[:, i % 4, :batch(q)], heads, AX, ALU.max, negate=True)\
                        .then_inc(max_done, 1)
                    return
                mask = cmp_mask[:, q, :].unsqueeze(1).to_broadcast([P, NH, CW])
                step(tt(cmp_s[:, :, :], ps[:, :NH * CW].rearrange("p (h c) -> p h c", h=NH), mask, ALU.add))
                step(nc.vector.tensor_reduce(nmax_c[:, :], cmp_s[:, :, :], AX, ALU.max, negate=True))
                tt(cmp_s[:, :, :], cmp_s[:, :, :], nmax_c[:, :].unsqueeze(2).to_broadcast([P, NH, CW]), ALU.add)\
                    .then_inc(max_done, 1)

            def factors(i):
                kind, q, h = items[i]
                heads = NH if kind == "c" else batch(q)
                total = sums[:, q, "aswc".index(kind), h:h + heads]
                f = fac[:, i % 4, :heads]
                dve.wait_ge(exp_done, i + 1)
                if i >= 4:
                    dve.wait_ge(scaled, i - 3)
                if kind == "c":
                    p = probs[i % 5][:, :NH * CW].rearrange("p (h c) -> p h c", h=NH)
                    step(nc.vector.tensor_reduce(total, p, AX, ALU.add))
                if kind == "a":
                    nc.vector.reciprocal(f, total).then_inc(fac_ready, 1)
                    return
                step(nc.vector.reciprocal(f, total))
                at = NH * "csw".index(kind) + h
                gate = tt(f, f, gb[:, q, at:at + heads], ALU.mult)
                if kind == "c":
                    step(gate)
                    gate = nc.vector.tensor_scalar(f, f, con[:, C_VALID + q:C_VALID + q + 1], None, ALU.mult)
                gate.then_inc(fac_ready, 1)

            def turned_lo(i):
                kind, q, h = items[i]
                ps = bank[3 + i % 2]
                if kind == "c":
                    dve.wait_ge(t_done, i + 1)
                    nc.vector.tensor_copy(cmp_t, ps[:, :2 * P]).then_inc(t_read, 1)
                    return
                u, part = pair_of[i]
                col = slice(part * S, part * S + batch(q) * (q + 1) * P)
                dve.wait_ge(t_hi_done, cut_no[i] + 1)
                tt(probs_t_lo[u % 2][:, col], ps[:, :col.stop - col.start], probs_t_hi[u % 2][:, col].bitcast(F32),
                   ALU.subtract).then_inc(t_read, 1)

            def sum_up(r):
                dve.wait_ge(y_part_ready, r + 1)
                if r:
                    dve.wait_ge(y_ready, r)
                for odd in range(2):
                    rows = slice(odd * HD, (odd + 1) * HD)
                    a, b = [x[:HD, :].rearrange("p (c o k) -> p c o k", c=2, o=2)[:, :, odd, :]
                            for x in (bank[5 + r % 3], y_part)]
                    add = tt(y_sum[rows, :2 * P].rearrange("p (c k) -> p c k", c=2), a, b, ALU.add)
                add.then_inc(y_summed, 1)

            def cut(r):
                dve.wait_ge(y_hi_done, r + 1)
                tt(y_cut(y_lo, r), y_sum[:, :2 * P].rearrange("p (c k) -> p c k", c=2), y_cut(y_hi, r).bitcast(F32),
                   ALU.subtract).then_inc(y_ready, 1)

            results = {i: r for r, i in result_end.items()}
            for i in range(n_items + CUT_LAG - 1):
                if i < n_items:
                    maxima(i)
                if 0 <= i - 1 < n_items:
                    factors(i - 1)
                if 0 <= i - TURN_LAG < n_items:
                    turned_lo(i - TURN_LAG)
                if i - CUT_LAG in results:
                    cut(results[i - CUT_LAG])
                if i - SUM_LAG in results:
                    sum_up(results[i - SUM_LAG])
            unit_lo(BR0)
            cut(4 * QB - 1)
            unit_lo(BR0 + 1)

            for c in range(DC):
                unit_lo(BR0 + c + 2)
                b = c % 2
                dve.wait_ge(units_done, CREDIT + BR0 + c + 1)
                tt(tmp[b][:, :], bank[2 * b][:, :], gates[:, c, :], ALU.mult)
                tt(tmp[2 + b][:, :], bank[2 * b + 1][:, :], gates[:, DC + c, :], ALU.mult).then_inc(merge_done, 1)
                dve.wait_ge(merge_done, CREDIT + c + 1)
                tt(tmp[b][:, :], tmp[b][:, :], tmp[2 + b][:, :], ALU.add).then_inc(mf_ready, 1)
                dve.wait_ge(mh_done, c + 1)
                tt(m_lo[:, c, :], tmp[b][:, :], m_hi[:, c, :].bitcast(F32), ALU.subtract).then_inc(m_ready, 1)
            add_bias(ADA_LATE, NADA)
            step(nc.vector.tensor_scalar(group(8), group(8), 0.5, None, ALU.mult))
            prepare(4, 2, 3, 6, 7)
            outputs(DC, MO0, 1, lambda c: mod[:, 5 * DC + c:5 * DC + c + 1], 1)
            norm(1, FFN2 + 1)
            inputs(2)
            ffn(1, FFN2, 2)
            norm(2, UNITS)
            for k in range(DC):
                dve.wait_ge(centred, 2 * DC + k + 1)
                tt(xa[:, k, :], xa[:, k, :], tmp[3][:, :], ALU.mult).then_inc(t_ready, 1)


def _layout(inputs, np):
    f = {k: np.asarray(v) for k, v in inputs.items()}

    def unit_blocks(w):
        k, n = w.shape
        return w.reshape(k // P, P, n // P, P).transpose(2, 1, 0, 3).reshape(n // P, P, k)

    def ffn(w_in, w_out):
        a, b = unit_blocks(w_in[:, :FF]), unit_blocks(w_in[:, FF:])
        first = np.stack([a, b], 1).reshape(2 * FC, P, UW)
        o = unit_blocks(w_out)
        o = np.concatenate([o, np.zeros((DC, P, OUT_UNITS * UW - FF), o.dtype)], 2)
        return [first, o.reshape(DC, P, OUT_UNITS, UW).transpose(0, 2, 1, 3).reshape(OUT_UNITS * DC, P, UW)]

    w = f["w_mix_in"][0]
    cut = np.cumsum([NH * HD, P, NI * HD, HD, NI, NH * HD, 6 * P, 3 * NH, 2 * D])
    qa, kv, qi, ki, wi, qb, kv6, gb, gm = np.split(w, cut[:-1], axis=1)
    small = np.concatenate([ki, wi, gb, np.zeros((D, P - HD - NI - 3 * NH), w.dtype)], 1)
    pairs = np.arange(NH).reshape(2, NH // 2).T.ravel()
    qb = qb.reshape(D, NH, HD)[:, pairs, :].reshape(D, NH * HD)
    kc, vc, ks, vs, kw, vw = np.split(kv6, 6, axis=1)
    mix = unit_blocks(np.concatenate([small, kv, qi, qa, ks, kw, qb, kc, vc, vs, vw, gm], 1))
    br = np.concatenate([unit_blocks(f["w_br_a"][0]), unit_blocks(f["w_br_b"][0])], 2)
    stream = np.concatenate(
        ffn(f["ffn1_w_in"][0], f["ffn1_w_out"][0]) + [mix, br, unit_blocks(f["w_mix_out"][0])]
        + ffn(f["ffn2_w_in"][0], f["ffn2_w_out"][0]), 0)

    def col(v):
        return v.reshape(-1, P).T

    vecs = np.concatenate([col(f[k][0]) for k in ("b_ada", "ln1_g", "ln1_b", "ln2_g", "ln2_b", "ln3_g", "ln3_b", "kv_norm_g")], 1)
    up = f["w_kv_up"][0]
    w2k = f["cmp_w2_k"][0].reshape(2, P, HD).transpose(1, 0, 2)
    w2v = f["cmp_w2_v"][0].reshape(2, P, HD).transpose(1, 0, 2)

    def pe(v):
        v = v.reshape(CL2, 2, HD).transpose(2, 1, 0).reshape(HD, 2 * CL2)
        return np.concatenate([v, v], 0)

    small_w = np.concatenate([
        np.concatenate([w2k, w2k], 2).reshape(P, 4 * HD), w2v.reshape(P, 2 * HD),
        up[:, :HD], up[:, :HD], up[:, HD:], pe(f["cmp_pe_k"][0]), pe(f["cmp_pe_v"][0])], 1)
    cmp_w1 = np.stack([f[k][0].reshape(CL2, P, 2 * P).transpose(1, 0, 2) for k in ("cmp_w1_k", "cmp_w1_v")], 1)

    row = np.arange(P)
    consts = np.zeros((P, C_N), np.float32)
    consts[:, C_ID:C_ID + P] = np.eye(P)
    consts[:, C_CAUSAL:C_CAUSAL + P] = np.where(row[None, :] <= row[:, None], 0.0, NEG)
    token = row[:, None, None] + P * np.arange(QB)[None, :, None]
    block = np.arange(CW)[None, None, :]
    seen = (block < NC) & (16 * block + 31 <= token)
    consts[:, C_CMP:C_VALID] = np.where(seen, 0.0, NEG).reshape(P, QB * CW)
    consts[:, C_VALID:] = seen.any(2)
    half = HD // 2
    inv = (10000.0 ** (-np.arange(half) / half)).astype(np.float32)
    ang = (np.arange(S, dtype=np.float32)[None, :] * inv[:, None]).astype(np.float32)
    cos, sin = np.cos(ang).astype(np.float32), np.sin(ang).astype(np.float32)
    rope = np.stack([np.concatenate([cos] * 4, 0), np.concatenate([-sin, sin, -sin, sin], 0)], 1)

    c = np.ascontiguousarray
    return {
        "x_t": c(f["x"][0].T.reshape(DC, P, S).transpose(1, 0, 2)),
        "c_row": c(f["c"].reshape(1, D)),
        "w_ada_t": c(f["w_ada"][0].T.reshape(NADA, P, D)),
        "vecs": c(vecs),
        "consts": consts,
        "rope_tab": c(rope),
        "small_w": c(small_w),
        "cmp_w1": c(cmp_w1.reshape(P, 2, CL2, 2 * P)),
        "stream": c(stream),
    }


def kernel(**inputs):
    import numpy as np
    import concourse.bacc as bacc
    from concourse.bass_utils import run_bass_kernel_spmd

    arrays = _layout(inputs, np)
    nc = bacc.Bacc("TRN2", target_bir_lowering=False, num_devices=1)
    args = [nc.dram_tensor(k, a.shape, mybir.dt.from_np(a.dtype), kind="ExternalInput").ap()
            for k, a in arrays.items()]
    out = nc.dram_tensor("out", (P, DC, S), F32, kind="ExternalOutput").ap()
    decoder_layer(nc, *args, out)
    got = run_bass_kernel_spmd(nc, [arrays], core_ids=[0]).results[0]["out"]
    return np.ascontiguousarray(got.transpose(1, 0, 2).reshape(D, S).T).reshape(1, S, D)
```

```python
from contextlib import ExitStack

import concourse.bass as bass
from concourse import mybir

F32 = mybir.dt.float32
F32R = mybir.dt.float32r
BF16 = mybir.dt.bfloat16
ACT = mybir.ActivationFunctionType
ALU = mybir.AluOpType
AX = mybir.AxisListType.X

P = 128
S = 512
D = 1024
DC = D // P
FF = 2816
FC = FF // P
HD = 64
QB = S // P
NH = 8
HC = NH * HD // P
NI = 4
TOPK = S // 4
ALPHA = 2.0 ** 0.25
EPS = 1e-5
NEG = -1e30
TAKEN = -3e38
NMOD = 9
NADA = NMOD * DC
NC = 31
CW = 32
CL2 = 16

UW = DC * P
OUT_UNITS = 3
FFN_UNITS = 2 * FC + OUT_UNITS * DC
MIX0 = FFN_UNITS
N_ROPE = 12
N_MIX = 18
N_GATE = 2 * DC
G0 = MIX0 + N_MIX
BR0 = G0 + N_GATE
MO0 = BR0 + DC
FFN2 = MO0 + DC
UNITS = FFN2 + FFN_UNITS
RAW = 4
SPLIT = 2
FIRST_PAIRS = [0, MIX0, BR0, MO0, FFN2]
BUSY = 36
CREDIT = 2
ADA_FIRST = 2 * DC
ADA_LATE = ADA_FIRST + 2 * FC
ADA_RING = 2
TURN_LAG, VALUE_LAG, SUM_LAG, CUT_LAG = 6, 8, 10, 11
PROBS, FACTORS = 8, 8
ADA_WITH = [[ADA_LATE + 2 * c, ADA_LATE + 2 * c + 1] if c < 4 else [ADA_LATE + 4 + c] for c in range(DC)]

V_BADA, V_LN, V_KVG = 0, NADA, NADA + 6 * DC
V_N = V_KVG + 1
C_ID, C_CAUSAL, C_CMP, C_VALID = 0, P, 2 * P, 2 * P + QB * CW
C_N = C_VALID + QB
M_W2K, M_W2V, M_WK, M_WV, M_PEK, M_PEV = 0, 256, 384, 512, 576, 608
M_N = 640


def batch(q):
    return max(1, S // (P * (q + 1)))


def schedule():
    items = []
    for q in range(QB):
        items += [("a", q, h) for h in range(0, NH, batch(q))]
        items.append(("c", q, 0))
        for g in range(2):
            items += [(kind, q, h) for kind in "sw" for h in range(4 * g, 4 * g + 4, batch(q))]
    return items


def decoder_layer(nc, x_t, c_row, w_ada_t, vecs, consts, rope_tab, small_w, cmp_w1, stream, out):
    items = schedule()
    n_items = len(items)
    pairs = []
    for i, (kind, q, h) in enumerate(items):
        if kind == "c":
            continue
        if batch(q) == 1 and h % 2:
            pairs[-1][1].append(i)
        else:
            pairs.append((4 * q + 2 * (kind != "a") + h // 4, [i]))
    pair_of = {i: (u, part) for u, (_, its) in enumerate(pairs) for part, i in enumerate(its)}
    cut_no = {i: n for n, i in enumerate(pair_of)}
    result_end = {r: its[-1] for r, its in pairs}
    last_a = {q: max(i for i, it in enumerate(items) if it[:2] == ("a", q)) for q in range(QB)}
    last_b = {q: max(i for i, it in enumerate(items) if it[:2] == ("w", q)) for q in range(QB)}

    ctx = ExitStack()
    with ctx:
        def sb(name, shape, dt=F32, stack=ctx):
            return stack.enter_context(nc.sbuf_tensor(name, shape, dt))

        def sem(name):
            return ctx.enter_context(nc.semaphore(name))

        xa = sb("xa", [P, DC, S])
        raw = [sb(f"raw{i}", [P, UW]) for i in range(RAW)]
        w_hi = [sb(f"w_hi{i}", [P, UW], F32R) for i in range(SPLIT)]
        w_lo = [sb(f"w_lo{i}", [P, UW], F32R) for i in range(SPLIT)]
        tmp = [sb(f"tmp{i}", [P, S]) for i in range(8)]
        vec = sb("vec", [P, V_N])
        con = sb("con", [P, C_N])
        smw = sb("smw", [P, M_N])
        mod = sb("mod", [P, NADA])
        aff = sb("aff", [P, 12, DC])
        ones_d = sb("ones_d", [P, P])
        ones_r = sb("ones_r", [P, P])
        eps = sb("eps", [P, 1])
        warm = sb("warm", [P, 1])
        ident_b = sb("ident_b", [P, P], BF16)
        causal_b = sb("causal_b", [P, P], BF16)
        wi = sb("wi", [P, QB, NI])
        gb = sb("gb", [P, QB, 3 * NH])
        kcmp = sb("kcmp", [P, 2, CW])
        vbd = sb("vbd", [P, 2, 4 * HD])
        sums = sb("sums", [P, QB, 4, NH])
        fac = sb("fac", [P, FACTORS, NH])
        nmax = sb("nmax", [P, 4, 4])
        nmax_c = sb("nmax_c", [P, NH])
        ub = [tmp[0], tmp[1], tmp[6], tmp[7]]
        pause = sb("pause", [P, 1])
        max8 = sb("max8", [P, 3, 8])

        with ExitStack() as use_u:
            u_hi = sb("u_hi", [P, DC, S], F32R, use_u)
            u_lo = sb("u_lo", [P, DC, S], F32R, use_u)
        y_hi = [sb(f"y_hi{m}", [P, HC, S], F32R) for m in range(2)]
        y_lo = [sb(f"y_lo{m}", [P, HC, S], F32R) for m in range(2)]
        k_a = tmp[4]
        y_part, y_sum = tmp[3], tmp[4]
        probs_t_hi, probs_t_lo = w_hi, w_lo
        cmp_s = tmp[6][:, :NH * CW].rearrange("p (h c) -> p h c", h=NH)
        cmp_t = tmp[6][:, NH * CW:]

        with ExitStack() as use_start:
            ada_first = sb("ada_first", [P, ADA_FIRST, D], F32, use_start)
        with ExitStack() as use_ffn:
            h_hi = sb("h_hi", [P, FC, S], F32R, use_ffn)
            h_lo = sb("h_lo", [P, FC, S], F32R, use_ffn)
            ada = [sb(f"ada{i}", [P, D], F32, use_ffn) for i in range(ADA_RING)]
            c_act = sb("c_act", [P, D], F32, use_ffn)
        with ExitStack() as mixers:
            with ExitStack() as use_rope:
                roped = sb("roped", [P, N_ROPE, S], F32, use_rope)
            v_s = sb("v_s", [P, QB * 2, 2, HD], F32R, mixers)
            sb("rest_of_roped", [P, (N_ROPE - 2) * S], F32, mixers)
            v_a = sb("v_a", [P, QB, 2, HD], F32R, mixers)
            v_w = sb("v_w", [P, QB * 2, 2, HD], F32R, mixers)
            mask_a = [sb(f"mask_a{q}", [P, P * (q + 1)], BF16, mixers) for q in range(1, QB)]
        m_hi = sb("m_hi", [P, DC, S], F32R)
        m_lo = sb("m_lo", [P, DC, S], F32R)
        sb("rest_of_masks", [P, 64])
        gates = sb("gates", [P, N_GATE, S])
        w1 = gates[:, :, :].rearrange("p a b -> p (a b)").rearrange("p (t l n) -> p t l n", t=2, l=CL2)
        with ExitStack() as early:
            ki2 = sb("ki2", [P, S], F32, early)
            small = sb("small", [P, S], F32, early)
            kvl = sb("kvl", [P, S], F32, early)
            kvsq = sb("kvsq", [P, S], F32, early)
            kc = sb("kc", [P, S], F32, early)
            vc = sb("vc", [P, S], F32, early)
            vs_t = sb("vs_t", [P, S], F32, early)
            vw_t = sb("vw_t", [P, S], F32, early)
            cmp_in = [sb(f"cmp_in{t}", [P, CL2, 2, NC], F32, early) for t in range(2)]
            hid_k = sb("hid_k", [P, 2, 2, CW], F32, early)
            hid_v = sb("hid_v", [P, 2, 2, 4, CW], F32, early)
            cs_tab = sb("cs_tab", [P, 2, S], F32, early)
            acc = [sb(f"acc{q}", [P, P * (q + 1)], F32, early) for q in range(1, QB)]
        k_hi = sb("k_hi", [P, 5, S], F32R)
        k_lo = sb("k_lo", [P, 5, S], F32R)
        def places(tile):
            return [tile[:, 2 * i:2 * i + 2, :].rearrange("p a s -> p (a s)") for i in range(SPLIT)]

        pair_hi, pair_lo = places(k_hi), places(k_lo)
        pair_mix_hi, pair_mix_lo = places(h_hi[:, :4, :]), places(h_hi[:, 4:8, :])
        q_cut = [sb(f"q_cut{m}", [P, NH, P], F32R) for m in range(2)]
        probs = [tmp[i] for i in (0, 1, 2, 5, 7)] + [sb(f"probs{i}", [P, S]) for i in range(PROBS - 5)]

        bank = [ctx.enter_context(nc.psum_tensor(f"bank{i}", [P, S], F32)) for i in range(8)]

        ident = con[:, C_ID:C_ID + P]
        causal = con[:, C_CAUSAL:C_CAUSAL + P]
        cmp_mask = con[:, C_CMP:C_VALID].rearrange("p (q c) -> p q c", q=QB)
        cos, sin = cs_tab[:, 0, :], cs_tab[:, 1, :]
        w2k = smw[:, M_W2K:M_W2V].rearrange("p (a b) -> p a b", a=2)
        w2v = smw[:, M_W2V:M_WK].rearrange("p (a b) -> p a b", a=2)
        pe_tab = [smw[:, o:o + 32].rearrange("p (a l) -> p a l", a=2) for o in (M_PEK, M_PEV)]

        c_loaded, vec_loaded, con_loaded = sem("c_loaded"), sem("vec_loaded"), sem("con_loaded")
        rope_loaded, w1_loaded = sem("rope_loaded"), sem("w1_loaded")
        raw_loaded = [sem(f"raw_loaded{i}") for i in range(RAW)]
        chunk_loaded = [sem(f"chunk_loaded{k}") for k in range(DC)]
        ada_loaded = [sem(f"ada_loaded{i}") for i in range(ADA_RING)]
        hi_ready, lo_ready = sem("hi_ready"), sem("lo_ready")
        units_done = sem("units_done")
        consts_ready = sem("consts_ready")
        c_ready, ada_done = sem("c_ready"), sem("ada_done")
        silu_done, hmul_done, hh_done, h_ready = sem("silu_done"), sem("hmul_done"), sem("hh_done"), sem("h_ready")
        z_done, sq_done, added_done = sem("z_done"), sem("sq_done"), sem("added_done")
        centred, t_ready = sem("centred"), sem("t_ready")
        sum_ready, stats_done = sem("sum_ready"), sem("stats_done")
        mean_ready, mean2_ready = sem("mean_ready"), sem("mean2_ready")
        var_ready, std_ready = sem("var_ready"), sem("std_ready")
        ub_ready, uh_ready, u_ready, xa_ready = sem("ub_ready"), sem("uh_ready"), sem("u_ready"), sem("xa_ready")
        mix_evac, rope_done = sem("mix_evac"), sem("rope_done")
        ms_done, kv_std, kvn_ready = sem("ms_done"), sem("kv_std"), sem("kvn_ready")
        small_turned, small_read = sem("small_turned"), sem("small_read")
        logits_done, relu_done, acc_done = sem("logits_done"), sem("relu_done"), sem("acc_done")
        kv_done, kv_read = sem("kv_done"), sem("kv_read")
        v_turned, v_read = sem("v_turned"), sem("v_read")
        cmp_in_ready, hid_done, hid_ready = sem("cmp_in_ready"), sem("hid_done"), sem("hid_ready")
        cmp_done, cmp_read = sem("cmp_done"), sem("cmp_read")
        gate_done, q_scaled, mask_ready = sem("gate_done"), sem("q_scaled"), sem("mask_ready")
        s_done, max_done, exp_done = sem("s_done"), sem("max_done"), sem("exp_done")
        fac_ready, scaled = sem("fac_ready"), sem("scaled")
        t_done, t_hi_done, t_read, pv_done = sem("t_done"), sem("t_hi_done"), sem("t_read"), sem("pv_done")
        y_part_ready, y_summed = sem("y_part_ready"), sem("y_summed")
        y_hi_done, y_ready = sem("y_hi_done"), sem("y_ready")
        k_hi_done, k_ready = sem("k_hi_done"), sem("k_ready")
        v_cut, q_hi_done, q_ready = sem("v_cut"), sem("q_hi_done"), sem("q_ready")
        merge_done, mf_ready, mh_done, m_ready = sem("merge_done"), sem("mf_ready"), sem("mh_done"), sem("m_ready")
        final_ready, stored = sem("final_ready"), sem("stored")
        dve_step = sem("dve_step")

        key_pieces = [(0, k_a[:, :], slice(0, P), slice(0, P))]
        for g in range(2):
            for at in (0, HD):
                for n in range(2):
                    rows = slice(g * HD, (g + 1) * HD)
                    key_pieces.append((1 + 2 * n + g, roped[rows, 6 + n, :], rows, slice(at, at + HD)))

        def parts(u):
            hi, lo = w_hi, w_lo
            if u // 2 * 2 == MIX0:
                hi, lo = pair_mix_hi, pair_mix_lo
            elif u // 2 * 2 in FIRST_PAIRS:
                hi, lo = pair_hi, pair_lo
            return hi[u % SPLIT][:, :], lo[u % SPLIT][:, :]

        def parts_free(u):
            first = u // 2 * 2
            if first == MIX0:
                return MIX0 - OUT_UNITS + 1
            if first in FIRST_PAIRS:
                n = FIRST_PAIRS.index(first)
                return FIRST_PAIRS[n - 1] + SPLIT if n else 0
            return max(0, u - 3 if first - 2 in FIRST_PAIRS else u - 1)

        def ahead(u0, per, c):
            if per == 1 and c < 2:
                return range(0)
            return range(u0 + c * per + 2, u0 + (c + 1) * per + 2 - (c == DC - 1))

        def branches_ahead(c):
            first = [2, 4, 4, 5, 6, 7, 9, 10, 10]
            return range(BR0 + first[c], BR0 + first[c + 1])

        def query_pieces(m, q):
            pieces = []
            for r in range(2):
                rows = slice(r * HD, (r + 1) * HD)
                src = roped[rows, (2, 8)[m]:(2, 8)[m] + 4, q * P:(q + 1) * P]
                heads = slice(r, NH, 2) if m == 0 else slice(r * 4, r * 4 + 4)
                other = slice((1 - r) * HD, (2 - r) * HD)
                pieces.append((src, q_cut[m][rows, heads, :], q_cut[m][other, heads, :]))
            return pieces

        def pair_heads(tile, q, t):
            heads = max(2, batch(q))
            apart = S if batch(q) == 1 else P * (q + 1)
            return tile[:, :heads * apart].rearrange("p (h k) -> p h k", h=heads)[:, :, t * P:(t + 1) * P]

        def branch_gate(kind, q, h, heads):
            at = NH * "csw".index(kind) + h
            return gb[:, q, at:at + heads]

        def y_cut(tile, r):
            q, x = r // 4, r % 2
            return tile[r % 4 // 2][:, 2 * x:2 * x + 2, q * P:(q + 1) * P]

        block = ctx.enter_context(nc.Block())

        @block.sync
        def _(sp):
            def load_unit(slot, u):
                src = stream[bass.ts(u, 1), :, :].rearrange("a p n -> (a p) n")
                sp.dma_start(raw[slot][:, :], src).then_inc(raw_loaded[slot], 16)

            def load_ada(slot, b):
                src = w_ada_t[bass.ts(b, 1), :, :].rearrange("a p n -> (a p) n")
                sp.dma_start(ada[slot][:, :], src).then_inc(ada_loaded[slot], 16)

            def units(first, count, with_ada=False):
                with sp.Fori(0, count // RAW) as it:
                    for k in range(RAW):
                        sp.wait_ge(lo_ready, it * RAW + (first + k - RAW + 1))
                        load_unit((first + k) % RAW, it * RAW + (first + k))
                        if with_ada:
                            sp.wait_ge(ada_done, it * RAW + (ADA_FIRST + k - ADA_RING + 1))
                            load_ada(k % ADA_RING, it * RAW + (ADA_FIRST + k))

            sp.dma_start(c_act[:, :], c_row.partition_broadcast(P)).then_inc(c_loaded, 16)
            sp.dma_start(vec[:, :], vecs).then_inc(vec_loaded, 16)
            for k in range(DC):
                for b in (k, DC + k):
                    sp.dma_start(ada_first[:, b, :], w_ada_t[b]).then_inc(chunk_loaded[k], 16)
                sp.dma_start(xa[:, k, :], x_t[:, k, :]).then_inc(chunk_loaded[k], 16)
                if 2 <= k < 4:
                    load_unit(k - 2, k - 2)
            for u in range(2, RAW):
                load_unit(u, u)
            sp.dma_start(con[:, :], consts).then_inc(con_loaded, 16)
            sp.dma_start(smw[:, :], small_w).then_inc(con_loaded, 16)
            units(RAW, 2 * FC - RAW, with_ada=True)
            b = ADA_FIRST + 2 * FC - RAW
            ada_at = [*range(RAW)] + [RAW + OUT_UNITS * c + i for c in range(4) for i in range(2)] \
                + [RAW + OUT_UNITS * c for c in range(4, 8)]
            for u in range(2 * FC, MIX0 + RAW):
                if u - 2 * FC in ada_at:
                    sp.wait_ge(ada_done, b - ADA_RING + 1)
                    load_ada(b % ADA_RING, b)
                    b += 1
                sp.wait_ge(lo_ready, u - RAW + 1)
                load_unit(u % RAW, u)
            assert b == NADA
            first = MIX0 + RAW
            sp.wait_ge(ada_done, NADA)
            sp.wait_ge(units_done, MIX0 + CREDIT)
            sp.dma_start(cs_tab[:, :, :], rope_tab).then_inc(rope_loaded, 16)
            sp.dma_start(w1, cmp_w1).then_inc(w1_loaded, 16)
            rest = UNITS - first
            units(first, rest)
            for k in range(rest // RAW * RAW, rest):
                sp.wait_ge(lo_ready, first + k - RAW + 1)
                load_unit((first + k) % RAW, first + k)
            for k in range(DC):
                sp.wait_ge(final_ready, k + 1)
                sp.dma_start(out[:, k, :], xa[:, k, :]).then_inc(stored, 16)
            sp.wait_ge(stored, 16 * DC)

        @block.gpsimd
        def _(pool):
            nc.gpsimd.memset(ones_d[:, :], 1.0 / D).then_inc(consts_ready, 1)
            nc.gpsimd.memset(ones_r[:, :], 1.0 / P).then_inc(consts_ready, 1)
            nc.gpsimd.memset(warm[:, :], 1.0).then_inc(consts_ready, 1)
            nc.gpsimd.memset(eps[:, :], EPS).then_inc(consts_ready, 1)
            nc.gpsimd.memset(vbd[:, :, :], 0.0).then_inc(consts_ready, 1)
            nc.gpsimd.memset(kcmp[:, :, :], 0.0).then_inc(consts_ready, 1)
            pool.wait_ge(con_loaded, 32)
            nc.gpsimd.tensor_copy(ident_b[:, :], ident).then_inc(consts_ready, 1)
            nc.gpsimd.tensor_copy(causal_b[:, :], causal).then_inc(consts_ready, 1)
            def centre(p):
                pool.wait_ge(mean_ready, p + 1)
                for k in range(DC):
                    nc.gpsimd.tensor_tensor(xa[:, k, :], xa[:, k, :], tmp[2][:, :], ALU.subtract).then_inc(centred, 1)

            centre(0)
            pool.wait_ge(units_done, MIX0 + CREDIT)
            nc.gpsimd.memset(hid_k[:, :, :, :], 0.0).then_inc(consts_ready, 1)
            nc.gpsimd.memset(hid_v[:, :, :, :, :], 0.0).then_inc(consts_ready, 1)
            pool.wait_ge(rope_done, N_ROPE + 2)
            for first in (2, 8):
                q = roped[:, first:first + 4, :]
                nc.gpsimd.tensor_scalar(q, q, HD ** -0.5, 0.0, ALU.mult, ALU.add).then_inc(q_scaled, 1)
            def queries_lo(m, q):
                for r, (src, hi, lo) in enumerate(query_pieces(m, q)):
                    pool.wait_ge(q_hi_done, 4 * q + 2 * m + r + 1)
                    nc.gpsimd.tensor_tensor(lo, src, hi.bitcast(F32), ALU.subtract).then_inc(q_ready, 1)
                    pool.wait_ge(q_ready, 4 * q + 2 * m + r + 1)

            pool.wait_ge(q_scaled, 2)
            for m in range(2):
                queries_lo(m, 0)
            for n, (j, src, rows, to) in enumerate(key_pieces):
                pool.wait_ge(k_hi_done, len(key_pieces))
                nc.gpsimd.tensor_tensor(k_lo[to, j, :], src, k_hi[rows, j, :].bitcast(F32), ALU.subtract)\
                    .then_inc(k_ready, 1)
                pool.wait_ge(k_ready, n + 1)
            for i, (kind, q, h) in enumerate(items):
                heads = NH if kind == "c" else batch(q)
                width = CW if kind == "c" else P * (q + 1)
                p = probs[i % PROBS][:, :heads * width].rearrange("p (h k) -> p h k", h=heads)
                pool.wait_ge(fac_ready, i + 1)
                if heads == 1 and kind != "a":
                    nc.gpsimd.tensor_scalar(p, p, fac[:, i % FACTORS, :1], branch_gate(kind, q, h, 1), ALU.mult, ALU.mult)\
                        .then_inc(scaled, 1)
                else:
                    nc.gpsimd.tensor_tensor(p, p, fac[:, i % FACTORS, :heads].unsqueeze(2).to_broadcast([P, heads, width]),
                                            ALU.mult).then_inc(scaled, 1)
                if q + 1 < QB and i in (last_a[q], last_b[q]):
                    pool.wait_ge(scaled, i + 1)
                    queries_lo(int(i == last_b[q]), q + 1)
            centre(1)
            centre(2)

        @block.tensor
        def _(pe):
            def unit(u, slot, groups, at=0, ends=True):
                hi, lo = parts(u) if slot is None else (w_hi[slot][:, :], w_lo[slot][:, :])
                pe.wait_ge(lo_ready, u + 1)
                for psum, x_hi, x_lo, chunks, first, last in groups:
                    for n, k in enumerate(chunks):
                        w = slice(at * P, (at + 1) * P)
                        one, end = first and n == 0, last and n == len(chunks) - 1
                        nc.tensor.matmul(psum, hi[:, w], x_hi[:, k, :], start=one, stop=False)
                        nc.tensor.matmul(psum, hi[:, w], x_lo[:, k, :], start=False, stop=False)
                        mm = nc.tensor.matmul(psum, lo[:, w], x_hi[:, k, :], start=False, stop=end)
                        at += 1
                if ends:
                    mm.then_inc(units_done, 1)

            def first_pair(u, psums, ready, count, x_hi=u_hi, x_lo=u_lo, head=1):
                order = [(i, k) for i in range(2) for k in range(head)]
                order += [(i, k) for k in range(head, DC) for i in range(2)]
                for i, k in order:
                    if k == 0:
                        pe.wait_ge(lo_ready, u + i + 1)
                    if i == 0:
                        pe.wait_ge(ready, count + k + 1)
                    w = slice(k * P, (k + 1) * P)
                    psum = psums[i]
                    hi, lo = parts(u + i)
                    nc.tensor.matmul(psum, hi[:, w], x_hi[:, k, :], start=k == 0, stop=False)
                    nc.tensor.matmul(psum, hi[:, w], x_lo[:, k, :], start=False, stop=False)
                    mm = nc.tensor.matmul(psum, lo[:, w], x_hi[:, k, :], start=False, stop=k == DC - 1)
                    if k == DC - 1:
                        mm.then_inc(units_done, 1)

            def keep_busy(u, x):
                pe.wait_ge(hi_ready, u + 1)
                for n in range(BUSY):
                    nc.tensor.matmul(bank[3][:, :], parts(u)[0][:, :P], x[:, n % DC, :], start=True, stop=True)

            def ffn(f, u0, phase):
                def hidden(j, u, jj):
                    pe.wait_ge(silu_done, j + 1)
                    unit(u, 0, [(bank[2 * jj][:, :], u_hi, u_lo, range(DC), True, True)])
                    pe.wait_ge(hmul_done, j + 1)
                    unit(u + 1, 1, [(bank[2 * jj + 1][:, :], u_hi, u_lo, range(DC), True, True)])

                pe.wait_ge(silu_done, FC * f + 1)
                pe.wait_ge(hmul_done, FC * f + 1)
                if f:
                    keep_busy(u0, m_hi)
                first_pair(u0, (bank[0][:, :], bank[1][:, :]), u_ready, phase * DC, head=1 if f else 3)
                hidden(FC * f + 1, u0 + 2, 1)
                with pe.Fori(0, FC // 2 - 1) as it:
                    for jj in range(2):
                        hidden(it * 2 + (FC * f + 2 + jj), it * 4 + (u0 + 4 + 2 * jj), jj)

                def output(it, cc, last=False):
                    pe.wait_ge(z_done, it * 2 + (2 * DC * f + cc + 1))
                    for n in range(OUT_UNITS):
                        ks = range(8 * n, min(8 * n + 8, FC))
                        u = it * (2 * OUT_UNITS) + (u0 + 2 * FC + cc * OUT_UNITS + n)
                        pe.wait_ge(h_ready, FC * f + ks[-1] + 1)
                        if last and n == OUT_UNITS - 1:
                            stats(phase, "sums")
                        unit(u, (cc * OUT_UNITS + n) % SPLIT,
                             [(bank[4 + cc][:, :], h_hi, h_lo, ks, n == 0, n == OUT_UNITS - 1)])

                with pe.Fori(0, DC // 2 - 1) as it:
                    for cc in range(2):
                        output(it, cc)
                for cc in range(2):
                    output(DC // 2 - 1, cc, last=cc == 1)
                stats(phase, "last chunk")

            def stats(p, part):
                for n in range(2):
                    if part == "sums":
                        pe.wait_ge(*((added_done, (DC - 1) * (p + 1)) if n else (sum_ready, p + 1)))
                        of = tmp[4 + n][:, :]
                    elif n == 0:
                        pe.wait_ge(z_done, CREDIT + DC * (p + 1))
                        of = xa[:, DC - 1, :]
                    else:
                        pe.wait_ge(sq_done, DC * (p + 1))
                        of = tmp[6 + (DC - 1) % 2][:, :]
                    mm = nc.tensor.matmul(bank[6 + n][:, :], ones_d[:, :], of, start=part == "sums", stop=part != "sums")
                    if part != "sums":
                        mm.then_inc(stats_done, 1)

            pe.sem_inc(units_done, CREDIT)
            pe.wait_ge(consts_ready, 1)
            ffn(0, 0, 0)
            pe.wait_ge(consts_ready, 8)

            keep_busy(MIX0, h_hi[:, DC:, :])
            first_pair(MIX0, (bank[0][:, :], bank[1][:, :]), u_ready, DC)
            with pe.Fori(0, N_MIX // 2 - 1) as it:
                for b in range(2):
                    pe.wait_ge(mix_evac, it * 2 + (b + 1 + CREDIT))
                    unit(it * 2 + (MIX0 + 2 + b), b, [(bank[b][:, :], u_hi, u_lo, range(DC), True, True)])
            pe.wait_ge(mix_evac, CREDIT + 2)
            nc.tensor.matmul(bank[2][:, :], ones_r[:, :], kvsq[:, :], start=True, stop=True).then_inc(ms_done, 1)
            for q in range(QB):
                tr = nc.tensor.transpose(bank[3][:, q * P:(q + 1) * P], small[:, q * P:(q + 1) * P], ident)
            tr.then_inc(small_turned, 1)
            def gate_chunk(b, c):
                u = G0 + b
                if c == 0:
                    pe.wait_ge(gate_done, b + 1)
                    pe.wait_ge(lo_ready, u + 1)
                slot, w = u % SPLIT, slice(c * P, (c + 1) * P)
                nc.tensor.matmul(bank[6 + b % 2][:, :], w_hi[slot][:, w], u_hi[:, c, :], start=c == 0, stop=False)
                nc.tensor.matmul(bank[6 + b % 2][:, :], w_hi[slot][:, w], u_lo[:, c, :], start=False, stop=False)
                mm = nc.tensor.matmul(bank[6 + b % 2][:, :], w_lo[slot][:, w], u_hi[:, c, :], start=False, stop=c == DC - 1)
                if c == DC - 1:
                    mm.then_inc(units_done, 1)

            def hidden_layer(t, chunk):
                pe.wait_ge(cmp_in_ready, 4 * (t + 1))
                for hc in range(2):
                    for l in range(CL2):
                        mm = nc.tensor.matmul(bank[t][:, hc * 64:hc * 64 + 2 * NC], w1[:, t, l, hc * P:(hc + 1) * P],
                                              cmp_in[t][:, l, :, :].rearrange("p g i -> p (g i)"),
                                              start=l == 0, stop=l == CL2 - 1)
                        if l % 4 == 3:
                            gate_chunk(chunk // DC, chunk % DC)
                            chunk += 1
                mm.then_inc(hid_done, 1)

            pe.wait_ge(mix_evac, CREDIT + N_MIX)
            pe.wait_ge(w1_loaded, 16)
            hidden_layer(0, 0)
            pe.wait_ge(rope_done, 4)
            for n in range((QB - 1) * NI):
                q, h = 1 + n // NI, n % NI
                rows = slice((h % 2) * HD, (h % 2) * HD + HD)
                if n >= 2:
                    pe.wait_ge(relu_done, n - 1)
                nc.tensor.matmul(bank[4 + n % 2][:, :P * (q + 1)], roped[rows, h // 2, q * P:(q + 1) * P],
                                 ki2[rows, :P * (q + 1)], start=True, stop=True).then_inc(logits_done, 1)
                gate_chunk((DC + n) // DC, (DC + n) % DC)
            hidden_layer(1, 20)
            for n in range(28, 4 * DC):
                gate_chunk(n // DC, n % DC)
            pe.wait_ge(kvn_ready, 1)
            pe.wait_ge(hid_ready, 2 + 16)
            nc.tensor.matmul(bank[0][:, :], smw[:, M_WK:M_WV], kvl[:, :], start=True, stop=True).then_inc(kv_done, 1)
            for t in range(QB):
                mm = nc.tensor.matmul(bank[1][:, t * HD:(t + 1) * HD], kvl[:, t * P:(t + 1) * P],
                                      smw[:, M_WV:M_PEK], start=True, stop=True)
            mm.then_inc(kv_done, 1)
            pe.wait_ge(kv_std, 1)
            pe.wait_ge(small_read, 2)
            for n, src in enumerate((vs_t, vw_t)):
                for t in range(QB):
                    tr = nc.tensor.transpose(bank[2 + n][:, t * P:(t + 1) * P], src[:, t * P:(t + 1) * P], ident)
                tr.then_inc(v_turned, 1)
            pe.wait_ge(relu_done, (QB - 1) * NI)
            for hc in range(2):
                mm = nc.tensor.matmul(bank[4][:, :2 * CW], w2k[:, hc, :],
                                      hid_k[:, hc, :, :].rearrange("p g i -> p (g i)"), start=hc == 0, stop=hc == 1)
            mm.then_inc(cmp_done, 1)
            for g in range(2):
                for hc in range(2):
                    mm = nc.tensor.matmul(bank[5][:, g * HD:(g + 1) * HD],
                                          hid_v[:, hc, g, :, :].rearrange("p r i -> p (r i)"), w2v[:, hc, :],
                                          start=hc == 0, stop=hc == 1)
            mm.then_inc(cmp_done, 1)
            with pe.Fori(0, N_GATE // 2 - 3) as it:
                for b in range(2):
                    pe.wait_ge(gate_done, it * 2 + (b + 5))
                    unit(it * 2 + (G0 + 4 + b), b, [(bank[6 + b][:, :], u_hi, u_lo, range(DC), True, True)])

            def scores(i):
                kind, q, h = items[i]
                keys = P * (q + 1)
                if i >= 3:
                    pe.wait_ge(exp_done, i - 2)
                ps = bank[i % 3]
                if kind == "c":
                    heads = ps[:, :NH * CW].rearrange("p (g c i) -> p c g i", g=2, c=NH // 2)
                    for c in range(NH // 2):
                        mm = nc.tensor.matmul(heads[:, c, :, :], roped[:, 8 + c, q * P:(q + 1) * P],
                                              kcmp[:, :, :].rearrange("p g i -> p (g i)"), start=True, stop=True)
                    mm.then_inc(s_done, 1)
                    return
                if h == 0 and kind != "w":
                    pe.wait_ge(q_ready, 4 * q + 2 * (1 + (kind == "s")))
                for hh in range(h, h + batch(q)):
                    to = ps[:, (hh - h) * keys:(hh - h + 1) * keys]
                    j = 0 if kind == "a" else (1 if kind == "s" else 3) + hh // 4
                    query = q_cut[int(kind != "a")][:, hh, :]
                    nc.tensor.matmul(to, query, k_hi[:, j, :keys], start=True, stop=False)
                    nc.tensor.matmul(to, query, k_lo[:, j, :keys], start=False, stop=False)
                    if kind == "a" and q:
                        pe.wait_ge(mask_ready, q)
                        mm = nc.tensor.matmul(to, ident_b[:, :], mask_a[q - 1][:, :], start=False, stop=True)
                    else:
                        mm = nc.tensor.matmul(to[:, keys - P:], ident_b[:, :], causal_b[:, :], start=False, stop=True)
                mm.then_inc(s_done, 1)

            def turns(i):
                kind, q, h = items[i]
                if i >= 2:
                    pe.wait_ge(t_read, i - 1)
                pe.wait_ge(scaled, i + 1)
                for t in range(2 if kind == "c" else batch(q) * (q + 1)):
                    tr = nc.tensor.transpose(bank[3 + i % 2][:, t * P:(t + 1) * P], probs[i % PROBS][:, t * P:(t + 1) * P], ident)
                tr.then_inc(t_done, 1)

            def values(u):
                r, its = pairs[u]
                kind, q, h = items[its[0]]
                pe.wait_ge(t_read, its[-1] + 1)
                first, last = u == 0 or pairs[u - 1][0] != r, its[-1] == result_end[r]
                if first and r >= 3:
                    pe.wait_ge(y_summed, r - 2)
                ps = bank[5 + r % 3]
                heads = max(2, batch(q))
                to = ps[:, h % 4 * P:(h % 4 + heads) * P].rearrange("p (h k) -> p h k", h=heads)
                if kind == "w" and last:
                    for x in range(4):
                        nc.tensor.matmul(ps[:HD, x * P:(x + 1) * P], vbd[:, h // 4, x * HD:(x + 1) * HD],
                                         cmp_t[:, h // 4 * P:(h // 4 + 1) * P], start=False, stop=False)
                for t in range(q + 1):
                    v = v_a[:, t, :, :] if kind == "a" else (v_s if kind == "s" else v_w)[:, 2 * t + h // 4, :, :]
                    v = v.rearrange("p a d -> p (a d)")
                    for n, part in enumerate((probs_t_hi, probs_t_lo)):
                        mm = nc.tensor.matmul(to, v, pair_heads(part[u % 2], q, t), start=first and t == 0 and n == 0,
                                              stop=last and t == q and n == 1)
                mm.then_inc(pv_done, 1)

            pe.wait_ge(k_ready, len(key_pieces))
            pe.wait_ge(v_cut, 3)
            pe.wait_ge(cmp_read, 10)
            pe.wait_ge(kv_read, 2)
            for i in range(3):
                scores(i)
                if i < 2:
                    b = N_GATE - 2 + i
                    pe.wait_ge(gate_done, b + 1)
                    unit(G0 + b, b % 2, [(bank[6 + b % 2][:, :], u_hi, u_lo, range(DC), True, True)])
            for i in range(3, n_items + VALUE_LAG):
                if i < n_items:
                    scores(i)
                if 0 <= i - TURN_LAG < n_items:
                    turns(i - TURN_LAG)
                if i == VALUE_LAG:
                    pe.wait_ge(gate_done, CREDIT + N_GATE)
                j = i - VALUE_LAG
                if j in pair_of and pairs[pair_of[j][0]][1][-1] == j:
                    values(pair_of[j][0])
            def branch(b, m):
                return bank[2 * b + m][:, :], y_hi[m], y_lo[m], range(HC), True, True

            pe.wait_ge(y_ready, 4 * QB - 2)
            for b in range(2):
                unit(BR0 + b, None, [branch(b, 0)], ends=False)
            pe.wait_ge(y_ready, 4 * QB)
            for b in range(2):
                unit(BR0 + b, None, [branch(b, 1)], at=HC)
            with pe.Fori(1, DC // 2) as it:
                for b in range(2):
                    pe.wait_ge(merge_done, it * 2 + (b + 1))
                    unit(it * 2 + (BR0 + b), b, [branch(b, m) for m in range(2)])
            first_pair(MO0, (bank[4][:, :], bank[5][:, :]), m_ready, 0, m_hi, m_lo)
            with pe.Fori(0, DC // 2 - 1) as it:
                for b in range(2):
                    pe.wait_ge(z_done, it * 2 + (DC + b + 1 + CREDIT))
                    unit(it * 2 + (MO0 + 2 + b), b, [(bank[4 + b][:, :], m_hi, m_lo, range(DC), True, True)])
            for part in ("sums", "last chunk"):
                stats(1, part)
            ffn(1, FFN2, 2)

        @block.scalar
        def _(act):
            def copy(to, of, scale=1.0):
                return nc.scalar.activation(to, of, ACT.Copy, scale=scale)

            def hi_at(base, it, per, n):
                u = base + n
                act.wait_ge(raw_loaded[u % RAW], it * (16 * per // RAW) + 16 * (u // RAW + 1))
                act.wait_ge(units_done, it * per + (u + 1))
                copy(w_hi[u % SPLIT][:, :], raw[u % RAW][:, :]).then_inc(hi_ready, 1)

            def unit_hi(u):
                if u < UNITS:
                    act.wait_ge(raw_loaded[u % RAW], 16 * (u // RAW + 1))
                    act.wait_ge(units_done, CREDIT + parts_free(u))
                    copy(parts(u)[0], raw[u % RAW][:, :]).then_inc(hi_ready, 1)

            def inputs(p, ready):
                def hi(k):
                    act.wait_ge(ub_ready, p * DC + k + 1)
                    copy(u_hi[:, k, :], ub[k % 4][:, :]).then_inc(uh_ready, 1)

                for k in range(DC):
                    act.wait_ge(t_ready, p * DC + k + 1)
                    if k >= 4:
                        act.wait_ge(u_ready, p * DC + k - 3)
                    scale, shift = ready(k)
                    nc.scalar.activation(ub[k % 4][:, :], xa[:, k, :], ACT.Identity, scale=scale, bias=shift)\
                        .then_inc(ub_ready, 1)
                    if k:
                        hi(k - 1)
                    if p == 0 and 3 <= k < 5:
                        unit_hi(k - 3)
                hi(DC - 1)
                for n in range(2):
                    unit_hi((0, MIX0, FFN2)[p] + 2 + n)

            def squares(z0, u0, per, residual):
                for c in range(DC):
                    scale, shift = residual(c)
                    nc.scalar.activation(xa[:, c, :], xa[:, c, :], ACT.Identity, scale=scale, bias=shift)\
                        .then_inc(xa_ready, 1)
                    for u in ahead(u0, per, c):
                        unit_hi(u)
                    act.wait_ge(z_done, CREDIT + z0 + c + 1)
                    if c >= 2:
                        act.wait_ge(added_done, z0 // DC * (DC - 1) + c - 1)
                    nc.scalar.activation(tmp[6 + c % 2][:, :], xa[:, c, :], ACT.Square).then_inc(sq_done, 1)

            def norm(p, next_unit):
                unit_hi(next_unit)
                act.wait_ge(stats_done, 2 * p + 1)
                copy(tmp[2][:, :], bank[6][:, :]).then_inc(mean_ready, 1)
                nc.scalar.activation(tmp[3][:, :], bank[6][:, :], ACT.Square).then_inc(mean2_ready, 1)
                nc.scalar.activation(warm[:, :], warm[:, :], ACT.Sqrt)
                act.wait_ge(var_ready, p + 1)
                nc.scalar.activation(tmp[3][:, :], tmp[3][:, :], ACT.Sqrt).then_inc(std_ready, 1)

            def ffn(f, u0, residual):
                def hidden(it, jj, first=False):
                    j = it * 2 + (FC * f + jj)
                    if not first:
                        hi_at(u0, it, 4, 2 * jj + 2)
                    act.wait_ge(units_done, it * 4 + (u0 + 2 * jj + 1 + CREDIT))
                    nc.scalar.activation(tmp[jj][:, :], bank[2 * jj][:, :], ACT.Silu).then_inc(silu_done, 1)
                    if not first:
                        hi_at(u0, it, 4, 2 * jj + 3)
                    act.wait_ge(hmul_done, j + (CREDIT + 1))
                    act.wait_ge(consts_ready, 1)
                    copy(h_hi[:, bass.ts(it * 2 + jj, 1), :], tmp[2 + jj][:, :].unsqueeze(1)).then_inc(hh_done, 1)

                hidden(0, 0, first=True)
                hidden(0, 1)
                with act.Fori(1, FC // 2) as it:
                    for jj in range(2):
                        hidden(it, jj)
                squares(2 * DC * f, u0 + 2 * FC, OUT_UNITS, residual)

            act.sem_inc(silu_done, CREDIT)
            act.sem_inc(mix_evac, CREDIT)
            act.sem_inc(gate_done, CREDIT)
            act.wait_ge(c_loaded, 16)
            nc.scalar.activation(c_act[:, :], c_act[:, :], ACT.Silu).then_inc(c_ready, 1)
            inputs(0, lambda k: (aff[:, 0, k:k + 1], mod[:, k:k + 1]))
            ffn(0, 0, lambda c: (ALPHA, 0.0))
            act.wait_ge(consts_ready, 8)
            norm(0, MIX0 + 1)
            inputs(1, lambda k: (aff[:, 0, k:k + 1], aff[:, 1, k:k + 1]))

            def swap(to, of, rows):
                for r in range(0, rows, 64):
                    copy(to[r:r + 32, :], of[r + 32:r + 64, :])
                    last = copy(to[r + 32:r + 64, :], of[r:r + 32, :])
                return last

            act.wait_ge(units_done, CREDIT + MIX0)
            for b in range(2):
                act.wait_ge(units_done, CREDIT + MIX0 + b + 1)
                if b == 0:
                    copy(small[:, :], bank[0][:, :])
                    swap(tmp[2], bank[0], HD).then_inc(mix_evac, 1)
                else:
                    copy(kvl[:, :], bank[1][:, :])
                    nc.scalar.activation(kvsq[:, :], bank[1][:, :], ACT.Square).then_inc(mix_evac, 1)
            with act.Fori(0, N_ROPE // 4) as it:
                for b in range(4):
                    hi_at(MIX0 + 2, it, 4, b + 2)
                    act.wait_ge(units_done, it * 4 + (MIX0 + 2 + b + 1 + CREDIT))
                    act.wait_ge(consts_ready, 1)
                    act.wait_ge(rope_done, it * 4 + (b + 1))
                    copy(tmp[b % 2][:, :], bank[b % 2][:, :])
                    swap(tmp[2 + b % 2], bank[b % 2], P).then_inc(mix_evac, 1)
            for n, to in ((14, kc), (15, vc), (16, vs_t), (17, vw_t)):
                unit_hi(MIX0 + n + 2)
                act.wait_ge(units_done, CREDIT + MIX0 + n + 1)
                if n == 14:
                    act.wait_ge(rope_done, 13)
                    copy(tmp[0][:, :], bank[0][:, :])
                    swap(tmp[2], bank[0], P).then_inc(mix_evac, 1)
                else:
                    copy(to[:, :], bank[n % 2][:, :]).then_inc(mix_evac, 1)
            act.wait_ge(ms_done, 1)
            nc.scalar.activation(kvsq[:, :], bank[2][:, :], ACT.Sqrt, bias=eps[:, :]).then_inc(kv_std, 1)
            act.wait_ge(small_turned, 1)
            turned = bank[3][:, :].rearrange("p (q f) -> p q f", q=QB)
            copy(wi[:, :, :], turned[:, :, HD:HD + NI], scale=NI ** -0.5).then_inc(small_read, 1)
            nc.scalar.activation(gb[:, :, :], turned[:, :, HD + NI:HD + NI + 3 * NH], ACT.Sigmoid).then_inc(small_read, 1)
            def gate(b):
                act.wait_ge(units_done, G0 + b + 1 + CREDIT)
                nc.scalar.activation(gates[:, b, :], bank[6 + b % 2][:, :], ACT.Sigmoid).then_inc(gate_done, 1)

            act.wait_ge(consts_ready, 10)
            def hidden(t):
                act.wait_ge(hid_done, t + 1)
                for hc in range(2):
                    hid = bank[t][:, hc * 64:hc * 64 + 2 * NC].rearrange("p (g i) -> p g i", g=2)
                    if t == 0:
                        nc.scalar.activation(hid_k[:, hc, :, 0:NC], hid, ACT.Silu).then_inc(hid_ready, 1)
                    else:
                        for g in range(2):
                            for r in range(4):
                                nc.scalar.activation(hid_v[:, hc, g, r, 0:NC], hid[:, g, :], ACT.Silu)\
                                    .then_inc(hid_ready, 1)

            unit_hi(G0 + 2)
            for n in range((QB - 1) * NI):
                q = 1 + n // NI
                if n == DC - 4:
                    gate(0)
                if n == DC:
                    unit_hi(G0 + 3)
                    gate(1)
                act.wait_ge(logits_done, n + 1)
                if n >= 2:
                    act.wait_ge(acc_done, n - 1)
                else:
                    act.wait_ge(rope_done, N_ROPE + 3)
                nc.scalar.activation(tmp[n % 2][:, :P * (q + 1)], bank[4 + n % 2][:, :P * (q + 1)], ACT.Relu)\
                    .then_inc(relu_done, 1)
            unit_hi(G0 + 4)
            gate(2)
            hidden(0)
            hidden(1)
            unit_hi(G0 + 5)
            gate(3)
            act.wait_ge(kv_done, 2)
            copy(tmp[6][:, :], bank[0][:, :])
            swap(tmp[7], bank[0], P).then_inc(kv_read, 1)
            copy(v_a[:, :, 0, :], bank[1][:, :QB * HD].rearrange("p (t d) -> p t d", t=QB)).then_inc(kv_read, 1)
            act.wait_ge(v_turned, 2)
            for n, to in enumerate((v_s, v_w)):
                copy(to[:, :, 0, :], bank[2 + n][:, :].rearrange("p (t d) -> p t d", t=2 * QB)).then_inc(v_read, 1)
            act.wait_ge(cmp_done, 1)
            for g in range(2):
                rows = slice(g * HD, (g + 1) * HD)
                copy(kcmp[rows, g, :], bank[4][rows, g * CW:(g + 1) * CW]).then_inc(cmp_read, 1)
            act.wait_ge(cmp_done, 2)
            for g in range(2):
                for r in range(4):
                    copy(vbd[r * CW:(r + 1) * CW, g, r * HD:(r + 1) * HD],
                         bank[5][r * CW:(r + 1) * CW, g * HD:(g + 1) * HD]).then_inc(cmp_read, 1)
            def queries_hi(m, q):
                for src, hi, _ in query_pieces(m, q):
                    copy(hi, src).then_inc(q_hi_done, 1)

            def keys_hi(pieces):
                for j, src, rows, to in pieces:
                    copy(k_hi[to, j, :], src).then_inc(k_hi_done, 1)

            beside = [lambda: keys_hi(key_pieces[1:5]), lambda: keys_hi(key_pieces[5:]),
                      lambda: queries_hi(0, 0), lambda: queries_hi(1, 0)]
            for b in range(4):
                unit_hi(G0 + b + 6)
                gate(b + 4)
                if b == 2:
                    act.wait_ge(q_scaled, 2)
                if b == 3:
                    act.wait_ge(rope_done, N_ROPE + 4)
                    keys_hi(key_pieces[:1])
                beside[b]()
            for b in range(8, N_GATE - 2):
                unit_hi(G0 + b + 2)
                gate(b)

            def exps(i):
                kind, q, h = items[i]
                act.wait_ge(max_done, i + 1)
                if i >= PROBS:
                    act.wait_ge(t_done, i - PROBS + 1)
                if kind == "c":
                    nc.scalar.activation(probs[i % PROBS][:, :NH * CW], tmp[6][:, :NH * CW], ACT.Exp).then_inc(exp_done, 1)
                else:
                    keys = P * (q + 1)
                    for b in range(batch(q)):
                        col = slice(b * keys, (b + 1) * keys)
                        last = nc.scalar.activation(probs[i % PROBS][:, col], bank[i % 3][:, col], ACT.Exp,
                                                    bias=nmax[:, i % 4, b:b + 1],
                                                    accum_out=sums[:, q, "aswc".index(kind), h + b:h + b + 1])
                    last.then_inc(exp_done, 1)
                if q + 1 < QB and i in (last_a[q], last_b[q]):
                    queries_hi(int(i == last_b[q]), q + 1)

            def turned_hi(i):
                if items[i][0] == "c":
                    return
                u, part = pair_of[i]
                q = items[i][1]
                act.wait_ge(t_done, i + 1)
                if u >= 2:
                    act.wait_ge(pv_done, u - 1)
                width = batch(q) * (q + 1) * P
                copy(probs_t_hi[u % 2][:, part * S:part * S + width], bank[3 + i % 2][:, :width]).then_inc(t_hi_done, 1)

            results = {i: r for r, i in result_end.items()}
            for i in range(3):
                exps(i)
                if i < 2:
                    b = N_GATE - 2 + i
                    act.wait_ge(units_done, G0 + b + 1 + CREDIT)
                    copy(gates[:, b, :], bank[6 + b % 2][:, :]).then_inc(gate_done, 1)
            for i in range(3, n_items + CUT_LAG - 1):
                if 0 <= i - TURN_LAG < n_items:
                    turned_hi(i - TURN_LAG)
                if i < n_items:
                    exps(i)
                if i - CUT_LAG in results:
                    r = results[i - CUT_LAG]
                    act.wait_ge(y_summed, r + 1)
                    copy(y_cut(y_hi, r), y_sum[:, :2 * P].rearrange("p (c k) -> p c k", c=2)).then_inc(y_hi_done, 1)
                if i - SUM_LAG in results:
                    r = results[i - SUM_LAG]
                    act.wait_ge(pv_done, pair_of[i - SUM_LAG][0] + 1)
                    if r:
                        act.wait_ge(y_summed, r)
                    copy(y_part[:HD, :], bank[5 + r % 3][HD:, :]).then_inc(y_part_ready, 1)
                if i == n_items - 1 + TURN_LAG:
                    act.wait_ge(s_done, n_items)
                    for n in range(2):
                        unit_hi(BR0 + n)
            act.wait_ge(y_summed, 4 * QB)
            copy(y_cut(y_hi, 4 * QB - 1), y_sum[:, :2 * P].rearrange("p (c k) -> p c k", c=2)).then_inc(y_hi_done, 1)
            for c in range(DC):
                for u in branches_ahead(c):
                    unit_hi(u)
                act.wait_ge(mf_ready, c + 1)
                copy(m_hi[:, c, :], tmp[c % 2][:, :]).then_inc(mh_done, 1)
                if c == 0:
                    act.wait_ge(gate_done, CREDIT + N_GATE)
                    last = gates[:, N_GATE - 2:, :]
                    nc.scalar.activation(last, last, ACT.Sigmoid).then_inc(gate_done, 1)
            for n in range(2):
                unit_hi(MO0 + 2 + n)
            squares(DC, MO0, 1, lambda c: (aff[:, 2, c:c + 1], aff[:, 3, c:c + 1]))
            norm(1, FFN2 + 1)
            inputs(2, lambda k: (aff[:, 4, k:k + 1], aff[:, 5, k:k + 1]))
            ffn(1, FFN2, lambda c: (aff[:, 6, c:c + 1], aff[:, 7, c:c + 1]))
            norm(2, UNITS)
            for k in range(DC):
                act.wait_ge(t_ready, 3 * DC + k + 1)
                nc.scalar.activation(xa[:, k, :], xa[:, k, :], ACT.Identity, scale=vec[:, V_LN + 4 * DC + k:V_LN + 4 * DC + k + 1],
                                     bias=vec[:, V_LN + 5 * DC + k:V_LN + 5 * DC + k + 1]).then_inc(final_ready, 1)

        @block.vector
        def _(dve):
            count, turn = [0], [None]

            def mark(instruction):
                instruction.then_inc(dve_step, 1)
                count[0] += 1

            def hold():
                dve.wait_ge(dve_step, count[0] if turn[0] is None else turn[0][0] * turn[0][1] + count[0])

            def step(instruction):
                mark(instruction)
                hold()

            tt = nc.vector.tensor_tensor

            def lo_at(u0, it, per, n):
                u = u0 + n
                dve.wait_ge(hi_ready, u + 1 if it is None else it * per + (u + 1))
                tt(w_lo[u % SPLIT][:, :], raw[u % RAW][:, :], w_hi[u % SPLIT][:, :].bitcast(F32), ALU.subtract)\
                    .then_inc(lo_ready, 1)

            def unit_lo(u):
                if u < UNITS:
                    dve.wait_ge(hi_ready, u + 1)
                    hi, lo = parts(u)
                    tt(lo, raw[u % RAW][:, :], hi.bitcast(F32), ALU.subtract).then_inc(lo_ready, 1)

            def ada_block(slot, turn, b):
                dve.wait_ge(ada_loaded[slot], turn)
                ada_product(ada[slot][:, :], b)

            def ada_product(w, b):
                nc.vector.scalar_tensor_tensor(out=w, in0=w, scalar=1.0, in1=c_act[:, :],
                                               op0=ALU.mult, op1=ALU.mult, accum_out=mod[:, bass.ts(b, 1)])\
                    .then_inc(ada_done, 1)

            def add_bias(b0, b1):
                dve.wait_ge(ada_done, b1)
                step(tt(mod[:, b0:b1], mod[:, b0:b1], vec[:, V_BADA + b0:V_BADA + b1], ALU.add))

            def group(m):
                return mod[:, m * DC:(m + 1) * DC]

            def ln(n):
                return vec[:, V_LN + n * DC:V_LN + (n + 1) * DC]

            def prepare(at, g, b, shift, scale):
                step(nc.vector.tensor_scalar(aff[:, at + 1, :], group(scale), 1.0, None, ALU.add))
                step(tt(aff[:, at, :], aff[:, at + 1, :], ln(g), ALU.mult))
                step(tt(aff[:, at + 1, :], aff[:, at + 1, :], ln(b), ALU.mult))
                step(tt(aff[:, at + 1, :], aff[:, at + 1, :], group(shift), ALU.add))
                step(nc.vector.tensor_scalar(aff[:, at + 2, :], ln(g), ALPHA, None, ALU.mult))
                step(nc.vector.tensor_scalar(aff[:, at + 3, :], ln(b), ALPHA, None, ALU.mult))

            def input_lo(p, k):
                dve.wait_ge(uh_ready, p * DC + k + 1)
                tt(u_lo[:, k, :], ub[k % 4][:, :], u_hi[:, k, :].bitcast(F32), ALU.subtract).then_inc(u_ready, 1)

            def inputs(p):
                for k in range(DC):
                    dve.wait_ge(centred, (p - 1) * DC + k + 1)
                    tt(xa[:, k, :], xa[:, k, :], tmp[3][:, :], ALU.mult).then_inc(t_ready, 1)
                    if k >= 2:
                        input_lo(p, k - 2)
                for k in range(DC - 2, DC):
                    input_lo(p, k)
                for n in range(2):
                    unit_lo((MIX0, FFN2)[p - 1] + 2 + n)

            def outputs(z0, u0, per, gate, sublayer):
                step(nc.vector.memset(tmp[4][:, :], 0.0))
                step(nc.vector.memset(tmp[5][:, :], 0.0))
                for c in range(DC):
                    if sublayer == 0:
                        for b in ADA_WITH[c]:
                            ada_block(b % ADA_RING, 16 * ((b - ADA_FIRST) // ADA_RING + 1), b)
                    for u in ahead(u0, per, c):
                        unit_lo(u)
                    dve.wait_ge(units_done, CREDIT + u0 + (c + 1) * per)
                    dve.wait_ge(xa_ready, DC * sublayer + c + 1)
                    nc.vector.scalar_tensor_tensor(out=xa[:, c, :], in0=bank[4 + c % 2][:, :], scalar=gate(c),
                                                   in1=xa[:, c, :], op0=ALU.mult, op1=ALU.add).then_inc(z_done, 1)
                    if c == DC - 1:
                        break
                    dve.wait_ge(z_done, CREDIT + z0 + c + 1)
                    add = tt(tmp[4][:, :], tmp[4][:, :], xa[:, c, :], ALU.add)
                    if c == DC - 2:
                        add.then_inc(sum_ready, 1)
                    else:
                        step(add)
                    dve.wait_ge(sq_done, z0 + c + 1)
                    tt(tmp[5][:, :], tmp[5][:, :], tmp[6 + c % 2][:, :], ALU.add).then_inc(added_done, 1)
                    dve.wait_ge(added_done, (DC - 1) * sublayer + c + 1)

            def norm(p, next_unit):
                unit_lo(next_unit)
                dve.wait_ge(mean2_ready, p + 1)
                dve.wait_ge(stats_done, 2 * p + 2)
                step(tt(tmp[3][:, :], bank[7][:, :], tmp[3][:, :], ALU.subtract))
                nc.vector.tensor_scalar(tmp[3][:, :], tmp[3][:, :], 0.0, EPS, ALU.max, ALU.add).then_inc(var_ready, 1)
                dve.wait_ge(std_ready, p + 1)
                step(nc.vector.reciprocal(tmp[3][:, :], tmp[3][:, :]))

            def ffn(f, u0, sublayer):
                def hidden(it, jj, first=False):
                    j = it * 2 + (FC * f + jj)
                    for n in range(2):
                        if not first:
                            lo_at(u0, it, 4, 2 * jj + n + 2)
                        if f == 0:
                            k = 2 * jj + n
                            ada_block(k % ADA_RING, it * (16 * 4 // ADA_RING) + 16 * (k // ADA_RING + 1),
                                      it * 4 + (ADA_FIRST + k))
                    dve.wait_ge(units_done, it * 4 + (u0 + 2 * jj + 2 + CREDIT))
                    dve.wait_ge(silu_done, j + (CREDIT + 1))
                    tt(tmp[2 + jj][:, :], bank[2 * jj + 1][:, :], tmp[jj][:, :], ALU.mult).then_inc(hmul_done, 1)
                    dve.wait_ge(hh_done, j + 1)
                    tt(h_lo[:, bass.ts(it * 2 + jj, 1), :], tmp[2 + jj][:, :].unsqueeze(1),
                       h_hi[:, bass.ts(it * 2 + jj, 1), :].bitcast(F32), ALU.subtract).then_inc(h_ready, 1)

                hidden(0, 0, first=True)
                hidden(0, 1)
                with dve.Fori(1, FC // 2) as it:
                    for jj in range(2):
                        hidden(it, jj)
                if f == 0:
                    add_bias(ADA_FIRST, ADA_LATE)
                    step(nc.vector.tensor_scalar(group(2), group(2), 0.5, None, ALU.mult))
                    prepare(0, 0, 1, 3, 4)
                m = 2 if f == 0 else 8
                outputs(2 * DC * f, u0 + 2 * FC, OUT_UNITS, lambda c: mod[:, m * DC + c:m * DC + c + 1], sublayer)

            dve.sem_inc(hmul_done, CREDIT)
            dve.sem_inc(z_done, CREDIT)
            dve.sem_inc(merge_done, CREDIT)
            dve.wait_ge(c_ready, 1)
            dve.wait_ge(vec_loaded, 16)
            for k in range(DC):
                dve.wait_ge(chunk_loaded[k], 48)
                for n in range(2):
                    ada_product(ada_first[:, n * DC + k, :], n * DC + k)
                dve.wait_ge(ada_done, 2 * k + 2)
                pair = mod[:, k:k + DC + 1:DC]
                step(tt(pair, pair, vec[:, V_BADA + k:V_BADA + k + DC + 1:DC], ALU.add))
                nc.vector.tensor_scalar(aff[:, 0, k:k + 1], mod[:, DC + k:DC + k + 1], 1.0, None, ALU.add)\
                    .then_inc(t_ready, 1)
                if k >= 2:
                    input_lo(0, k - 2)
                if 4 <= k < 6:
                    unit_lo(k - 4)
            for k in range(DC - 2, DC):
                input_lo(0, k)
            for u in range(2, 4):
                unit_lo(u)
            ffn(0, 0, 0)
            norm(0, MIX0 + 1)
            inputs(1)

            def rotate(to, x, turned, rows, count, part):
                tt(part[:rows, :], x[:rows, :], cos[:rows, :], ALU.mult)
                step(tt(turned[:rows, :], turned[:rows, :], sin[:rows, :], ALU.mult))
                tt(to, part[:rows, :] if count is None else part[:rows, :].unsqueeze(1),
                   turned[:rows, :] if count is None else turned[:rows, :].unsqueeze(1), ALU.add).then_inc(rope_done, 1)

            dve.wait_ge(rope_loaded, 16)
            dve.wait_ge(mix_evac, CREDIT + 1)
            rotate(ki2[:HD, :], small, tmp[2], HD, None, tmp[4])
            dve.wait_ge(rope_done, 1)
            nc.vector.tensor_copy(ki2[HD:, :], ki2[:HD, :]).then_inc(rope_done, 1)
            with dve.Fori(0, N_ROPE // 4) as it:
                turn[0] = (it, 4)
                for b in range(4):
                    lo_at(MIX0 + 2, it, 4, b + 2)
                    dve.wait_ge(mix_evac, it * 4 + (CREDIT + 2 + b + 1))
                    dve.wait_ge(rope_done, it * 4 + (b + 1))
                    rotate(roped[:, bass.ts(it * 4 + b, 1), :], tmp[b % 2], tmp[2 + b % 2], P, 1, tmp[4 + b % 2])
                turn[0], count[0] = None, count[0] + 4 * (N_ROPE // 4 - 1)
            unit_lo(MIX0 + 16)
            dve.wait_ge(mix_evac, CREDIT + 15)
            dve.wait_ge(rope_done, N_ROPE + 1)
            rotate(kc[:, :], tmp[0], tmp[2], P, None, tmp[4])
            for t, src in enumerate((kc, vc)):
                unit_lo(MIX0 + 17 + t)
                if t == 0:
                    dve.wait_ge(rope_done, N_ROPE + 3)
                else:
                    dve.wait_ge(mix_evac, CREDIT + 16)
                for par in range(2):
                    for g in range(2):
                        rows = slice(g * HD, (g + 1) * HD)
                        x = src[rows, :].rearrange("p (i l a) -> p a l i", i=S // 16, l=8, a=2)
                        for half in range(2):
                            dst = cmp_in[t][par * HD:(par + 1) * HD, half * 8:(half + 1) * 8, g, :]
                            pe_v = pe_tab[t][rows, par, half * 8:(half + 1) * 8].unsqueeze(2).to_broadcast([HD, 8, NC])
                            add = tt(dst, x[:, par, :, half:half + NC], pe_v, ALU.add)
                        add.then_inc(cmp_in_ready, 1)
            unit_lo(MIX0 + 19)
            dve.wait_ge(kv_std, 1)
            step(nc.vector.reciprocal(kvsq[:, :], kvsq[:, :]))
            nc.vector.scalar_tensor_tensor(out=kvl[:, :], in0=kvl[:, :], scalar=vec[:, V_KVG:V_KVG + 1], in1=kvsq[:, :],
                                           op0=ALU.mult, op1=ALU.mult).then_inc(kvn_ready, 1)
            unit_lo(G0 + 2)
            dve.wait_ge(small_read, 1)
            for n in range((QB - 1) * NI):
                q, h = 1 + n // NI, n % NI
                a, r = acc[q - 1][:, :], tmp[n % 2][:, :P * (q + 1)]
                if n == DC:
                    unit_lo(G0 + 3)
                dve.wait_ge(relu_done, n + 1)
                if h == 0:
                    nc.vector.tensor_scalar(a, r, wi[:, q, h:h + 1], None, ALU.mult).then_inc(acc_done, 1)
                else:
                    dve.wait_ge(acc_done, n)
                    nc.vector.scalar_tensor_tensor(out=a, in0=r, scalar=wi[:, q, h:h + 1], in1=a,
                                                   op0=ALU.mult, op1=ALU.add).then_inc(acc_done, 1)
            dve.wait_ge(acc_done, (QB - 1) * NI)
            for q in range(1, QB):
                last = acc[q - 1][:, q * P:]
                step(tt(last, last, causal, ALU.add))
            def top_rounds(it, u0, rounds, halves):
                def beside(x):
                    hold()
                    if x is None:
                        return nc.vector.memset(pause[:, :], 0.0)
                    u = u0 + x // 2
                    cols = slice(x % 2 * UW // 2, (x % 2 + 1) * UW // 2)
                    if x % 2 == 0:
                        dve.wait_ge(hi_ready, u + 1 if it is None else it * 4 + (u + 1))
                    part = tt(w_lo[u % SPLIT][:, cols], raw[u % RAW][:, cols], w_hi[u % SPLIT][:, cols].bitcast(F32),
                              ALU.subtract)
                    if x % 2:
                        part.then_inc(lo_ready, 1)

                for n in range(rounds):
                    beside(halves[2 * n])
                    for q in range(3):
                        last = nc.vector.max(max8[:, q, :], acc[q][:, :])
                    mark(last)
                    beside(halves[2 * n + 1])
                    for q in range(3):
                        last = nc.vector.match_replace(acc[q][:, :], max8[:, q, :], acc[q][:, :], TAKEN)
                    mark(last)

            top_rounds(None, G0 + 4, 4, [None, None, 0, 1, None, None, 2, 3])
            hold()
            dve.wait_ge(kv_read, 1)
            rotate(k_a[:, :], tmp[6], tmp[7], P, None, tmp[5])
            dve.wait_ge(kv_read, 2)
            tt(v_a[:, :, 1, :], bank[1][:, :QB * HD].rearrange("p (t d) -> p t d", t=QB), v_a[:, :, 0, :].bitcast(F32),
               ALU.subtract).then_inc(v_cut, 1)
            for n, v in enumerate((v_s, v_w)):
                dve.wait_ge(v_read, n + 1)
                tt(v[:, :, 1, :], bank[2 + n][:, :].rearrange("p (t d) -> p t d", t=2 * QB), v[:, :, 0, :].bitcast(F32),
                   ALU.subtract).then_inc(v_cut, 1)
            with dve.Fori(0, 2) as it:
                turn[0] = (it, 2 * 5)
                top_rounds(it, G0 + 6, 5, [0, 1, None, 2, 3, 4, 5, None, 6, 7])
                turn[0], count[0] = None, count[0] + 2 * 5
            top_rounds(None, G0 + 14, TOPK // 8 - 14, [0, 1, 2, 3])
            hold()
            for q in range(3):
                nc.vector.tensor_scalar(mask_a[q][:, :], acc[q][:, :], TAKEN / 2, NEG, ALU.is_gt, ALU.mult)\
                    .then_inc(mask_ready, 1)

            def maxima(i):
                kind, q, h = items[i]
                dve.wait_ge(s_done, i + 1)
                ps = bank[i % 3]
                if kind != "c":
                    if i >= 4:
                        dve.wait_ge(exp_done, i - 3)
                    heads = ps[:, :batch(q) * P * (q + 1)].rearrange("p (b k) -> p b k", b=batch(q))
                    nc.vector.tensor_reduce(nmax[:, i % 4, :batch(q)], heads, AX, ALU.max, negate=True)\
                        .then_inc(max_done, 1)
                    return
                mask = cmp_mask[:, q, :].unsqueeze(1).to_broadcast([P, NH, CW])
                step(tt(cmp_s[:, :, :], ps[:, :NH * CW].rearrange("p (h c) -> p h c", h=NH), mask, ALU.add))
                step(nc.vector.tensor_reduce(nmax_c[:, :], cmp_s[:, :, :], AX, ALU.max, negate=True))
                tt(cmp_s[:, :, :], cmp_s[:, :, :], nmax_c[:, :].unsqueeze(2).to_broadcast([P, NH, CW]), ALU.add)\
                    .then_inc(max_done, 1)

            def factors(i):
                kind, q, h = items[i]
                heads = NH if kind == "c" else batch(q)
                total = sums[:, q, "aswc".index(kind), h:h + heads]
                f = fac[:, i % FACTORS, :heads]
                dve.wait_ge(exp_done, i + 1)
                if i >= FACTORS:
                    dve.wait_ge(scaled, i - FACTORS + 1)
                if kind == "c":
                    p = probs[i % PROBS][:, :NH * CW].rearrange("p (h c) -> p h c", h=NH)
                    step(nc.vector.tensor_reduce(total, p, AX, ALU.add))
                if kind == "a" or heads == 1:
                    nc.vector.reciprocal(f, total).then_inc(fac_ready, 1)
                    return
                step(nc.vector.reciprocal(f, total))
                gate = tt(f, f, branch_gate(kind, q, h, heads), ALU.mult)
                if kind == "c":
                    step(gate)
                    gate = nc.vector.tensor_scalar(f, f, con[:, C_VALID + q:C_VALID + q + 1], None, ALU.mult)
                gate.then_inc(fac_ready, 1)

            def turned_lo(i):
                kind, q, h = items[i]
                ps = bank[3 + i % 2]
                if kind == "c":
                    dve.wait_ge(t_done, i + 1)
                    nc.vector.tensor_copy(cmp_t, ps[:, :2 * P]).then_inc(t_read, 1)
                    return
                u, part = pair_of[i]
                col = slice(part * S, part * S + batch(q) * (q + 1) * P)
                dve.wait_ge(t_hi_done, cut_no[i] + 1)
                tt(probs_t_lo[u % 2][:, col], ps[:, :col.stop - col.start], probs_t_hi[u % 2][:, col].bitcast(F32),
                   ALU.subtract).then_inc(t_read, 1)

            def sum_up(r):
                dve.wait_ge(y_part_ready, r + 1)
                if r:
                    dve.wait_ge(y_ready, r)
                for odd in range(2):
                    rows = slice(odd * HD, (odd + 1) * HD)
                    a, b = [x[:HD, :].rearrange("p (c o k) -> p c o k", c=2, o=2)[:, :, odd, :]
                            for x in (bank[5 + r % 3], y_part)]
                    add = tt(y_sum[rows, :2 * P].rearrange("p (c k) -> p c k", c=2), a, b, ALU.add)
                add.then_inc(y_summed, 1)

            def cut(r):
                dve.wait_ge(y_hi_done, r + 1)
                tt(y_cut(y_lo, r), y_sum[:, :2 * P].rearrange("p (c k) -> p c k", c=2), y_cut(y_hi, r).bitcast(F32),
                   ALU.subtract).then_inc(y_ready, 1)

            results = {i: r for r, i in result_end.items()}
            for i in range(n_items + CUT_LAG - 1):
                if i < n_items:
                    maxima(i)
                if 0 <= i - 1 < n_items:
                    factors(i - 1)
                if 0 <= i - TURN_LAG < n_items:
                    turned_lo(i - TURN_LAG)
                if i - CUT_LAG in results:
                    cut(results[i - CUT_LAG])
                if i - SUM_LAG in results:
                    sum_up(results[i - SUM_LAG])
                if i == n_items - 1 + TURN_LAG:
                    for n in range(2):
                        unit_lo(BR0 + n)
            cut(4 * QB - 1)

            for c in range(DC):
                for u in branches_ahead(c):
                    unit_lo(u)
                b = c % 2
                dve.wait_ge(units_done, CREDIT + BR0 + c + 1)
                if c == DC - 2:
                    dve.wait_ge(gate_done, CREDIT + N_GATE + 1)
                tt(tmp[b][:, :], bank[2 * b][:, :], gates[:, c, :], ALU.mult)
                tt(tmp[2 + b][:, :], bank[2 * b + 1][:, :], gates[:, DC + c, :], ALU.mult).then_inc(merge_done, 1)
                dve.wait_ge(merge_done, CREDIT + c + 1)
                tt(tmp[b][:, :], tmp[b][:, :], tmp[2 + b][:, :], ALU.add).then_inc(mf_ready, 1)
                dve.wait_ge(mh_done, c + 1)
                tt(m_lo[:, c, :], tmp[b][:, :], m_hi[:, c, :].bitcast(F32), ALU.subtract).then_inc(m_ready, 1)
            for n in range(2):
                unit_lo(MO0 + 2 + n)
            add_bias(ADA_LATE, NADA)
            step(nc.vector.tensor_scalar(group(8), group(8), 0.5, None, ALU.mult))
            prepare(4, 2, 3, 6, 7)
            outputs(DC, MO0, 1, lambda c: mod[:, 5 * DC + c:5 * DC + c + 1], 1)
            norm(1, FFN2 + 1)
            inputs(2)
            ffn(1, FFN2, 2)
            norm(2, UNITS)
            for k in range(DC):
                dve.wait_ge(centred, 2 * DC + k + 1)
                tt(xa[:, k, :], xa[:, k, :], tmp[3][:, :], ALU.mult).then_inc(t_ready, 1)


def _layout(inputs, np):
    f = {k: np.asarray(v) for k, v in inputs.items()}

    def unit_blocks(w):
        k, n = w.shape
        return w.reshape(k // P, P, n // P, P).transpose(2, 1, 0, 3).reshape(n // P, P, k)

    def ffn(w_in, w_out):
        a, b = unit_blocks(w_in[:, :FF]), unit_blocks(w_in[:, FF:])
        first = np.stack([a, b], 1).reshape(2 * FC, P, UW)
        o = unit_blocks(w_out)
        o = np.concatenate([o, np.zeros((DC, P, OUT_UNITS * UW - FF), o.dtype)], 2)
        return [first, o.reshape(DC, P, OUT_UNITS, UW).transpose(0, 2, 1, 3).reshape(OUT_UNITS * DC, P, UW)]

    w = f["w_mix_in"][0]
    cut = np.cumsum([NH * HD, P, NI * HD, HD, NI, NH * HD, 6 * P, 3 * NH, 2 * D])
    qa, kv, qi, ki, wi, qb, kv6, gb, gm = np.split(w, cut[:-1], axis=1)
    small = np.concatenate([ki, wi, gb, np.zeros((D, P - HD - NI - 3 * NH), w.dtype)], 1)
    pairs = np.arange(NH).reshape(2, NH // 2).T.ravel()
    qb = qb.reshape(D, NH, HD)[:, pairs, :].reshape(D, NH * HD)
    kc, vc, ks, vs, kw, vw = np.split(kv6, 6, axis=1)
    mix = unit_blocks(np.concatenate([small, kv, qi, qa, ks, kw, qb, kc, vc, vs, vw, gm], 1))
    br = np.concatenate([unit_blocks(f["w_br_a"][0]), unit_blocks(f["w_br_b"][0])], 2)
    stream = np.concatenate(
        ffn(f["ffn1_w_in"][0], f["ffn1_w_out"][0]) + [mix, br, unit_blocks(f["w_mix_out"][0])]
        + ffn(f["ffn2_w_in"][0], f["ffn2_w_out"][0]), 0)

    def col(v):
        return v.reshape(-1, P).T

    vecs = np.concatenate([col(f[k][0]) for k in ("b_ada", "ln1_g", "ln1_b", "ln2_g", "ln2_b", "ln3_g", "ln3_b", "kv_norm_g")], 1)
    up = f["w_kv_up"][0]
    w2k = f["cmp_w2_k"][0].reshape(2, P, HD).transpose(1, 0, 2)
    w2v = f["cmp_w2_v"][0].reshape(2, P, HD).transpose(1, 0, 2)

    def pe(v):
        v = v.reshape(CL2, 2, HD).transpose(2, 1, 0).reshape(HD, 2 * CL2)
        return np.concatenate([v, v], 0)

    small_w = np.concatenate([
        np.concatenate([w2k, w2k], 2).reshape(P, 4 * HD), w2v.reshape(P, 2 * HD),
        up[:, :HD], up[:, :HD], up[:, HD:], pe(f["cmp_pe_k"][0]), pe(f["cmp_pe_v"][0])], 1)
    cmp_w1 = np.stack([f[k][0].reshape(CL2, P, 2 * P).transpose(1, 0, 2) for k in ("cmp_w1_k", "cmp_w1_v")], 1)

    row = np.arange(P)
    consts = np.zeros((P, C_N), np.float32)
    consts[:, C_ID:C_ID + P] = np.eye(P)
    consts[:, C_CAUSAL:C_CAUSAL + P] = np.where(row[None, :] <= row[:, None], 0.0, NEG)
    token = row[:, None, None] + P * np.arange(QB)[None, :, None]
    block = np.arange(CW)[None, None, :]
    seen = (block < NC) & (16 * block + 31 <= token)
    consts[:, C_CMP:C_VALID] = np.where(seen, 0.0, NEG).reshape(P, QB * CW)
    consts[:, C_VALID:] = seen.any(2)
    half = HD // 2
    inv = (10000.0 ** (-np.arange(half) / half)).astype(np.float32)
    ang = (np.arange(S, dtype=np.float32)[None, :] * inv[:, None]).astype(np.float32)
    cos, sin = np.cos(ang).astype(np.float32), np.sin(ang).astype(np.float32)
    rope = np.stack([np.concatenate([cos] * 4, 0), np.concatenate([-sin, sin, -sin, sin], 0)], 1)

    c = np.ascontiguousarray
    return {
        "x_t": c(f["x"][0].T.reshape(DC, P, S).transpose(1, 0, 2)),
        "c_row": c(f["c"].reshape(1, D)),
        "w_ada_t": c(f["w_ada"][0].T.reshape(NADA, P, D)),
        "vecs": c(vecs),
        "consts": consts,
        "rope_tab": c(rope),
        "small_w": c(small_w),
        "cmp_w1": c(cmp_w1.reshape(P, 2, CL2, 2 * P)),
        "stream": c(stream),
    }


def kernel(**inputs):
    import numpy as np
    import concourse.bacc as bacc
    from concourse.bass_utils import run_bass_kernel_spmd

    arrays = _layout(inputs, np)
    nc = bacc.Bacc("TRN2", target_bir_lowering=False, num_devices=1)
    args = [nc.dram_tensor(k, a.shape, mybir.dt.from_np(a.dtype), kind="ExternalInput").ap()
            for k, a in arrays.items()]
    out = nc.dram_tensor("out", (P, DC, S), F32, kind="ExternalOutput").ap()
    decoder_layer(nc, *args, out)
    got = run_bass_kernel_spmd(nc, [arrays], core_ids=[0]).results[0]["out"]
    return np.ascontiguousarray(got.transpose(1, 0, 2).reshape(D, S).T).reshape(1, S, D)
```
